# Optimizing a Trainium2 kernel written in Bass

```python
import math, functools
import jax, jax.numpy as jnp
from jax import lax
import numpy as np
import math
import jax
import jax.numpy as jnp

D_MODEL = 1024
BATCH = 1
SEQ = 256
DEPTH = 1

GRID_W = 64
CTX_LEN = 256
HEAD_DIM = 64
A_HEADS = 8
A_KV_HEADS = 2
A_GROUP = A_HEADS // A_KV_HEADS
A_WIDTH = A_HEADS * HEAD_DIM
B_HEADS = 4
B_V_DIM = 2 * HEAD_DIM
B_WIDTH = B_HEADS * B_V_DIM
N_BRANCH = 2
A_Q_COLS = A_HEADS * HEAD_DIM
A_KV_COLS = A_KV_HEADS * HEAD_DIM
B_QK_COLS = B_HEADS * 2 * HEAD_DIM
IN_SPLIT = [A_Q_COLS, A_KV_COLS, A_KV_COLS, B_QK_COLS, B_QK_COLS, B_WIDTH, D_MODEL, D_MODEL]
IN_COLS = sum(IN_SPLIT)
IN_OFFSETS = [int(v) for v in np.cumsum(IN_SPLIT)[:-1]]
ROPE_THETA = 10000.0
AXIS_PAIRS = HEAD_DIM // 4
Q_BLOCK = 128
N_EXPERTS = 32
TOP_K = 4
D_EXPERT = D_MODEL
SWIGLU_LIMIT = 7.0
SWIGLU_ALPHA = 1.702
MOE_BLOCK = 128
N_MOD = 6
EPS = 1e-6
SUBLN_EPS = 1e-5


def _rmsnorm(x, gain, eps=EPS):
    xf = x.astype(jnp.float32)
    y = xf * lax.rsqrt(jnp.mean(xf * xf, axis=-1, keepdims=True) + eps)
    return (y * gain.astype(jnp.float32)).astype(x.dtype)

def _modulate(h, shift, scale):
    return h * (1 + scale) + shift

def _axial_rope(rows):
    row = jnp.repeat(jnp.arange(rows, dtype=jnp.float32), GRID_W)
    col = jnp.tile(jnp.arange(GRID_W, dtype=jnp.float32), rows)
    inv = 1.0 / (ROPE_THETA ** (jnp.arange(AXIS_PAIRS, dtype=jnp.float32) / AXIS_PAIRS))
    ang = jnp.concatenate([row[:, None] * inv, col[:, None] * inv], axis=-1)
    return jnp.cos(ang), jnp.sin(ang)

def _apply_rope(x, cos, sin):
    extra = x.ndim - 3
    cos = cos.reshape(cos.shape[0], *([1] * extra), cos.shape[1])
    sin = sin.reshape(sin.shape[0], *([1] * extra), sin.shape[1])
    xp = x.reshape(*x.shape[:-1], HEAD_DIM // 2, 2)
    x0, x1 = xp[..., 0], xp[..., 1]
    out = jnp.stack([x0 * cos - x1 * sin, x0 * sin + x1 * cos], axis=-1)
    return out.reshape(x.shape).astype(x.dtype)

def _project(h, w_in, q_norm_a, k_norm_a, q_norm_b, k_norm_b):
    b, n, _ = h.shape
    qa, ka, va, qb, kb, vb, ga, gb = jnp.split(h @ w_in, IN_OFFSETS, axis=-1)
    qa = _rmsnorm(qa.reshape(b, n, A_HEADS, HEAD_DIM), q_norm_a)
    ka = _rmsnorm(ka.reshape(b, n, A_KV_HEADS, HEAD_DIM), k_norm_a)
    va = va.reshape(b, n, A_KV_HEADS, HEAD_DIM)
    qb = _rmsnorm(qb.reshape(b, n, B_HEADS, 2, HEAD_DIM), q_norm_b)
    kb = _rmsnorm(kb.reshape(b, n, B_HEADS, 2, HEAD_DIM), k_norm_b)
    vb = vb.reshape(b, n, B_HEADS, B_V_DIM)
    return qa, ka, va, qb, kb, vb, ga, gb

def _gqa_attend(q, k, v):
    b, n = q.shape[:2]
    qg = q.reshape(b, n, A_KV_HEADS, A_GROUP, HEAD_DIM)
    s = jnp.einsum('bqhgd,bkhd->bhgqk', qg, k).astype(jnp.float32) * (HEAD_DIM ** -0.5)
    p = jax.nn.softmax(s, axis=-1).astype(v.dtype)
    o = jnp.einsum('bhgqk,bkhd->bqhgd', p, v)
    return o.reshape(b, n, A_WIDTH)

def _diff_attend(q, k, v, lam):
    s = jnp.einsum('bqhmd,bkhmd->bhmqk', q, k).astype(jnp.float32) * (HEAD_DIM ** -0.5)
    p = jax.nn.softmax(s, axis=-1)
    a = (p[:, :, 0] - lam * p[:, :, 1]).astype(v.dtype)
    return jnp.einsum('bhqk,bkhe->bqhe', a, v)

def _sweep_query_blocks(attend, q, k, v):
    b, s = q.shape[:2]
    nb = s // Q_BLOCK
    qb = jnp.moveaxis(q.reshape(b, nb, Q_BLOCK, *q.shape[2:]), 1, 0)
    o = lax.map(lambda qq: attend(qq, k, v), qb)
    o = jnp.moveaxis(o, 0, 1)
    return o.reshape(b, s, *o.shape[3:])

def _diff_out(o, subln, lam_init):
    o = _rmsnorm(o, subln, SUBLN_EPS) * (1.0 - lam_init)
    return o.reshape(o.shape[0], o.shape[1], B_WIDTH)

def _merge(ya, yb, ga, gb, w_oa, w_ob, w_out):
    merged = jax.nn.sigmoid(ga) * (ya @ w_oa) + jax.nn.sigmoid(gb) * (yb @ w_ob)
    return merged @ w_out

def _moe(h, router_w, router_b, w_gate, b_gate, w_up, b_up, w_down, b_down):
    t = h.shape[0]
    logits = (h @ router_w + router_b).astype(jnp.float32)
    top_logit, top_e = lax.top_k(logits, TOP_K)
    top_w = jax.nn.softmax(top_logit, axis=-1)
    n_assign = t * TOP_K
    flat_e = top_e.reshape(-1)
    order = jnp.argsort(flat_e)
    sorted_e = flat_e[order]
    sorted_tok = order // TOP_K
    sorted_w = top_w.reshape(-1)[order]
    counts = jnp.bincount(flat_e, length=N_EXPERTS)
    padded = (counts + MOE_BLOCK - 1) // MOE_BLOCK * MOE_BLOCK
    pad_end = jnp.cumsum(padded)
    pad_start = pad_end - padded
    start = jnp.cumsum(counts) - counts
    dest = pad_start[sorted_e] + jnp.arange(n_assign) - start[sorted_e]
    n_blocks = -(-n_assign // MOE_BLOCK) + N_EXPERTS
    buf_tok = jnp.zeros((n_blocks * MOE_BLOCK,), jnp.int32).at[dest].set(sorted_tok.astype(jnp.int32))
    block_e = jnp.minimum(jnp.searchsorted(pad_end, jnp.arange(n_blocks) * MOE_BLOCK, side='right'),
                          N_EXPERTS - 1)
    xb = h[buf_tok].reshape(n_blocks, MOE_BLOCK, h.shape[-1])

    def expert_block(args):
        xe, e = args
        gate = jnp.minimum(xe @ w_gate[e] + b_gate[e], SWIGLU_LIMIT)
        up = jnp.clip(xe @ w_up[e] + b_up[e], -SWIGLU_LIMIT, SWIGLU_LIMIT)
        act = (up + 1) * (gate * jax.nn.sigmoid(SWIGLU_ALPHA * gate))
        return act @ w_down[e] + b_down[e]

    yb = lax.map(expert_block, (xb, block_e)).reshape(-1, h.shape[-1])
    y = yb[dest] * sorted_w[:, None].astype(h.dtype)
    return jax.ops.segment_sum(y, sorted_tok, num_segments=t)

def first_inputs(seed: int = 0) -> dict:
    key = jax.random.key(seed)
    ks = jax.random.split(key, 32)
    f32 = jnp.float32
    L = DEPTH

    def nrm(k, shape, scale):
        return jax.random.normal(k, shape, f32) * scale

    def gain(k, shape):
        return 1.0 + 0.05 * jax.random.normal(k, shape, f32)

    return {
        "x": nrm(ks[0], (BATCH, SEQ, D_MODEL), 1.0),
        "c": nrm(ks[1], (BATCH, D_MODEL), 1.0),
        "ctx": nrm(ks[2], (BATCH, CTX_LEN, D_MODEL), 1.0),
        "c_ctx": nrm(ks[3], (D_MODEL,), 1.0),
        "w_ada": nrm(ks[4], (L, D_MODEL, N_MOD * D_MODEL), 0.5 * D_MODEL ** -0.5),
        "b_ada": nrm(ks[5], (L, N_MOD * D_MODEL), 0.02),
        "norm_attn": gain(ks[6], (L, D_MODEL)),
        "w_in": nrm(ks[7], (L, D_MODEL, IN_COLS), D_MODEL ** -0.5),
        "q_norm_a": gain(ks[8], (L, HEAD_DIM)),
        "k_norm_a": gain(ks[9], (L, HEAD_DIM)),
        "q_norm_b": gain(ks[10], (L, HEAD_DIM)),
        "k_norm_b": gain(ks[11], (L, HEAD_DIM)),
        "lambda_q1": nrm(ks[12], (L, HEAD_DIM), 0.1),
        "lambda_k1": nrm(ks[13], (L, HEAD_DIM), 0.1),
        "lambda_q2": nrm(ks[14], (L, HEAD_DIM), 0.1),
        "lambda_k2": nrm(ks[15], (L, HEAD_DIM), 0.1),
        "subln_b": gain(ks[16], (L, B_V_DIM)),
        "w_oa": nrm(ks[17], (L, A_WIDTH, D_MODEL), A_WIDTH ** -0.5),
        "w_ob": nrm(ks[18], (L, B_WIDTH, D_MODEL), B_WIDTH ** -0.5),
        "w_out": nrm(ks[19], (L, D_MODEL, D_MODEL), D_MODEL ** -0.5),
        "norm_mlp": gain(ks[20], (L, D_MODEL)),
        "router_w": nrm(ks[21], (L, D_MODEL, N_EXPERTS), D_MODEL ** -0.5),
        "router_b": nrm(ks[22], (L, N_EXPERTS), 0.01),
        "w_gate": nrm(ks[23], (L, N_EXPERTS, D_MODEL, D_EXPERT), D_MODEL ** -0.5),
        "b_gate": nrm(ks[24], (L, N_EXPERTS, D_EXPERT), 0.02),
        "w_up": nrm(ks[25], (L, N_EXPERTS, D_MODEL, D_EXPERT), D_MODEL ** -0.5),
        "b_up": nrm(ks[26], (L, N_EXPERTS, D_EXPERT), 0.02),
        "w_down": nrm(ks[27], (L, N_EXPERTS, D_EXPERT, D_MODEL), D_EXPERT ** -0.5),
        "b_down": nrm(ks[28], (L, N_EXPERTS, D_MODEL), 0.02),
    }

def first_block(x, c, ctx, c_ctx, w_ada, b_ada, norm_attn, w_in, q_norm_a, k_norm_a, q_norm_b,
              k_norm_b, lambda_q1, lambda_k1, lambda_q2, lambda_k2, subln_b, w_oa, w_ob, w_out,
              norm_mlp, router_w, router_b, w_gate, b_gate, w_up, b_up, w_down, b_down):
    b, s, d = x.shape
    rows = s // GRID_W
    cos, sin = _axial_rope(rows)
    cx = ctx
    for l in range(DEPTH):
        last = l == DEPTH - 1
        lam_init = 0.8 - 0.6 * math.exp(-0.3 * l)
        lam = (jnp.exp(jnp.sum(lambda_q1[l].astype(jnp.float32) * lambda_k1[l].astype(jnp.float32)))
               - jnp.exp(jnp.sum(lambda_q2[l].astype(jnp.float32) * lambda_k2[l].astype(jnp.float32)))
               + lam_init)
        mod_x = (jax.nn.silu(c) @ w_ada[l] + b_ada[l])[:, None, :]
        mod_c = (jax.nn.silu(c_ctx) @ w_ada[l] + b_ada[l])[None, None, :]
        sh_a, sc_a, g_a, sh_m, sc_m, g_m = jnp.split(mod_x, N_MOD, axis=-1)
        csh_a, csc_a, cg_a, csh_m, csc_m, cg_m = jnp.split(mod_c, N_MOD, axis=-1)
        proj = functools.partial(_project, w_in=w_in[l], q_norm_a=q_norm_a[l], k_norm_a=k_norm_a[l],
                                 q_norm_b=q_norm_b[l], k_norm_b=k_norm_b[l])

        hx = _modulate(_rmsnorm(x, norm_attn[l]), sh_a, sc_a)
        hc = _modulate(_rmsnorm(cx, norm_attn[l]), csh_a, csc_a)
        qa, ka, va, qb, kb, vb, ga, gb = proj(hx)
        cqa, cka, cva, cqb, ckb, cvb, cga, cgb = proj(hc)
        qa, ka = _apply_rope(qa, cos, sin), _apply_rope(ka, cos, sin)
        qb, kb = _apply_rope(qb, cos, sin), _apply_rope(kb, cos, sin)
        ka_all = jnp.concatenate([ka, cka], axis=1)
        va_all = jnp.concatenate([va, cva], axis=1)
        kb_all = jnp.concatenate([kb, ckb], axis=1)
        vb_all = jnp.concatenate([vb, cvb], axis=1)
        ya = _sweep_query_blocks(_gqa_attend, qa, ka_all, va_all)
        yb = _sweep_query_blocks(lambda qq, kk, vv: _diff_attend(qq, kk, vv, lam), qb, kb_all, vb_all)
        yb = _diff_out(yb, subln_b[l], lam_init)
        x = x + g_a * _merge(ya, yb, ga, gb, w_oa[l], w_ob[l], w_out[l])
        if not last:
            cya = _gqa_attend(cqa, cka, cva)
            cyb = _diff_out(_diff_attend(cqb, ckb, cvb, lam), subln_b[l], lam_init)
            cx = cx + cg_a * _merge(cya, cyb, cga, cgb, w_oa[l], w_ob[l], w_out[l])

        moe = functools.partial(_moe, router_w=router_w[l], router_b=router_b[l], w_gate=w_gate[l],
                                b_gate=b_gate[l], w_up=w_up[l], b_up=b_up[l], w_down=w_down[l],
                                b_down=b_down[l])
        hx = _modulate(_rmsnorm(x, norm_mlp[l]), sh_m, sc_m)
        x = x + g_m * moe(hx.reshape(b * s, d)).reshape(b, s, d)
        if not last:
            hc = _modulate(_rmsnorm(cx, norm_mlp[l]), csh_m, csc_m)
            cx = cx + cg_m * moe(hc.reshape(-1, d)).reshape(cx.shape)
    return x


DEPTH_2 = 2

N_MIXERS = 4
F32 = jnp.float32
OUT_SCALE = 0.5
A_HEADS_2 = 4
A_DQK = 128
A_DV = 256
A_CHUNK = 64
A_IN = 2 * A_HEADS_2 * A_DQK + 2 * A_HEADS_2 * A_DV + 2 * A_HEADS_2
B_HEADS_2 = 8
B_DH = 128
B_BLOCK = 256
B_TOPK = 3
B_QBLOCK = 128
ROPE_THETA_2 = 500000.0
ROPE_DIMS = B_DH // 4
B_IN = 3 * B_HEADS_2 * B_DH
C_HEADS = 4
C_DK = D_MODEL // C_HEADS
C_DV = 2 * C_DK
C_CHUNK = 128
C_ROPE_THETA = 10000.0
C_IN = 2 * C_HEADS * C_DK + 2 * C_HEADS * C_DV
D_RNN = D_MODEL
D_BLOCKS = 4
D_BW = D_RNN // D_BLOCKS
D_CONV = 4
LRU_C = 8.0
D_FF = ((8 * D_MODEL // 3 + 255) // 256) * 256
N_LAYERS_A = len(range(0, DEPTH_2, N_MIXERS))
N_LAYERS_B = len(range(1, DEPTH_2, N_MIXERS))
N_LAYERS_C = len(range(2, DEPTH_2, N_MIXERS))
N_LAYERS_D = len(range(3, DEPTH_2, N_MIXERS))


def rmsnorm(x, g):
    xf = x.astype(F32)
    y = xf * lax.rsqrt(jnp.mean(xf * xf, axis=-1, keepdims=True) + EPS)
    return (y * g.astype(F32)).astype(x.dtype)

def rotary(x, pos, n_rot, theta):
    half = n_rot // 2
    inv = theta ** (-jnp.arange(half, dtype=F32) * (2.0 / n_rot))
    ang = pos.astype(F32)[:, None, :, None] * inv
    cos, sin = jnp.cos(ang), jnp.sin(ang)
    xf = x.astype(F32)
    x1, x2 = xf[..., :half], xf[..., half:n_rot]
    out = jnp.concatenate([x1 * cos - x2 * sin, x2 * cos + x1 * sin, xf[..., n_rot:]], axis=-1)
    return out.astype(x.dtype)

def split_heads(t, h):
    b, s, _ = t.shape
    return t.reshape(b, s, h, -1).transpose(0, 2, 1, 3)

def merge_heads(t):
    b, h, s, d = t.shape
    return t.transpose(0, 2, 1, 3).reshape(b, s, h * d)

def to_chunks(t, l):
    b, h, s, d = t.shape
    return t.reshape(b, h, s // l, l, d).transpose(2, 0, 1, 3, 4)

def from_chunks(t):
    nc, b, h, l, d = t.shape
    return t.transpose(1, 2, 0, 3, 4).reshape(b, h, nc * l, d)

def mlstm_mixer(u, w_in, b_gates, g_out, w_out):
    b, s, _ = u.shape
    h, l = A_HEADS_2, A_CHUNK
    nc = s // l
    sq, sv = h * A_DQK, h * A_DV
    q, k, v, o, gl = jnp.split(u @ w_in, [sq, 2 * sq, 2 * sq + sv, 2 * sq + 2 * sv], axis=-1)
    gl = gl.astype(F32) + b_gates.astype(F32)
    log_i = gl[..., :h]
    log_f = jax.nn.log_sigmoid(gl[..., h:])
    qh = split_heads(q, h).astype(F32) * (A_DQK ** -0.5)
    kh = split_heads(k, h).astype(F32)
    vh = split_heads(v, h).astype(F32)

    def gate_chunks(g):
        return g.transpose(0, 2, 1).reshape(b, h, nc, l).transpose(2, 0, 1, 3)

    causal = jnp.tril(jnp.ones((l, l), dtype=bool))

    def step(carry, xs):
        c_st, n_st, m_st = carry
        qc, kc, vc, ic, fc = xs
        bcum = jnp.cumsum(fc, axis=-1)
        btot = bcum[..., -1]
        dmat = jnp.where(causal, bcum[..., :, None] - bcum[..., None, :] + ic[..., None, :], -jnp.inf)
        inter = bcum + m_st[..., None]
        m_t = jnp.maximum(inter, jnp.max(dmat, axis=-1))
        w_intra = jnp.exp(dmat - m_t[..., None])
        w_inter = jnp.exp(inter - m_t)
        qk = jnp.einsum('bhtd,bhsd->bhts', qc, kc) * w_intra
        num = jnp.einsum('bhts,bhsv->bhtv', qk, vc) + w_inter[..., None] * jnp.einsum('bhvd,bhtd->bhtv', c_st, qc)
        den = jnp.sum(qk, axis=-1) + w_inter * jnp.einsum('bhd,bhtd->bht', n_st, qc)
        h_out = num / jnp.maximum(jnp.abs(den), jnp.exp(-m_t))[..., None]
        dec = btot[..., None] - bcum + ic
        m_new = jnp.maximum(btot + m_st, jnp.max(dec, axis=-1))
        ws = jnp.exp(dec - m_new[..., None])
        wc = jnp.exp(btot + m_st - m_new)
        c_new = wc[..., None, None] * c_st + jnp.einsum('bhs,bhsv,bhsd->bhvd', ws, vc, kc)
        n_new = wc[..., None] * n_st + jnp.einsum('bhs,bhsd->bhd', ws, kc)
        return (c_new, n_new, m_new), h_out

    init = (jnp.zeros((b, h, A_DV, A_DQK), F32), jnp.zeros((b, h, A_DQK), F32), jnp.zeros((b, h), F32))
    xs = (to_chunks(qh, l), to_chunks(kh, l), to_chunks(vh, l), gate_chunks(log_i), gate_chunks(log_f))
    _, hc = lax.scan(step, init, xs)
    hs = rmsnorm(from_chunks(hc), g_out[:, None, :])
    y = merge_heads(hs).astype(u.dtype) * jax.nn.sigmoid(o)
    return y @ w_out

def moba_mixer(u, positions, w_in, g_q, g_k, w_out):
    b, s, _ = u.shape
    h, dh = B_HEADS_2, B_DH
    q, k, v = jnp.split(u @ w_in, 3, axis=-1)
    qh = rotary(rmsnorm(split_heads(q, h), g_q), positions, ROPE_DIMS, ROPE_THETA_2)
    kh = rotary(rmsnorm(split_heads(k, h), g_k), positions, ROPE_DIMS, ROPE_THETA_2)
    vh = split_heads(v, h)
    nblk = -(-s // B_BLOCK)
    sp = nblk * B_BLOCK
    pad = ((0, 0), (0, 0), (0, sp - s), (0, 0))
    qh, kh, vh = jnp.pad(qh, pad), jnp.pad(kh, pad), jnp.pad(vh, pad)
    kb = kh.reshape(b, h, nblk, B_BLOCK, dh)
    vb = vh.reshape(b, h, nblk, B_BLOCK, dh)
    kmean = jnp.mean(kb.astype(F32), axis=3)
    nqb = sp // B_QBLOCK
    per_blk = B_BLOCK // B_QBLOCK
    topk = min(B_TOPK, nblk - 1)
    qblocks = qh.reshape(b, h, nqb, B_QBLOCK, dh).transpose(0, 2, 1, 3, 4).reshape(b * nqb, h, B_QBLOCK, dh)
    scale = dh ** -0.5
    qoff = jnp.arange(B_QBLOCK)
    koff = jnp.arange(B_BLOCK)

    def attend(args):
        idx, qc = args
        bi = idx // nqb
        qi = idx % nqb
        j = qi // per_blk
        kb_b, vb_b = kb[bi], vb[bi]
        qf = qc.astype(F32) * scale
        qpos = qi * B_QBLOCK + qoff
        kpos = j * B_BLOCK + koff
        k_own = kb_b[:, j].astype(F32)
        v_own = vb_b[:, j].astype(F32)
        s_own = jnp.einsum('hqd,hnd->hqn', qf, k_own)
        s_own = jnp.where(kpos[None, None, :] <= qpos[None, :, None], s_own, -jnp.inf)
        if topk > 0:
            gate = jnp.einsum('hqd,hnd->hqn', qf, kmean[bi])
            gate = jnp.where(jnp.arange(nblk)[None, None, :] < j, gate, -jnp.inf)
            _, sel = lax.top_k(gate, topk)
            k_sel = jax.vmap(lambda kh_, ih_: kh_[ih_])(kb_b, sel).astype(F32)
            v_sel = jax.vmap(lambda vh_, ih_: vh_[ih_])(vb_b, sel).astype(F32)
            s_sel = jnp.einsum('hqd,hqtnd->hqtn', qf, k_sel)
            valid = jnp.arange(topk) < j
            s_sel = jnp.where(valid[None, None, :, None], s_sel, -jnp.inf)
            logits = jnp.concatenate([s_sel.reshape(h, B_QBLOCK, topk * B_BLOCK), s_own], axis=-1)
            p = jax.nn.softmax(logits, axis=-1)
            p_sel = p[..., :topk * B_BLOCK].reshape(h, B_QBLOCK, topk, B_BLOCK)
            out = jnp.einsum('hqtn,hqtnd->hqd', p_sel, v_sel) + jnp.einsum('hqn,hnd->hqd', p[..., topk * B_BLOCK:], v_own)
        else:
            p = jax.nn.softmax(s_own, axis=-1)
            out = jnp.einsum('hqn,hnd->hqd', p, v_own)
        return out.astype(qc.dtype)

    out = lax.map(attend, (jnp.arange(b * nqb, dtype=jnp.int32), qblocks))
    out = out.reshape(b, nqb, h, B_QBLOCK, dh).transpose(0, 2, 1, 3, 4).reshape(b, h, sp, dh)[:, :, :s]
    return merge_heads(out) @ w_out

def retention_mixer(u, positions, w_in, g_out, w_out):
    b, s, _ = u.shape
    h, l = C_HEADS, C_CHUNK
    sk, sv = h * C_DK, h * C_DV
    q, k, v, g = jnp.split(u @ w_in, [sk, 2 * sk, 2 * sk + sv], axis=-1)
    qh = rotary(split_heads(q, h), positions, C_DK, C_ROPE_THETA).astype(F32)
    kh = rotary(split_heads(k, h), positions, C_DK, C_ROPE_THETA).astype(F32) * (C_DK ** -0.5)
    vh = split_heads(v, h).astype(F32)
    log_g = jnp.log1p(-jnp.exp2(-5.0 - jnp.arange(h, dtype=F32)))
    idx = jnp.arange(l, dtype=F32)
    diff = idx[:, None] - idx[None, :]
    intra = jnp.where(diff >= 0, jnp.exp(jnp.maximum(diff, 0.0)[None] * log_g[:, None, None]), 0.0)
    xi = jnp.exp((idx + 1.0)[None, :] * log_g[:, None])
    zeta = jnp.exp((l - 1.0 - idx)[None, :] * log_g[:, None])
    g_chunk = jnp.exp(l * log_g)

    def step(r_st, xs):
        qc, kc, vc = xs
        inner = jnp.einsum('bhts,bhsv->bhtv', jnp.einsum('bhtd,bhsd->bhts', qc, kc) * intra, vc)
        cross = jnp.einsum('bhtd,bhdv->bhtv', qc, r_st) * xi[None, :, :, None]
        r_new = g_chunk[None, :, None, None] * r_st + jnp.einsum('bhsd,bhsv->bhdv', kc * zeta[None, :, :, None], vc)
        return r_new, inner + cross

    _, yc = lax.scan(step, jnp.zeros((b, h, C_DK, C_DV), F32), (to_chunks(qh, l), to_chunks(kh, l), to_chunks(vh, l)))
    ys = from_chunks(yc)
    mu = jnp.mean(ys, axis=-1, keepdims=True)
    var = jnp.mean(jnp.square(ys - mu), axis=-1, keepdims=True)
    yn = (ys - mu) * lax.rsqrt(var + EPS) * g_out[:, None, :].astype(F32)
    y = merge_heads(yn).astype(u.dtype) * jax.nn.silu(g)
    return y @ w_out

def lru_combine(c1, c2):
    a1, b1 = c1
    a2, b2 = c2
    return a1 * a2, a2 * b1 + b2

def rglru_mixer(u, w_in, conv_w, conv_b, w_gates, b_gates, lru_param, w_out):
    b, s, _ = u.shape
    gate_br, xb = jnp.split(u @ w_in, 2, axis=-1)
    xc = lax.conv_general_dilated(xb, conv_w[:, None, :].astype(xb.dtype), window_strides=(1,),
                                  padding=[(D_CONV - 1, 0)], dimension_numbers=('NWC', 'WIO', 'NWC'),
                                  feature_group_count=D_RNN) + conv_b
    gates = jnp.einsum('bsnc,nce->bsne', xc.reshape(b, s, D_BLOCKS, D_BW), w_gates) + b_gates
    r = jax.nn.sigmoid(gates[..., :D_BW].astype(F32)).reshape(b, s, D_RNN)
    i = jax.nn.sigmoid(gates[..., D_BW:].astype(F32)).reshape(b, s, D_RNN)
    log_a = -LRU_C * r * jax.nn.softplus(-lru_param.astype(F32))
    a = jnp.exp(log_a)
    bterm = jnp.sqrt(-jnp.expm1(2.0 * log_a)) * (i * xc.astype(F32))
    _, hs = lax.associative_scan(lru_combine, (a, bterm), axis=1)
    y = hs.astype(u.dtype) * jax.nn.gelu(gate_br)
    return y @ w_out

def swiglu(u, w_in, w_out):
    gt, up = jnp.split(u @ w_in, 2, axis=-1)
    return (jax.nn.silu(gt) * up) @ w_out

def second_inputs(seed: int = 0) -> dict:
    key = jax.random.key(seed)
    ks = list(jax.random.split(key, 32))

    def rnd(shape, scale):
        return scale * jax.random.normal(ks.pop(), shape, F32)

    def gain(shape):
        return 1.0 + rnd(shape, 0.02)

    x = rnd((BATCH, SEQ, D_MODEL), 1.0)
    offs = jax.random.randint(ks.pop(), (BATCH, 1), 0, 1024, dtype=jnp.int32)
    positions = jnp.arange(SEQ, dtype=jnp.int32)[None, :] + offs
    norm_mix = gain((DEPTH_2, D_MODEL))
    norm_ffn = gain((DEPTH_2, D_MODEL))
    ffn_w_in = rnd((DEPTH_2, D_MODEL, 2 * D_FF), D_MODEL ** -0.5)
    ffn_w_out = rnd((DEPTH_2, D_FF, D_MODEL), OUT_SCALE * D_FF ** -0.5)
    a_w_in = rnd((N_LAYERS_A, D_MODEL, A_IN), D_MODEL ** -0.5)
    b_i = -1.0 + rnd((N_LAYERS_A, A_HEADS_2), 0.1)
    b_f = jnp.linspace(3.0, 6.0, A_HEADS_2, dtype=F32)[None, :] + rnd((N_LAYERS_A, A_HEADS_2), 0.1)
    a_b_gates = jnp.concatenate([b_i, b_f], axis=-1)
    a_g_out = gain((N_LAYERS_A, A_HEADS_2, A_DV))
    a_w_out = rnd((N_LAYERS_A, A_HEADS_2 * A_DV, D_MODEL), OUT_SCALE * (A_HEADS_2 * A_DV) ** -0.5)
    b_w_in = rnd((N_LAYERS_B, D_MODEL, B_IN), D_MODEL ** -0.5)
    b_g_q = gain((N_LAYERS_B, B_DH))
    b_g_k = gain((N_LAYERS_B, B_DH))
    b_w_out = rnd((N_LAYERS_B, B_HEADS_2 * B_DH, D_MODEL), OUT_SCALE * (B_HEADS_2 * B_DH) ** -0.5)
    c_w_in = rnd((N_LAYERS_C, D_MODEL, C_IN), D_MODEL ** -0.5)
    c_g_out = gain((N_LAYERS_C, C_HEADS, C_DV))
    c_w_out = rnd((N_LAYERS_C, C_HEADS * C_DV, D_MODEL), OUT_SCALE * (C_HEADS * C_DV) ** -0.5)
    d_w_in = rnd((N_LAYERS_D, D_MODEL, 2 * D_RNN), D_MODEL ** -0.5)
    d_conv_w = rnd((N_LAYERS_D, D_CONV, D_RNN), D_CONV ** -0.5)
    d_conv_b = rnd((N_LAYERS_D, D_RNN), 0.02)
    d_w_gates = rnd((N_LAYERS_D, D_BLOCKS, D_BW, 2 * D_BW), D_BW ** -0.5)
    d_b_gates = rnd((N_LAYERS_D, D_BLOCKS, 2 * D_BW), 0.1)
    a0 = jax.random.uniform(ks.pop(), (N_LAYERS_D, D_RNN), F32, minval=0.9, maxval=0.999)
    d_lru = jnp.log(a0) - jnp.log1p(-a0)
    d_w_out = rnd((N_LAYERS_D, D_RNN, D_MODEL), OUT_SCALE * D_RNN ** -0.5)
    return {'x': x, 'positions': positions, 'norm_mix': norm_mix, 'norm_ffn': norm_ffn,
            'ffn_w_in': ffn_w_in, 'ffn_w_out': ffn_w_out,
            'a_w_in': a_w_in, 'a_b_gates': a_b_gates, 'a_g_out': a_g_out, 'a_w_out': a_w_out,
            'b_w_in': b_w_in, 'b_g_q': b_g_q, 'b_g_k': b_g_k, 'b_w_out': b_w_out,
            'c_w_in': c_w_in, 'c_g_out': c_g_out, 'c_w_out': c_w_out,
            'd_w_in': d_w_in, 'd_conv_w': d_conv_w, 'd_conv_b': d_conv_b, 'd_w_gates': d_w_gates,
            'd_b_gates': d_b_gates, 'd_lru': d_lru, 'd_w_out': d_w_out}

def second_block(x, positions, norm_mix, norm_ffn, ffn_w_in, ffn_w_out,
              a_w_in, a_b_gates, a_g_out, a_w_out,
              b_w_in, b_g_q, b_g_k, b_w_out,
              c_w_in, c_g_out, c_w_out,
              d_w_in, d_conv_w, d_conv_b, d_w_gates, d_b_gates, d_lru, d_w_out):
    h = x
    for layer in range(DEPTH_2):
        mixer, r = layer % N_MIXERS, layer // N_MIXERS
        u = rmsnorm(h, norm_mix[layer])
        if mixer == 0:
            y = mlstm_mixer(u, a_w_in[r], a_b_gates[r], a_g_out[r], a_w_out[r])
        elif mixer == 1:
            y = moba_mixer(u, positions, b_w_in[r], b_g_q[r], b_g_k[r], b_w_out[r])
        elif mixer == 2:
            y = retention_mixer(u, positions, c_w_in[r], c_g_out[r], c_w_out[r])
        else:
            y = rglru_mixer(u, d_w_in[r], d_conv_w[r], d_conv_b[r], d_w_gates[r], d_b_gates[r], d_lru[r], d_w_out[r])
        h = h + y
        h = h + swiglu(rmsnorm(h, norm_ffn[layer]), ffn_w_in[layer], ffn_w_out[layer])
    return h


def setup_inputs(seed=0):
    out = dict(first_inputs(seed))
    for name, value in second_inputs(seed + 1).items():
        if name != "x":
            out[name + "_2"] = value
    return out


def reference(
    x, c, ctx, c_ctx, w_ada, b_ada, norm_attn, w_in, q_norm_a, k_norm_a, q_norm_b, k_norm_b,
    lambda_q1, lambda_k1, lambda_q2, lambda_k2, subln_b, w_oa, w_ob, w_out, norm_mlp, router_w,
    router_b, w_gate, b_gate, w_up, b_up, w_down, b_down, positions_2, norm_mix_2, norm_ffn_2,
    ffn_w_in_2, ffn_w_out_2, a_w_in_2, a_b_gates_2, a_g_out_2, a_w_out_2, b_w_in_2, b_g_q_2,
    b_g_k_2, b_w_out_2, c_w_in_2, c_g_out_2, c_w_out_2, d_w_in_2, d_conv_w_2, d_conv_b_2,
    d_w_gates_2, d_b_gates_2, d_lru_2, d_w_out_2,
):
    x = first_block(
        x, c, ctx, c_ctx, w_ada, b_ada, norm_attn, w_in, q_norm_a, k_norm_a, q_norm_b, k_norm_b,
        lambda_q1, lambda_k1, lambda_q2, lambda_k2, subln_b, w_oa, w_ob, w_out, norm_mlp,
        router_w, router_b, w_gate, b_gate, w_up, b_up, w_down, b_down,
    )
    return second_block(
        x, positions_2, norm_mix_2, norm_ffn_2, ffn_w_in_2, ffn_w_out_2, a_w_in_2, a_b_gates_2,
        a_g_out_2, a_w_out_2, b_w_in_2, b_g_q_2, b_g_k_2, b_w_out_2, c_w_in_2, c_g_out_2,
        c_w_out_2, d_w_in_2, d_conv_w_2, d_conv_b_2, d_w_gates_2, d_b_gates_2, d_lru_2,
        d_w_out_2,
    )


_drawn_inputs = setup_inputs


def setup_inputs(seed=0):
    import zlib

    import numpy as np

    out = dict(_drawn_inputs(seed))
    spreads = {}
    factors = {'norm_attn': 4.703,
     'q_norm_a': 8.0,
     'k_norm_a': 8.0,
     'q_norm_b': 7.121,
     'k_norm_b': 7.069,
     'lambda_q1': 4.512,
     'lambda_q2': 8.0,
     'lambda_k2': 4.711,
     'subln_b': 4.081,
     'router_b': 4.101,
     'b_gate': 8.0,
     'b_up': 8.0,
     'b_down': 8.0,
     'norm_mix_2': 4.642,
     'norm_ffn_2': 5.021,
     'a_g_out_2': 8.0,
     'b_g_q_2': 8.0,
     'b_g_k_2': 8.0}
    for name, (base, spread) in spreads.items():
        noise = np.random.default_rng([zlib.crc32(name.encode()), seed]).standard_normal(out[name].shape)
        drawn = base * np.exp(spread * noise) if base else spread * noise
        out[name] = jnp.asarray(drawn.astype(out[name].dtype))
    for name, factor in factors.items():
        out[name] = (out[name] * factor).astype(out[name].dtype)
    return out
```

```python
from contextlib import ExitStack
import math

import numpy as np
import concourse.bass as bass
import concourse.mybir as mybir

F32 = mybir.dt.float32
I32 = mybir.dt.int32
ALU = mybir.AluOpType
ACT = mybir.ActivationFunctionType
AX = mybir.AxisListType.X

T = 256
D = 1024
KT = 8
NE = 32
EPS = 1e-6
NEG = -1e30
LAM_INIT = 0.8 - 0.6 * math.exp(0.0)
DFF = 2816
FK = DFF // 128
SLOT = 4096
NSLOT = 6
ARENA = 21504

PCOL = {}
_at = 0
for _name, _n in (("norm_attn", 8), ("qna", 1), ("kna", 1), ("qnb", 1), ("knb", 1), ("subln", 1),
                  ("norm_mlp", 8), ("c2", 16), ("b_ada", 96), ("b_gate", 256), ("b_up", 256),
                  ("norm_mix", 16), ("norm_ffn", 16), ("a_g_out", 8), ("gq", 1), ("gk", 1),
                  ("lam", 4), ("bi", 1), ("bf", 1)):
    PCOL[_name] = _at
    _at += _n
NP = _at

CCOL = {}
_at = 0
for _name, _n in (("ident", 128), ("ones", 128), ("blk", 128), ("r1", 128), ("r2", 128), ("swp", 128),
                  ("cos1", 256), ("sin1", 256), ("mask0", 256), ("mask1", 256), ("inv", 1)):
    CCOL[_name] = _at
    _at += _n
NCC = _at


def shape_constants():
    c = np.zeros((128, NCC), np.float32)

    def put(name, a):
        c[:, CCOL[name]:CCOL[name] + a.shape[1]] = a

    i = np.arange(128)
    put("ident", np.eye(128, dtype=np.float32))
    put("ones", np.ones((128, 128), np.float32))
    put("blk", (i[:, None] // 64 == i[None, :] // 64).astype(np.float32))
    r = np.zeros((128, 128), np.float32)
    r[i[1::2], i[0::2]] = -1.0
    r[i[0::2], i[1::2]] = 1.0
    put("r1", r)
    r = np.zeros((128, 128), np.float32)
    r[i[16:32], i[0:16]] = -1.0
    r[i[0:16], i[16:32]] = 1.0
    put("r2", r)
    put("swp", ((i[:, None] + 64) % 128 == i[None, :]).astype(np.float32))
    n = np.arange(T)
    inv = (1.0 / (np.float32(10000.0) ** (np.arange(16, dtype=np.float32) / np.float32(16)))).astype(np.float32)
    ang = np.concatenate([(n // 64).astype(np.float32)[:, None] * inv,
                          (n % 64).astype(np.float32)[:, None] * inv], axis=1)
    pair = (i % 64) // 2
    put("cos1", np.cos(ang.astype(np.float64)).astype(np.float32).T[pair])
    put("sin1", np.sin(ang.astype(np.float64)).astype(np.float32).T[pair])
    for q in range(2):
        put(f"mask{q}", np.where(n[None, :] <= i[:, None] + 128 * q, 0.0, NEG).astype(np.float32))
    iv = np.zeros(128, np.float32)
    half = (np.float32(500000.0) ** (-np.arange(16, dtype=np.float32) * np.float32(2.0 / 32))).astype(np.float32)
    iv[0:16] = half
    iv[16:32] = half
    put("inv", iv[:, None])
    return c


class Queue:

    def __init__(self, sem):
        self.sem, self.n, self.items, self.met = sem, 0, [], {}

    def _waits(self, needs):
        top = {}

        def walk(x):
            if x is None:
                return
            if isinstance(x, list):
                for y in x:
                    walk(y)
                return
            k = id(x[0])
            if x[1] > self.met.get(k, 0) and x[1] > top.get(k, (None, 0))[1]:
                top[k] = x

        for x in needs:
            walk(x)
        for k, x in top.items():
            self.met[k] = x[1]
        return list(top.values())

    def __call__(self, fn, *needs):
        self.n += 1
        self.items.append((self._waits(needs), fn, self.sem, 1))
        return (self.sem, self.n)

    def dma(self, fn, sem, count, *needs):
        self.items.append((self._waits(needs), fn, sem, 16))
        return (sem, count)

    def last(self):
        return (self.sem, self.n)

    def wait(self, *needs):
        self.items.append((self._waits(needs), None, None, 0))

    def replay(self, eng):
        for waits, fn, sem, inc in self.items:
            for s, v in waits:
                eng.wait_ge(s, v)
            if fn is not None:
                fn(eng).then_inc(sem, inc)


class Ring:

    def __init__(self, aps):
        self.aps, self.free = aps, [(k, []) for k in range(len(aps))]

    def take(self):
        assert self.free, "no buffer of the ring is free"
        k, readers = self.free.pop(0)
        return k, self.aps[k], readers

    def give(self, k, *readers):
        self.free.append((k, list(readers)))


def pipeline(gens, width):
    gens, active = list(gens), []
    while gens or active:
        if gens and len(active) < width:
            active.append(gens.pop(0))
        still = []
        for g in active:
            try:
                next(g)
                still.append(g)
            except StopIteration:
                pass
        active = still


def build(nc, A, stage=99):
    with ExitStack() as ctx:
        def sb(name, shape, dt=F32):
            return ctx.enter_context(nc.sbuf_tensor(name, shape, dt))

        def sem(name):
            return ctx.enter_context(nc.semaphore(name))

        pe, dve, act, pool, sp = (Queue(sem(f"s_{n}")) for n in ("pe", "dve", "act", "pool", "sp"))

        con = sb("con", [128, NCC])
        par = sb("par", [128, NP])
        xT = sb("xT", [128, KT, T])
        bdn = sb("bdn", [NE, D])
        rw = sb("rw", [128, KT, NE])
        rb = sb("rb", [128, NE])
        wgt = sb("wgt", [128, KT, 8])
        pos = sb("pos", [128, T], I32)
        small = sb("small", [128, 512])
        arena = sb("arena", [128, ARENA])
        ringt = sb("ring", [128, NSLOT, SLOT])
        PS = [ctx.enter_context(nc.psum_tensor(f"ps{i}", [128, 512], F32)) for i in range(8)]

        s_ld = sem("s_ld")
        s_slot = [sem(f"s_slot{i}") for i in range(NSLOT)]
        s_out = sem("s_out")

        def C(name, w=128, p=128):
            return con[0:p, CCOL[name]:CCOL[name] + w]

        def P(name, j=0, w=1, p=128):
            return par[0:p, PCOL[name] + j:PCOL[name] + j + w]

        nld = [0]

        def load(dst, src):
            nld[0] += 16
            act.dma(lambda e: e.dma_start(dst, src), s_ld, nld[0])

        at = [0]

        def alloc(cols, p=128):
            a = arena[0:p, at[0]:at[0] + cols]
            at[0] += cols
            assert at[0] <= ARENA, at[0]
            return a

        def alloc3(k, n, p=128):
            return alloc(k * n, p).rearrange("p (k n) -> p k n", k=k)

        smat = [0]

        def tiny(cols, p=128):
            a = small[0:p, smat[0]:smat[0] + cols]
            smat[0] += cols
            assert smat[0] <= 512, smat[0]
            return a

        def phase():
            ends = [pe.last(), dve.last(), act.last(), pool.last()]
            for q in (pe, dve, act, pool):
                q.wait(ends)
            at[0] = 0
            smat[0] = 0

        ctxT = alloc3(KT, T)
        load(con[:, :], A["con"])
        load(par[:, :], A["par"])
        load(xT[:, :, :], A["xT"].rearrange("(k p) n -> p k n", p=128))
        load(ctxT[:, :, :], A["ctxT"].rearrange("(k p) n -> p k n", p=128))
        load(bdn[:, :], A["b_down"][0])
        load(rw[:, :, :], A["router_w"][0].rearrange("(k p) n -> p k n", p=128))
        load(rb[:, :], A["router_b"].partition_broadcast(128) if False else A["router_b"].broadcast_to([128, NE]))
        load(wgt[:, :, :], A["a_w_in"][0].rearrange("(k p) n -> p k n", p=128)[:, :, 3072:3080])
        load(pos[:, :], A["positions"].broadcast_to([128, T]))
        ld = (s_ld, nld[0])

        slot_n = [0] * NSLOT
        slots = Ring([ringt[:, i, :] for i in range(NSLOT)])

        class Slot:
            def __init__(self, src, k, n):
                self.k, ap, free = slots.take()
                self.ap = ap[:, 0:k * n].rearrange("p (k n) -> p k n", k=k)
                slot_n[self.k] += 16
                dst = self.ap
                self.tok = sp.dma(lambda e: e.dma_start(dst, src), s_slot[self.k], slot_n[self.k], free)

            def done(self, *toks):
                slots.give(self.k, *toks)

        def wcols(w, c0, n=512, k0=0, k=8):
            return Slot(w.rearrange("(k p) n -> p k n", p=128)[:, k0:k0 + k, c0:c0 + n], k, n)

        bank = Ring([p[:, :] for p in PS])

        def mms(out, pairs, *needs):
            pairs = list(pairs)

            def go(e):
                for i, (l, r) in enumerate(pairs):
                    m = e.matmul(out, l, r, start=i == 0, stop=i == len(pairs) - 1, skip_group_check=True)
                return m
            return pe(go, *needs)

        def tt(q, out, a, b, op, *needs):
            return q(lambda e: e.tensor_tensor(out, a, b, op), *needs)

        def ts(q, out, a, s1, s2, op0, op1, *needs):
            if op1 is None:
                return q(lambda e: e.tensor_scalar(out, a, s1, None, op0), *needs)
            return q(lambda e: e.tensor_scalar(out, a, s1, s2, op0, op1), *needs)

        def stt(out, a, s, b, op0, op1, *needs, acc=None):
            if acc is None:
                return dve(lambda e: e.scalar_tensor_tensor(out, a, s, b, op0, op1), *needs)
            return dve(lambda e: e.scalar_tensor_tensor(out, a, s, b, op0, op1, accum_out=acc), *needs)

        def af(out, a, func, *needs, **kw):
            return act(lambda e: e.activation(out, a, func, **kw), *needs)

        def inv_rms(out, ss_ps, ss_tok, n, eps, free):
            a = ts(dve, out, ss_ps, 1.0 / n, eps, ALU.mult, ALU.add, ss_tok, free)
            b = af(out, out, ACT.Sqrt, a)
            c = dve(lambda e: e.reciprocal(out, out), b)
            return c, a

        def norm_full(src, src_tok, rs, sqb, free):
            s = af(sqb[:, :, :], src, ACT.Square, src_tok, free)
            b, ps, fr = bank.take()
            m = mms(ps[:, 0:T], [(C("ones"), sqb[:, k, :]) for k in range(KT)], s, ld, fr)
            t, used = inv_rms(rs, ps[:, 0:T], m, D, EPS, free)
            bank.give(b, used)
            return t

        hx = alloc3(KT, T)
        hc = ctxT
        sq = alloc3(KT, T)
        mod = sb("mod", [128, 96])
        sc2 = tiny(16)
        t_silu = af(sc2, P("c2", 0, 16), ACT.Silu, ld)
        c2 = sc2.rearrange("p (k t) -> p k t", t=2)
        mod_tok = []

        def ada():
            for s in range(12):
                w = wcols(A["w_ada"][0], 512 * s)
                b, ps, fr = bank.take()
                for j in range(4):
                    m = mms(ps[:, 2 * j:2 * j + 2], [(w.ap[:, k, 128 * j:128 * j + 128], c2[:, k, :]) for k in range(KT)],
                            w.tok, t_silu, fr)
                w.done(m)
                t = tt(dve, mod[:, 8 * s:8 * s + 8], ps[:, 0:8], P("b_ada", 8 * s, 8), ALU.add, m, ld)
                bank.give(b, t)
                mod_tok.append(t)

        ada()

        def M(part, k, who=0):
            j = 2 * (8 * part + k) + who
            return mod[:, j:j + 1]

        ga1 = tiny(16)
        gm1 = tiny(8)
        m3 = mod[:, :].rearrange("p (c k t) -> p c k t", c=6, t=2)
        for who in range(2):
            g = ga1.rearrange("p (t k) -> p t k", t=2)[:, who, :]
            t_g = stt(g, m3[:, 1, :, who], 1.0, P("norm_attn", 0, 8), ALU.add, ALU.mult, mod_tok[-1], ld)

        def modulated(src, dst, rs, t_rs, gcol, shcol, t_g, scr):
            for k in range(KT):
                n, buf, fr = scr.take()
                a = stt(buf[:, 0:T], src[:, k, :], gcol(k), rs, ALU.mult, ALU.mult, t_rs, t_g, fr)
                b = af(dst[:, k, :], buf[:, 0:T], ACT.Identity, a, bias=shcol(k))
                scr.give(n, b)
            return b

        scrA = [alloc(512) for _ in range(6)]
        scr = Ring(scrA)
        rsx = alloc(T)
        rsc = alloc(T)
        t_rsx = norm_full(xT[:, :, :], ld, rsx, sq, None)
        t_rsc = norm_full(ctxT[:, :, :], ld, rsc, sq, pe.last())
        t_hx = modulated(xT, hx, rsx, t_rsx, lambda k: ga1[:, k:k + 1], lambda k: M(0, k, 0), t_g, scr)
        t_hc = modulated(ctxT, hc, rsc, t_rsc, lambda k: ga1[:, 8 + k:9 + k], lambda k: M(0, k, 1), t_g, scr)

        lam = tiny(1)
        nlam = tiny(1)
        lamt = tiny(4)
        b, ps, fr = bank.take()
        t = tt(dve, lamt[0:64, 0:2], P("lam", 0, 2, 64), P("lam", 2, 2, 64), ALU.mult, ld)
        t = mms(ps[:, 0:2], [(C("ones")[0:64, :], lamt[0:64, 0:2])], t, ld, fr)
        t = af(lamt[:, 2:4], ps[:, 0:2], ACT.Exp, t)
        bank.give(b, t)
        t = tt(dve, lam, lamt[:, 3:4], lamt[:, 2:3], ALU.subtract, t)
        t_lam = ts(dve, nlam, lam, -LAM_INIT, None, ALU.add, None, t)

        def head_norm(ps, tok, b, n, gcol, blk, div, dst, rot=None, needs=None):
            ks, s, fs = scr.take()
            kq, q, fq = scr.take()
            t1 = af(s[:, 0:n], ps[:, 0:n], ACT.Square, tok, fs)
            b2, ps2, fr2 = bank.take()
            m = mms(ps2[:, 0:n], [(blk, s[:, 0:n])], t1, fr2)
            yield
            t2, used = inv_rms(s[:, n:2 * n] if n <= 256 else s[:, 0:n], ps2[:, 0:n], m, div, EPS, None)
            rs = s[:, n:2 * n] if n <= 256 else s[:, 0:n]
            bank.give(b2, used)
            if rot is None:
                t3 = stt(dst, ps[:, 0:n], gcol, rs, ALU.mult, ALU.mult, t2, needs)
                bank.give(b, t3)
                scr.give(ks, t3)
                scr.give(kq)
                yield t3
                return
            R, cs, sn, t_rot = rot
            t3 = stt(q[:, 0:n], ps[:, 0:n], gcol, rs, ALU.mult, ALU.mult, t2, fq)
            bank.give(b, t3)
            yield
            b3, ps3, fr3 = bank.take()
            m = mms(ps3[:, 0:n], [(R, q[:, 0:n])], t3, fr3)
            t4 = tt(dve, q[:, n:2 * n], q[:, 0:n], cs, ALU.mult, t3, t_rot)
            t5 = tt(dve, s[:, 0:n], ps3[:, 0:n], sn, ALU.mult, m, t_rot)
            bank.give(b3, t5)
            t6 = tt(dve, dst, q[:, n:2 * n], s[:, 0:n], ALU.add, t4, t5, needs)
            scr.give(ks, t6)
            scr.give(kq, t6, m)
            yield t6

        qa = alloc3(4, T)
        qb = alloc3(4, T)
        kA = alloc(512)
        kS = alloc(512)
        kb = alloc3(4, 512)
        va = alloc3(4, 128)
        vb = alloc3(4, 512)
        rot1 = (C("r1"), C("cos1", 256), C("sin1", 256), ld)
        T_ = {}

        def run(gen, key):
            for t in gen:
                if t is not None:
                    T_[key] = t
                yield

        def qk_chunk(w, col, rhs, t_rhs, gcol, dst, rot, key, last=False):
            b, ps, fr = bank.take()
            m = mms(ps[:, 0:T], [(w.ap[:, k, col:col + 128], rhs[:, k, :]) for k in range(KT)], w.tok, t_rhs, fr)
            if last:
                w.done(m)
            yield
            yield from run(head_norm(ps, m, b, T, gcol, C("blk"), 64, dst, rot), key)

        W_in = A["w_in"][0]
        w0 = wcols(W_in, 0)
        w1 = wcols(W_in, 512)

        def v_tok(w, c0, n, rhs_tiles, dst, key, done=None):
            for j, (h, tk, q) in enumerate(rhs_tiles):
                b, ps, fr = bank.take()
                m = mms(ps[:, 0:n], [(h[:, k, 128 * q:128 * q + 128], w.ap[:, k, c0:c0 + n]) for k in range(KT)], w.tok, tk, fr)
                T_[key, j] = af(dst(j), ps[:, 0:n], ACT.Copy, m)
                bank.give(b, T_[key, j])
            return m

        four = [(hx, t_hx, 0), (hx, t_hx, 1), (hc, t_hc, 0), (hc, t_hc, 1)]
        pipeline([qk_chunk(w0, 128 * c, hx, t_hx, P("qna"), qa[:, c, :], rot1, ("qa", c), c == 3) for c in range(4)], 2)
        pipeline([qk_chunk(w1, 0, hx, t_hx, P("kna"), kA[:, 0:T], rot1, ("ka", 0)),
                  qk_chunk(w1, 0, hc, t_hc, P("kna"), kA[:, T:2 * T], None, ("ka", 1)),
                  qk_chunk(w1, 256, hx, t_hx, P("qnb"), qb[:, 0, :], rot1, ("qb", 0)),
                  qk_chunk(w1, 384, hx, t_hx, P("qnb"), qb[:, 1, :], rot1, ("qb", 1))], 2)
        m = v_tok(w1, 128, 128, four, lambda j: va[:, j, :], "va")
        w1.done(m)
        b, ps, fr = bank.take()
        m = mms(ps, [(C("swp"), kA)], T_["ka", 0], T_["ka", 1], fr)
        T_["kS"] = af(kS, ps, ACT.Copy, m)
        bank.give(b, T_["kS"])
        w2 = wcols(W_in, 1024)
        w3 = wcols(W_in, 1536)
        w4 = wcols(W_in, 2048)
        gens = [qk_chunk(w2, 0, hx, t_hx, P("qnb"), qb[:, 2, :], rot1, ("qb", 2)),
                qk_chunk(w2, 128, hx, t_hx, P("qnb"), qb[:, 3, :], rot1, ("qb", 3))]
        for c in range(4):
            w, col = (w2, 256 + 128 * c) if c < 2 else (w3, 128 * (c - 2))
            gens.append(qk_chunk(w, col, hx, t_hx, P("knb"), kb[:, c, 0:T], rot1, ("kb", c, 0)))
            gens.append(qk_chunk(w, col, hc, t_hc, P("knb"), kb[:, c, T:2 * T], None, ("kb", c, 1), c == 1))
        pipeline(gens, 2)
        m = v_tok(w3, 256, 256, four, lambda j: vb[:, j, 0:256], "vb0")
        w3.done(m)
        m = v_tok(w4, 0, 256, four, lambda j: vb[:, j, 256:512], "vb1")
        m_w4 = m

        yaT = alloc3(4, T)
        ybT = alloc3(4, T)
        PT = Ring([alloc3(4, T), alloc3(4, T)])

        smcol = sb("smcol", [128, 256])
        smn = [0]

        def smc():
            smn[0] = (smn[0] + 1) % 64
            return smcol[:, 4 * smn[0]:4 * smn[0] + 4]

        def softmax(qap, kap, n, scale, tq, mask=None):
            b, ps, fr = bank.take()
            m = mms(ps[:, 0:n], [(qap, kap)], tq, fr)
            yield
            st = smc()
            src = ps[:, 0:n]
            kp, p, fp = scr.take()
            if mask is not None:
                m = tt(dve, p[:, 0:n], ps[:, 0:n], mask, ALU.add, m, fp)
                bank.give(b, m)
                src = p[:, 0:n]
            t = dve(lambda e: e.tensor_reduce(st[:, 0:1], src, AX, ALU.max), m)
            t = ts(dve, st[:, 1:2], st[:, 0:1], -scale, None, ALU.mult, None, t)
            t = af(p[:, 0:n], src, ACT.Exp, t, fp, bias=st[:, 1:2], scale=scale, accum_out=st[:, 2:3])
            if mask is None:
                bank.give(b, t)
            yield
            t = dve(lambda e: e.reciprocal(st[:, 3:4], st[:, 2:3]), t)
            yield (kp, p, st, t)

        def turn(p, tp, n, pt, qt, ftok):
            b, ps, fr = bank.take()

            def go(e):
                for j in range(n // 128):
                    mm = e.transpose(ps[:, 128 * j:128 * j + 128], p[:, 128 * j:128 * j + 128], C("ident"))
                return mm
            m = pe(go, tp, fr, ld)
            src = ps[:, 0:n].rearrange("p (j q) -> p j q", q=128)
            t = af(pt[:, 0:n // 128, 128 * qt:128 * qt + 128], src, ACT.Copy, m, ftok)
            bank.give(b, t)
            return m, t

        def last_of(gen):
            r = None
            for r in gen:
                if r is None:
                    yield
            return r

        def head_a(h):
            g, half = h // 4, 64 * (h % 2)
            K, tk = (kA, [T_["ka", 0], T_["ka", 1]]) if g == h % 2 else (kS, T_["kS"])
            kpt, pt, fpt = PT.take()
            ev = []
            for qt in range(2):
                kp, p, st, t = yield from last_of(softmax(
                    qa[half:half + 64, h // 2, 128 * qt:128 * qt + 128], K[half:half + 64, :], 512, 0.125,
                    [tk, T_["qa", h // 2]]))
                t = ts(dve, p, p, st[:, 3:4], None, ALU.mult, None, t)
                yield
                m, e = turn(p, t, 512, pt, qt, fpt)
                scr.give(kp, m)
                ev.append(e)
            yield
            b, ps, fr = bank.take()
            m = mms(ps[half:half + 64, 0:T], [(va[:, j, 64 * g:64 * g + 64], pt[:, j, :]) for j in range(4)],
                    ev, [T_["va", j] for j in range(4)], fr)
            PT.give(kpt, m)
            T_["ya", h] = af(yaT[half:half + 64, h // 2, :], ps[half:half + 64, 0:T], ACT.Copy, m)
            bank.give(b, T_["ya", h])
            yield

        pipeline([head_a(h) for h in range(8)], 2)

        def head_b(h):
            kpt, pt, fpt = PT.take()
            ev = []
            for qt in range(2):
                r = []
                for mm in range(2):
                    half = 64 * mm
                    r.append((yield from last_of(softmax(
                        qb[half:half + 64, h, 128 * qt:128 * qt + 128], kb[half:half + 64, h, :], 512, 0.125,
                        [T_["qb", h], T_["kb", h, 0], T_["kb", h, 1]]))))
                (k0, p0, s0, t0), (k1, p1, s1, t1) = r
                t = tt(dve, s1[:, 3:4], s1[:, 3:4], nlam, ALU.mult, t1, t_lam)
                t = ts(dve, p1, p1, s1[:, 3:4], None, ALU.mult, None, t)
                t = stt(p0, p0, s0[:, 3:4], p1, ALU.mult, ALU.add, t, t0)
                scr.give(k1, t)
                yield
                m, e = turn(p0, t, 512, pt, qt, fpt)
                scr.give(k0, m)
                ev.append(e)
            yield
            b, ps, fr = bank.take()
            m = mms(ps[:, 0:T], [(vb[:, j, 128 * h:128 * h + 128], pt[:, j, :]) for j in range(4)],
                    ev, [T_["vb0", j] for j in range(4)], [T_["vb1", j] for j in range(4)], fr)
            PT.give(kpt, m)
            ks, s, fs = scr.take()
            t = af(s[:, 0:T], ps[:, 0:T], ACT.Square, m, fs)
            b2, ps2, fr2 = bank.take()
            m = mms(ps2[:, 0:T], [(C("ones"), s[:, 0:T])], t, fr2)
            yield
            t, used = inv_rms(s[:, T:2 * T], ps2[:, 0:T], m, 128, 1e-5, None)
            bank.give(b2, used)
            t = stt(s[:, 0:T], ps[:, 0:T], P("subln"), s[:, T:2 * T], ALU.mult, ALU.mult, t)
            bank.give(b, t)
            T_["yb", h] = ts(dve, ybT[:, h, :], s[:, 0:T], 1.0 - LAM_INIT, None, ALU.mult, None, t)
            scr.give(ks, T_["yb", h])
            yield

        pipeline([head_b(h) for h in range(4)], 2)

        att = [pe.last(), dve.last(), act.last()]
        sga = ctxT
        sgb = kb.rearrange("p k n -> p (k n)").rearrange("p (k n) -> p k n", k=8)
        w5 = wcols(W_in, 2560)
        w6 = wcols(W_in, 3072)
        w7 = wcols(W_in, 3584)
        w8 = wcols(W_in, 4096, 256)
        gcols = [(w4, 256), (w4, 384)] + [(w, 128 * j) for w in (w5, w6, w7) for j in range(4)] + [(w8, 0), (w8, 128)]
        for i, (w, col) in enumerate(gcols):
            b, ps, fr = bank.take()
            m = mms(ps[:, 0:T], [(w.ap[:, k, col:col + 128], hx[:, k, :]) for k in range(KT)], w.tok, fr, m_w4)
            if i in (1, 5, 9, 13, 15):
                w.done(m)
            dst = (sga if i < 8 else sgb)[:, i % 8, :]
            t = af(dst, ps[:, 0:T], ACT.Sigmoid, m, att)
            bank.give(b, t)
            T_["g", i] = t
        mg = sq
        for half in range(2):
            wa = wcols(A["w_oa"][0], 512 * half, 512, 0, 4)
            wb = wcols(A["w_ob"][0], 512 * half, 512, 0, 4)
            for j in range(4):
                c = 4 * half + j
                b, ps, fr = bank.take()
                m1 = mms(ps[:, 0:T], [(wa.ap[:, k, 128 * j:128 * j + 128], yaT[:, k, :]) for k in range(4)],
                         wa.tok, [T_["ya", h] for h in range(8)], fr)
                m2 = mms(ps[:, T:2 * T], [(wb.ap[:, k, 128 * j:128 * j + 128], ybT[:, k, :]) for k in range(4)],
                         wb.tok, [T_["yb", h] for h in range(4)])
                t1 = tt(dve, mg[:, c, :], ps[:, 0:T], sga[:, c, :], ALU.mult, m2, T_["g", c])
                kt_, u, fu = scr.take()
                t2 = tt(dve, u[:, 0:T], ps[:, T:2 * T], sgb[:, c, :], ALU.mult, m2, T_["g", 8 + c], fu)
                bank.give(b, t2)
                t3 = tt(dve, mg[:, c, :], mg[:, c, :], u[:, 0:T], ALU.add, t1, t2)
                scr.give(kt_, t3)
            wa.done(m1)
            wb.done(m2)

        def project_out(w_, K, src, t_src, gate, split=8):
            for half in range(2):
                ws = [wcols(w_, 512 * half, 512, k0, min(8, K - k0)) for k0 in range(0, K, 8)]
                for j in range(4):
                    c = 4 * half + j
                    b, ps, fr = bank.take()
                    prs = [(ws[k // 8].ap[:, k % 8, 128 * j:128 * j + 128], src[:, k, :]) for k in range(K)]
                    m = mms(ps[:, 0:T], prs, [w.tok for w in ws], t_src, fr)
                    if gate is None:
                        t = tt(dve, xT[:, c, :], ps[:, 0:T], xT[:, c, :], ALU.add, m)
                    else:
                        t = stt(xT[:, c, :], ps[:, 0:T], gate(c), xT[:, c, :], ALU.mult, ALU.add, m)
                    bank.give(b, t)
                for w in ws:
                    w.done(m)
            return t

        t_x = project_out(A["w_out"][0], KT, mg, t3, lambda c: M(2, c))

        def moe(t_x):
            phase()
            h2 = alloc3(KT, T)
            sq = alloc3(KT, T)
            acts = Ring([alloc3(KT, T), alloc3(KT, T)])
            scr = Ring([alloc(512) for _ in range(4)])
            rs = alloc(T)
            wT = alloc(T, NE)
            gm1 = tiny(8)
            t_g = stt(gm1, m3[:, 4, :, 0], 1.0, P("norm_mlp", 0, 8), ALU.add, ALU.mult)
            t_rs = norm_full(xT[:, :, :], t_x, rs, sq, None)
            t_h = modulated(xT, h2, rs, t_rs, lambda k: gm1[:, k:k + 1], lambda k: M(3, k), t_g, scr)
            tw = []
            for q in range(2):
                b, ps, fr = bank.take()
                m = mms(ps[:, 0:NE], [(h2[:, k, 128 * q:128 * q + 128], rw[:, k, :]) for k in range(KT)], t_h, fr)
                L, E_, G, Q, R_ = (tiny(NE) for _ in range(5))
                m8, s = tiny(8), tiny(4)
                t = tt(dve, L, ps[:, 0:NE], rb[:, :], ALU.add, m)
                bank.give(b, t)
                t = dve(lambda e, m8=m8, L=L: e.max(m8, L), t)
                t0 = ts(dve, s[:, 0:1], m8[:, 0:1], -1.0, None, ALU.mult, None, t)
                te = af(E_, L, ACT.Exp, t0, bias=s[:, 0:1])
                t1 = dve(lambda e, G=G, L=L, m8=m8, s=s: e.tensor_scalar(
                    G, L, m8[:, 3:4], 0.0, ALU.is_gt, ALU.add, accum_out=s[:, 1:2]), t)
                t2 = ts(dve, Q, L, m8[:, 3:4], None, ALU.is_equal, None, t)
                t3 = dve(lambda e, R_=R_, Q=Q: e.tensor_tensor_scan(R_, Q, Q, 0.0, ALU.add, ALU.bypass), t2)
                t4 = ts(dve, R_, R_, s[:, 1:2], 4.0, ALU.add, ALU.is_le, t3, t1)
                t5 = tt(dve, Q, Q, R_, ALU.mult, t4)
                t6 = tt(dve, G, G, Q, ALU.add, t5)
                t7 = stt(G, G, 1.0, E_, ALU.mult, ALU.mult, t6, te, acc=s[:, 2:3])
                t8 = dve(lambda e, s=s: e.reciprocal(s[:, 3:4], s[:, 2:3]), t7)
                t9 = ts(dve, G, G, s[:, 3:4], None, ALU.mult, None, t8)
                b, ps, fr = bank.take()
                m = pe(lambda e, ps=ps, G=G: e.transpose(ps[0:NE, 0:128], G, C("ident")), t9, fr)
                t = af(wT[:, 128 * q:128 * q + 128], ps[0:NE, 0:128], ACT.Copy, m)
                bank.give(b, t)
                tw.append(t)
            assert len(bank.free) == 8
            phase_y = [r for _, r in bank.free]
            banks = Ring([PS[i][:, :] for i in range(4)])
            banks.free = [(k, r) for k, r in bank.free if k < 4]
            Y = [PS[4 + c // 2][:, T * (c % 2):T * (c % 2) + T] for c in range(8)]
            for c in range(8):
                mY = pe(lambda e, c=c: e.matmul(Y[c], bdn[:, 128 * c:128 * c + 128], wT, start=c % 2 == 0, stop=False,
                                                skip_group_check=True), phase_y, tw)
            Wg, Wu, Wd = A["w_gate"][0], A["w_up"][0], A["w_down"][0]
            wb = Ring([alloc(T), alloc(T)])
            for ex in range(NE):
                ka, ac, fa = acts.take()
                kb_, bt, fb = banks.take()
                m = mms(bt[:, 0:T], [(C("ident")[0:NE, ex:ex + 1].to_broadcast([NE, 128]), wT)], tw, fb)
                kw, wbt, fw = wb.take()
                t_wb = af(wbt, bt[:, 0:T], ACT.Copy, m, fw)
                banks.give(kb_, t_wb)
                toks = []
                for half in range(2):
                    wg = wcols(Wg[ex], 512 * half)
                    wu = wcols(Wu[ex], 512 * half)
                    for j in range(4):
                        f = 4 * half + j
                        kp, ps, fr = banks.take()
                        m1 = mms(ps[:, 0:T], [(wg.ap[:, k, 128 * j:128 * j + 128], h2[:, k, :]) for k in range(KT)],
                                 wg.tok, fr)
                        m2 = mms(ps[:, T:2 * T], [(wu.ap[:, k, 128 * j:128 * j + 128], h2[:, k, :]) for k in range(KT)],
                                 wu.tok)
                        ks, s, fs = scr.take()
                        g, u = s[:, 0:T], s[:, T:2 * T]
                        t1 = ts(dve, g, ps[:, 0:T], P("b_gate", 8 * ex + f), 7.0, ALU.add, ALU.min, m2, fs)
                        t2 = ts(dve, u, ps[:, T:2 * T], P("b_up", 8 * ex + f), 7.0, ALU.add, ALU.min, m2, fs)
                        banks.give(kp, t1, t2)
                        t3 = af(ac[:, f, :], g, ACT.Sigmoid, t1, fa, scale=1.702)
                        t4 = ts(dve, u, u, -7.0, 1.0, ALU.max, ALU.add, t2)
                        t5 = tt(dve, u, u, wbt, ALU.mult, t4, t_wb)
                        t6 = tt(dve, g, g, u, ALU.mult, t5, t3)
                        t7 = tt(dve, ac[:, f, :], ac[:, f, :], g, ALU.mult, t6, t3)
                        scr.give(ks, t7)
                        toks.append(t7)
                    wg.done(m1)
                    wu.done(m2)
                wb.give(kw, toks[-1])
                for half in range(2):
                    wd = wcols(Wd[ex], 0, 1024, 4 * half, 4)
                    for j in range(4):
                        f = 4 * half + j

                        def go(e, wd=wd, j=j, f=f, ac=ac, last=ex == NE - 1 and f == 7):
                            for c in range(8):
                                m = e.matmul(Y[c], wd.ap[:, j, 128 * c:128 * c + 128], ac[:, f, :], start=False,
                                             stop=last, skip_group_check=True)
                            return m
                        m = pe(go, wd.tok, toks[f], mY)
                    wd.done(m)
                acts.give(ka, m)
            for c in range(8):
                t = stt(xT[:, c, :], Y[c], M(5, c), xT[:, c, :], ALU.mult, ALU.add, m)
            bank.free = banks.free + [(k, [t]) for k in range(4, 8)]
            return t

        if stage >= 2:
            t_x = moe(t_x)

        def normed(t_x, gname, layer):
            u = alloc3(KT, T)
            sq = alloc3(KT, T)
            rs = alloc(T)
            t_rs = norm_full(xT[:, :, :], t_x, rs, sq, None)
            for k in range(KT):
                t = stt(u[:, k, :], xT[:, k, :], P(gname, 8 * layer + k), rs, ALU.mult, ALU.mult, t_rs)
            return u, t, sq

        def ffn(t_x, layer):
            phase()
            u, t_u, sq = normed(t_x, "norm_ffn", layer)
            g = alloc3(FK, T)
            W = A["ffn_w_in"][layer]
            for s in range(11):
                w = wcols(W, 512 * s)
                for j in range(4):
                    c = 4 * s + j
                    b, ps, fr = bank.take()
                    m = mms(ps[:, 0:T], [(w.ap[:, k, 128 * j:128 * j + 128], u[:, k, :]) for k in range(KT)],
                            w.tok, t_u, fr)
                    if c < FK:
                        t = af(g[:, c, :], ps[:, 0:T], ACT.Silu, m)
                        T_["f", c] = t
                    else:
                        t = tt(dve, g[:, c - FK, :], ps[:, 0:T], g[:, c - FK, :], ALU.mult, m, T_["f", c - FK])
                    bank.give(b, t)
                w.done(m)
            return project_out(A["ffn_w_out"][layer], FK, g, t, None)

        def mlstm(t_x):
            nonlocal scr
            phase()
            u, t_u, sq = normed(t_x, "norm_mix", 0)
            scr = Ring([alloc(512) for _ in range(4)])
            qT = alloc3(4, T)
            kT = alloc3(4, T)
            v = alloc3(2, 1024)
            so = alloc3(8, T)
            y = sq
            qkT = Ring([alloc3(2, T), alloc3(2, T)])
            W = A["a_w_in"][0]
            ig, fg, tmp, F_, a_ = (alloc(T, 4) for _ in range(5))
            b, ps, fr = bank.take()
            m = mms(ps[0:4, 0:T], [(wgt[:, k, 0:4], u[:, k, :]) for k in range(KT)], t_u, fr)
            m = mms(ps[0:4, T:2 * T], [(wgt[:, k, 4:8], u[:, k, :]) for k in range(KT)])
            ti = ts(dve, ig, ps[0:4, 0:T], P("bi", p=4), None, ALU.add, None, m)
            t = ts(dve, fg, ps[0:4, T:2 * T], P("bf", p=4), None, ALU.add, None, m)
            bank.give(b, ti, t)
            t1 = af(tmp, fg, ACT.Abs, t)
            t1 = af(tmp, tmp, ACT.Exp, t1, scale=-1.0)
            t1 = ts(dve, tmp, tmp, 1.0, None, ALU.add, None, t1)
            t1 = af(tmp, tmp, ACT.Ln, t1)
            t = stt(fg, fg, 0.0, tmp, ALU.min, ALU.subtract, t1, t)
            t = dve(lambda e: e.tensor_tensor_scan(F_, fg, fg, 0.0, ALU.add, ALU.bypass), t)
            t_a = tt(dve, a_, ig, F_, ALU.subtract, t, ti)
            Fc = tiny(8)
            b, ps, fr = bank.take()
            for q in range(2):
                m = mms(ps[:, 4 * q:4 * q + 4], [(F_[:, 128 * q:128 * q + 128], C("ident", 4, 4))], t, fr)
            t_F = dve(lambda e, ps=ps: e.tensor_copy(Fc, ps[:, 0:8]), m)
            bank.give(b, t_F)
            tq = {}
            for which, dst in ((0, qT), (1, kT)):
                w = wcols(W, 512 * which)
                for j in range(4):
                    b, ps, fr = bank.take()
                    m = mms(ps[:, 0:T], [(w.ap[:, k, 128 * j:128 * j + 128], u[:, k, :]) for k in range(KT)],
                            w.tok, fr)
                    t = af(dst[:, j, :], ps[:, 0:T], ACT.Copy, m)
                    bank.give(b, t)
                    tq[which, j] = t
                w.done(m)
            tv = []
            for half in range(2):
                w = wcols(W, 1024 + 512 * half)
                for q in range(2):
                    b, ps, fr = bank.take()
                    m = mms(ps, [(u[:, k, 128 * q:128 * q + 128], w.ap[:, k, :]) for k in range(KT)], w.tok, fr)
                    t = af(v[:, q, 512 * half:512 * half + 512], ps, ACT.Copy, m)
                    bank.give(b, t)
                    tv.append(t)
                w.done(m)
            for half in range(2):
                w = wcols(W, 2048 + 512 * half)
                for j in range(4):
                    b, ps, fr = bank.take()
                    m = mms(ps[:, 0:T], [(w.ap[:, k, 128 * j:128 * j + 128], u[:, k, :]) for k in range(KT)],
                            w.tok, fr)
                    t_o = af(so[:, 4 * half + j, :], ps[:, 0:T], ACT.Sigmoid, m)
                    bank.give(b, t_o)
                w.done(m)
            ty = []

            def head(h):
                kq, qk, fqk = qkT.take()
                b, aps, fr = bank.take()
                ma = mms(aps[:, 0:T], [(C("ident", p=4)[:, h:h + 1].to_broadcast([4, 128]), a_)], t_a, fr)
                mz = None
                if True:
                    mz = dve(lambda e: e.memset(qk[:, 1, 0:128], 0.0), fqk)
                ev = [mz]
                for q in range(2):
                    n = 128 * (q + 1)
                    b2, sp_, fr2 = bank.take()
                    ms = mms(sp_[:, 0:n], [(qT[:, h, 128 * q:128 * q + 128], kT[:, h, 0:n])], tq[0, h], tq[1, h], fr2)
                    ks, s, fs = scr.take()
                    st = smc()
                    am, w = s[:, 0:n], s[:, T:T + n]
                    t1 = tt(dve, am, aps[:, 0:n], C(f"mask{q}", n), ALU.add, ma, fs)
                    t2 = dve(lambda e, st=st, am=am: e.tensor_reduce(st[:, 0:1], am, AX, ALU.max), t1)
                    t3 = ts(dve, st[:, 1:2], st[:, 0:1], 0.0, -1.0, ALU.max, ALU.mult, t2)
                    t4 = af(w, am, ACT.Exp, t3, bias=st[:, 1:2])
                    yield
                    t5 = stt(am, sp_[:, 0:n], 128.0 ** -0.5, w, ALU.mult, ALU.mult, t4, ms, acc=st[:, 2:3])
                    bank.give(b2, t5)
                    t6 = tt(dve, st[:, 1:2], st[:, 1:2], Fc[:, 4 * q + h:4 * q + h + 1], ALU.subtract, t4, t_F)
                    t7 = af(st[:, 1:2], st[:, 1:2], ACT.Exp, t6)
                    t8 = af(st[:, 2:3], st[:, 2:3], ACT.Abs, t5)
                    t9 = tt(dve, st[:, 2:3], st[:, 2:3], st[:, 1:2], ALU.max, t7, t8)
                    t10 = dve(lambda e, st=st: e.reciprocal(st[:, 3:4], st[:, 2:3]), t9)
                    t11 = ts(dve, am, am, st[:, 3:4], None, ALU.mult, None, t10)
                    yield
                    mt, te = turn(am, t11, n, qk, q, fqk)
                    scr.give(ks, mt)
                    ev.append(te)
                bank.give(b, t1)
                yield
                b, ps, fr = bank.take()
                for c in range(2):
                    m = mms(ps[:, T * c:T * c + T],
                            [(v[:, j, 256 * h + 128 * c:256 * h + 128 * c + 128], qk[:, j, :]) for j in range(2)],
                            ev, tv, fr)
                qkT.give(kq, m)
                ks, s, fs = scr.take()
                t = af(s, ps, ACT.Square, m, fs)
                b2, ps2, fr2 = bank.take()
                m2 = mms(ps2[:, 0:T], [(C("ones"), s[:, 0:T]), (C("ones"), s[:, T:2 * T])], t, fr2)
                yield
                t, used = inv_rms(s[:, 0:T], ps2[:, 0:T], m2, 256, EPS, None)
                bank.give(b2, used)
                for c in range(2):
                    j = 2 * h + c
                    t1 = stt(y[:, j, :], ps[:, T * c:T * c + T], P("a_g_out", j), s[:, 0:T], ALU.mult, ALU.mult, t)
                    t2 = tt(dve, y[:, j, :], y[:, j, :], so[:, j, :], ALU.mult, t1, t_o)
                bank.give(b, t1)
                scr.give(ks, t1)
                ty.append(t2)
                yield

            pipeline([head(h) for h in range(4)], 2)
            return project_out(A["a_w_out"][0], KT, y, ty, None)

        def moba(t_x):
            nonlocal scr
            phase()
            u, t_u, sq = normed(t_x, "norm_mix", 1)
            scr = Ring([alloc(512) for _ in range(4)])
            qT = alloc3(8, T)
            kT = alloc3(8, T)
            v = alloc3(2, 1024)
            y = alloc3(8, T)
            cs, sn = alloc(T), alloc(T)
            PT = Ring([alloc3(2, T), alloc3(2, T)])
            ang, kk, r = alloc(T), alloc(T), alloc(T)
            t = dve(lambda e: e.tensor_copy(r, pos[:, :]), ld)
            t_ang = ts(dve, ang, r, C("inv", 1), None, ALU.mult, None, t)
            MAGIC = 12582912.0
            C1, C2 = 6.28125, 0.0019350051879882812
            C3 = 2.0 * math.pi - C1 - C2
            tr = None
            for dst, shift in ((sn, 0.0), (cs, 0.25)):
                t = ts(dve, kk, ang, 1.0 / (2.0 * math.pi), shift, ALU.mult, ALU.add, t_ang, tr)
                t = ts(dve, kk, kk, MAGIC, None, ALU.add, None, t)
                t = ts(dve, kk, kk, MAGIC, None, ALU.subtract, None, t)
                t = stt(r, kk, -C1, ang, ALU.mult, ALU.add, t)
                t = stt(r, kk, -C2, r, ALU.mult, ALU.add, t)
                t = stt(r, kk, -C3, r, ALU.mult, ALU.add, t)
                t = ts(dve, r, r, 2.0 * math.pi * shift, 3.1415925, ALU.add, ALU.min, t)
                t = ts(dve, r, r, -3.1415925, None, ALU.max, None, t)
                tr = af(dst, r, ACT.Sin, t)
            rot2 = (C("r2"), cs, sn, tr)
            W = A["b_w_in"][0]

            def chunk(w, col, gcol, dst, key, last):
                b, ps, fr = bank.take()
                m = mms(ps[:, 0:T], [(w.ap[:, k, col:col + 128], u[:, k, :]) for k in range(KT)], w.tok, t_u, fr)
                if last:
                    w.done(m)
                yield
                yield from run(head_norm(ps, m, b, T, gcol, C("ones"), 128, dst, rot2), key)

            ws = [wcols(W, 512 * s) for s in range(4)]
            pipeline([chunk(ws[s], 128 * j, P("gq") if s < 2 else P("gk"), (qT if s < 2 else kT)[:, 4 * (s % 2) + j, :],
                            ("m", s // 2, 4 * (s % 2) + j), j == 3) for s in range(4) for j in range(4)], 2)
            tv = []
            for half in range(2):
                w = wcols(W, 2048 + 512 * half)
                for q in range(2):
                    b, ps, fr = bank.take()
                    m = mms(ps, [(u[:, k, 128 * q:128 * q + 128], w.ap[:, k, :]) for k in range(KT)], w.tok, fr)
                    t = af(v[:, q, 512 * half:512 * half + 512], ps, ACT.Copy, m)
                    bank.give(b, t)
                    tv.append(t)
                w.done(m)
            ty = []

            def head(h):
                kq, pt, fqk = PT.take()
                ev = [dve(lambda e: e.memset(pt[:, 1, 0:128], 0.0), fqk)]
                for q in range(2):
                    n = 128 * (q + 1)
                    kp, p, st, t = yield from last_of(softmax(
                        qT[:, h, 128 * q:128 * q + 128], kT[:, h, 0:n], n, 128.0 ** -0.5,
                        [T_["m", 0, h], T_["m", 1, h]], mask=C(f"mask{q}", n)))
                    t = ts(dve, p[:, 0:n], p[:, 0:n], st[:, 3:4], None, ALU.mult, None, t)
                    yield
                    mt, te = turn(p, t, n, pt, q, fqk)
                    scr.give(kp, mt)
                    ev.append(te)
                yield
                b, ps, fr = bank.take()
                m = mms(ps[:, 0:T], [(v[:, j, 128 * h:128 * h + 128], pt[:, j, :]) for j in range(2)], ev, tv, fr)
                PT.give(kq, m)
                t = af(y[:, h, :], ps[:, 0:T], ACT.Copy, m)
                bank.give(b, t)
                ty.append(t)
                yield

            pipeline([head(h) for h in range(8)], 2)
            return project_out(A["b_w_out"][0], KT, y, ty, None)

        if stage >= 3:
            t_x = mlstm(t_x)
        if stage >= 4:
            t_x = ffn(t_x, 0)
        if stage >= 5:
            t_x = moba(t_x)
        if stage >= 6:
            t_x = ffn(t_x, 1)

        end = sp.dma(lambda e: e.dma_start(A["out"].rearrange("(k p) n -> p k n", p=128), xT[:, :, :]), s_out, 16, t_x)
        sp.wait(end)

        block = ctx.enter_context(nc.Block())
        block.sync(sp.replay)
        block.scalar(act.replay)
        block.vector(dve.replay)
        block.gpsimd(pool.replay)
        block.tensor(pe.replay)


STAGE = 99
_DIRECT = ["b_down", "router_w", "router_b", "w_ada", "w_in", "w_oa", "w_ob", "w_out", "w_gate", "w_up", "w_down"]
_SECOND = {"a_w_in": "a_w_in_2", "a_w_out": "a_w_out_2", "b_w_in": "b_w_in_2", "b_w_out": "b_w_out_2",
           "ffn_w_in": "ffn_w_in_2", "ffn_w_out": "ffn_w_out_2", "positions": "positions_2"}


def kernel(**inputs):
    import numpy as _np
    import concourse.bacc as _bacc
    from concourse import mybir as _mybir
    from concourse.bass_utils import run_bass_kernel_spmd as _run

    I = {k: _np.asarray(v) for k, v in inputs.items()}
    par = _np.zeros((128, NP), _np.float32)

    def put(name, a):
        par[0:a.shape[0], PCOL[name]:PCOL[name] + a.shape[1]] = a

    def cols(v):
        return _np.ascontiguousarray(v.reshape(-1, 128).T)

    def twice(v):
        return _np.concatenate([v, v])[:, None]

    put("norm_attn", cols(I["norm_attn"][0]))
    put("qna", twice(I["q_norm_a"][0]))
    put("kna", twice(I["k_norm_a"][0]))
    put("qnb", twice(I["q_norm_b"][0]))
    put("knb", twice(I["k_norm_b"][0]))
    put("subln", cols(I["subln_b"][0]))
    put("norm_mlp", cols(I["norm_mlp"][0]))
    put("c2", _np.stack([cols(I["c"][0]), cols(I["c_ctx"])], axis=2).reshape(128, 16))
    put("b_ada", _np.repeat(cols(I["b_ada"][0]), 2, axis=1))
    put("b_gate", cols(I["b_gate"][0].reshape(-1)))
    put("b_up", cols(I["b_up"][0].reshape(-1)))
    put("norm_mix", cols(I["norm_mix_2"].reshape(-1)))
    put("norm_ffn", cols(I["norm_ffn_2"].reshape(-1)))
    put("a_g_out", cols(I["a_g_out_2"].reshape(-1)))
    put("gq", cols(I["b_g_q_2"][0]))
    put("gk", cols(I["b_g_k_2"][0]))
    put("lam", _np.stack([I["lambda_q1"][0], I["lambda_q2"][0], I["lambda_k1"][0], I["lambda_k2"][0]], axis=1))
    put("bi", I["a_b_gates_2"][0][0:4, None])
    put("bf", I["a_b_gates_2"][0][4:8, None])
    arrays = {"con": shape_constants(), "par": par,
              "xT": _np.ascontiguousarray(I["x"][0].T), "ctxT": _np.ascontiguousarray(I["ctx"][0].T)}
    for n in _DIRECT:
        arrays[n] = _np.ascontiguousarray(I[n])
    for n, src in _SECOND.items():
        arrays[n] = _np.ascontiguousarray(I[src])
    nc = _bacc.Bacc("TRN2", target_bir_lowering=False, num_devices=1)
    A = {n: nc.dram_tensor(f"in_{n}", a.shape, _mybir.dt.from_np(a.dtype), kind="ExternalInput").ap()
         for n, a in arrays.items()}
    A["out"] = nc.dram_tensor("out_0", (D, T), F32, kind="ExternalOutput").ap()
    build(nc, A, STAGE)
    r = _run(nc, [{f"in_{n}": a for n, a in arrays.items()}], core_ids=[0])
    return _np.ascontiguousarray(_np.asarray(r.results[0]["out_0"]).T)[None]
```

```python
from contextlib import ExitStack
import math

import numpy as np
import concourse.bass as bass
import concourse.mybir as mybir

F32 = mybir.dt.float32
I32 = mybir.dt.int32
ALU = mybir.AluOpType
ACT = mybir.ActivationFunctionType
AX = mybir.AxisListType.X

T = 256
D = 1024
KT = 8
NE = 32
EPS = 1e-6
NEG = -1e30
LAM_INIT = 0.8 - 0.6 * math.exp(0.0)
DFF = 2816
FK = DFF // 128
SLOT = 4096
NSLOT = 6
CAP = 96
LIMIT = CAP
ARENA = 21248

PCOL = {}
_at = 0
for _name, _n in (("norm_attn", 8), ("qna", 1), ("kna", 1), ("qnb", 1), ("knb", 1), ("subln", 1),
                  ("norm_mlp", 8), ("c2", 16), ("b_ada", 96), ("b_gate", 256), ("b_up", 256),
                  ("norm_mix", 16), ("norm_ffn", 16), ("a_g_out", 8), ("gq", 1), ("gk", 1),
                  ("lam", 4), ("bi", 1), ("bf", 1)):
    PCOL[_name] = _at
    _at += _n
NP = _at

CCOL = {}
_at = 0
for _name, _n in (("ident", 128), ("ones", 128), ("blk", 128), ("r1", 128), ("r2", 128), ("swp", 128),
                  ("cos1", 256), ("sin1", 256), ("mask0", 256), ("mask1", 256), ("inv", 1), ("iota", 128)):
    CCOL[_name] = _at
    _at += _n
NCC = _at


def shape_constants():
    c = np.zeros((128, NCC), np.float32)

    def put(name, a):
        c[:, CCOL[name]:CCOL[name] + a.shape[1]] = a

    i = np.arange(128)
    put("ident", np.eye(128, dtype=np.float32))
    put("ones", np.ones((128, 128), np.float32))
    put("blk", (i[:, None] // 64 == i[None, :] // 64).astype(np.float32))
    r = np.zeros((128, 128), np.float32)
    r[i[1::2], i[0::2]] = -1.0
    r[i[0::2], i[1::2]] = 1.0
    put("r1", r)
    r = np.zeros((128, 128), np.float32)
    r[i[16:32], i[0:16]] = -1.0
    r[i[0:16], i[16:32]] = 1.0
    put("r2", r)
    put("swp", ((i[:, None] + 64) % 128 == i[None, :]).astype(np.float32))
    n = np.arange(T)
    inv = (1.0 / (np.float32(10000.0) ** (np.arange(16, dtype=np.float32) / np.float32(16)))).astype(np.float32)
    ang = np.concatenate([(n // 64).astype(np.float32)[:, None] * inv,
                          (n % 64).astype(np.float32)[:, None] * inv], axis=1)
    pair = (i % 64) // 2
    put("cos1", np.cos(ang.astype(np.float64)).astype(np.float32).T[pair])
    put("sin1", np.sin(ang.astype(np.float64)).astype(np.float32).T[pair])
    for q in range(2):
        put(f"mask{q}", np.where(n[None, :] <= i[:, None] + 128 * q, 0.0, NEG).astype(np.float32))
    iv = np.zeros(128, np.float32)
    half = (np.float32(500000.0) ** (-np.arange(16, dtype=np.float32) * np.float32(2.0 / 32))).astype(np.float32)
    iv[0:16] = half
    iv[16:32] = half
    put("inv", iv[:, None])
    put("iota", np.tile(np.arange(128, dtype=np.float32), (128, 1)))
    return c


class Queue:

    def __init__(self, sem):
        self.sem, self.n, self.items, self.met = sem, 0, [], {}

    def _waits(self, needs):
        top = {}

        def walk(x):
            if x is None:
                return
            if isinstance(x, list):
                for y in x:
                    walk(y)
                return
            k = id(x[0])
            if x[1] > self.met.get(k, 0) and x[1] > top.get(k, (None, 0))[1]:
                top[k] = x

        for x in needs:
            walk(x)
        for k, x in top.items():
            self.met[k] = x[1]
        return list(top.values())

    def __call__(self, fn, *needs):
        self.n += 1
        self.items.append((self._waits(needs), fn, self.sem, 1))
        return (self.sem, self.n)

    def dma(self, fn, sem, count, *needs):
        self.items.append((self._waits(needs), fn, sem, 16))
        return (sem, count)

    def last(self):
        return (self.sem, self.n)

    def wait(self, *needs):
        self.items.append((self._waits(needs), None, None, 0))

    def replay(self, eng):
        self.play(eng, self.items)

    def play(self, eng, items):
        for waits, fn, sem, inc in items:
            for s, v in waits:
                eng.wait_ge(s, v)
            if sem == "fork":
                flag, within, beyond = fn
                count = eng.value_load(flag, min_val=0, max_val=T)
                with eng.If(count <= inc):
                    self.play(eng, within)
                with eng.Else():
                    self.play(eng, beyond)
            elif sem == "pad":
                eng.sem_inc(self.sem, inc)
            elif fn is not None:
                fn(eng).then_inc(sem, inc)


class Ring:

    def __init__(self, aps):
        self.aps, self.free = aps, [(k, []) for k in range(len(aps))]

    def take(self):
        assert self.free, "no buffer of the ring is free"
        k, readers = self.free.pop(0)
        return k, self.aps[k], readers

    def give(self, k, *readers):
        self.free.append((k, list(readers)))


def pipeline(gens, width):
    gens, active = list(gens), []
    while gens or active:
        if gens and len(active) < width:
            active.append(gens.pop(0))
        still = []
        for g in active:
            try:
                next(g)
                still.append(g)
            except StopIteration:
                pass
        active = still


def build(nc, A, stage=99):
    with ExitStack() as ctx:
        def sb(name, shape, dt=F32):
            return ctx.enter_context(nc.sbuf_tensor(name, shape, dt))

        def sem(name):
            return ctx.enter_context(nc.semaphore(name))

        pe, dve, act, pool, sp = (Queue(sem(f"s_{n}")) for n in ("pe", "dve", "act", "pool", "sp"))

        con = sb("con", [128, NCC])
        par = sb("par", [128, NP])
        xT = sb("xT", [128, KT, T])
        bdn = sb("bdn", [NE, D])
        rw = sb("rw", [128, KT, NE])
        rb = sb("rb", [128, NE])
        wgt = sb("wgt", [128, KT, 8])
        pos = sb("pos", [128, T], I32)
        small = sb("small", [128, 640])
        arena = sb("arena", [128, ARENA])
        ringt = sb("ring", [128, NSLOT, SLOT])
        PS = [ctx.enter_context(nc.psum_tensor(f"ps{i}", [128, 512], F32)) for i in range(8)]

        s_ld = sem("s_ld")
        s_slot = [sem(f"s_slot{i}") for i in range(NSLOT)]
        s_out = sem("s_out")

        def C(name, w=128, p=128):
            return con[0:p, CCOL[name]:CCOL[name] + w]

        def P(name, j=0, w=1, p=128):
            return par[0:p, PCOL[name] + j:PCOL[name] + j + w]

        nld = [0]

        def load(dst, src):
            nld[0] += 16
            act.dma(lambda e: e.dma_start(dst, src), s_ld, nld[0])

        at = [0]

        def alloc(cols, p=128):
            a = arena[0:p, at[0]:at[0] + cols]
            at[0] += cols
            assert at[0] <= ARENA, at[0]
            return a

        def alloc3(k, n, p=128):
            return alloc(k * n, p).rearrange("p (k n) -> p k n", k=k)

        smat = [0]

        def tiny(cols, p=128):
            a = small[0:p, smat[0]:smat[0] + cols]
            smat[0] += cols
            assert smat[0] <= 640, smat[0]
            return a

        def phase():
            ends = [pe.last(), dve.last(), act.last(), pool.last()]
            for q in (pe, dve, act, pool):
                q.wait(ends)
            at[0] = 0
            smat[0] = 0

        ctxT = alloc3(KT, T)
        load(con[:, :], A["con"])
        load(par[:, :], A["par"])
        load(xT[:, :, :], A["xT"].rearrange("(k p) n -> p k n", p=128))
        load(ctxT[:, :, :], A["ctxT"].rearrange("(k p) n -> p k n", p=128))
        load(bdn[:, :], A["b_down"][0])
        load(rw[:, :, :], A["router_w"][0].rearrange("(k p) n -> p k n", p=128))
        load(rb[:, :], A["router_b"].partition_broadcast(128) if False else A["router_b"].broadcast_to([128, NE]))
        load(wgt[:, :, :], A["a_w_in"][0].rearrange("(k p) n -> p k n", p=128)[:, :, 3072:3080])
        load(pos[:, :], A["positions"].broadcast_to([128, T]))
        ld = (s_ld, nld[0])

        slot_n = [0] * NSLOT
        slots = Ring([ringt[:, i, :] for i in range(NSLOT)])

        class Slot:
            def __init__(self, key, src, k, n):
                self.key = key
                self.k, ap, free = slots.take()
                self.ap = ap[:, 0:k * n].rearrange("p (k n) -> p k n", k=k)
                slot_n[self.k] += 16
                dst = self.ap
                self.tok = sp.dma(lambda e: e.dma_start(dst, src), s_slot[self.k], slot_n[self.k], free)

            def done(self, *toks):
                slots.give(self.k, *toks)

        early = []

        def wcols(w, c0, n=512, k0=0, k=8, ahead=False):
            key = (w.tensor.name, w.offset, c0, n, k0, k)
            if early and not ahead:
                assert early[0].key == key, (early[0].key, key)
                return early.pop(0)
            slot = Slot(key, w.rearrange("(k p) n -> p k n", p=128)[:, k0:k0 + k, c0:c0 + n], k, n)
            if ahead:
                early.append(slot)
            return slot

        queues = [pe, dve, act, pool, sp]

        def fork(flag, t_flag, limit, within, beyond, extra):
            base = [(q.n, dict(q.met)) for q in queues]
            state = (list(bank.free), list(slots.free), list(slot_n), list(early), list(extra.free))
            ends, bodies, left = [], [], []
            kept = [q.items for q in queues]
            for body in (within, beyond):
                bank.free, slots.free, slot_n[:], early[:], extra.free = (list(x) for x in state)
                for q, (n, met) in zip(queues, base):
                    q.n, q.met, q.items = n, dict(met), []
                body()
                ends.append([q.n for q in queues])
                bodies.append([q.items for q in queues])
                left.append(([k for k, _ in slots.free], list(slot_n), [(x.k, x.key) for x in early]))
            assert left[0] == left[1]
            for i, q in enumerate(queues):
                q.n = max(e[i] for e in ends)
                for e, items in zip(ends, bodies):
                    if e[i] < q.n:
                        items[i].append(([(q.sem, e[i])], None, "pad", q.n - e[i]))
                q.items, q.met = kept[i], dict(base[i][1])
                if bodies[0][i] or bodies[1][i]:
                    q.wait(t_flag)
                    q.items.append(([], (flag, bodies[0][i], bodies[1][i]), "fork", limit))
            end = [q.last() for q in (pe, dve, act)]
            bank.free = [(k, end) for k in range(8)]
            slots.free = [(k, end) for k, _ in slots.free]
            return end

        bank = Ring([p[:, :] for p in PS])

        def mms(out, pairs, *needs):
            pairs = list(pairs)

            def go(e):
                for i, (l, r) in enumerate(pairs):
                    m = e.matmul(out, l, r, start=i == 0, stop=i == len(pairs) - 1, skip_group_check=True)
                return m
            return pe(go, *needs)

        def tt(q, out, a, b, op, *needs):
            return q(lambda e: e.tensor_tensor(out, a, b, op), *needs)

        def ts(q, out, a, s1, s2, op0, op1, *needs):
            if op1 is None:
                return q(lambda e: e.tensor_scalar(out, a, s1, None, op0), *needs)
            return q(lambda e: e.tensor_scalar(out, a, s1, s2, op0, op1), *needs)

        def stt(out, a, s, b, op0, op1, *needs, acc=None):
            if acc is None:
                return dve(lambda e: e.scalar_tensor_tensor(out, a, s, b, op0, op1), *needs)
            return dve(lambda e: e.scalar_tensor_tensor(out, a, s, b, op0, op1, accum_out=acc), *needs)

        def af(out, a, func, *needs, **kw):
            return act(lambda e: e.activation(out, a, func, **kw), *needs)

        def inv_rms(out, ss_ps, ss_tok, n, eps, free):
            a = ts(dve, out, ss_ps, 1.0 / n, eps, ALU.mult, ALU.add, ss_tok, free)
            b = af(out, out, ACT.Sqrt, a)
            c = dve(lambda e: e.reciprocal(out, out), b)
            return c, a

        def norm_full(src, src_tok, rs, sqb, free):
            s = af(sqb[:, :, :], src, ACT.Square, src_tok, free)
            b, ps, fr = bank.take()
            m = mms(ps[:, 0:T], [(C("ones"), sqb[:, k, :]) for k in range(KT)], s, ld, fr)
            t, used = inv_rms(rs, ps[:, 0:T], m, D, EPS, free)
            bank.give(b, used)
            return t

        hx = alloc3(KT, T)
        hc = ctxT
        sq = alloc3(KT, T)
        mod = sb("mod", [128, 96])
        sc2 = tiny(16)
        t_silu = af(sc2, P("c2", 0, 16), ACT.Silu, ld)
        c2 = sc2.rearrange("p (k t) -> p k t", t=2)
        mod_tok = []

        def ada():
            for s in range(12):
                w = wcols(A["w_ada"][0], 512 * s)
                b, ps, fr = bank.take()
                for j in range(4):
                    m = mms(ps[:, 2 * j:2 * j + 2], [(w.ap[:, k, 128 * j:128 * j + 128], c2[:, k, :]) for k in range(KT)],
                            w.tok, t_silu, fr)
                w.done(m)
                t = tt(dve, mod[:, 8 * s:8 * s + 8], ps[:, 0:8], P("b_ada", 8 * s, 8), ALU.add, m, ld)
                bank.give(b, t)
                mod_tok.append(t)

        ada()

        def M(part, k, who=0):
            j = 2 * (8 * part + k) + who
            return mod[:, j:j + 1]

        ga1 = tiny(16)
        gm1 = tiny(8)
        m3 = mod[:, :].rearrange("p (c k t) -> p c k t", c=6, t=2)
        for who in range(2):
            g = ga1.rearrange("p (t k) -> p t k", t=2)[:, who, :]
            t_g = stt(g, m3[:, 1, :, who], 1.0, P("norm_attn", 0, 8), ALU.add, ALU.mult, mod_tok[-1], ld)

        def modulated(src, dst, rs, t_rs, gcol, shcol, t_g, scr):
            for k in range(KT):
                n, buf, fr = scr.take()
                a = stt(buf[:, 0:T], src[:, k, :], gcol(k), rs, ALU.mult, ALU.mult, t_rs, t_g, fr)
                b = af(dst[:, k, :], buf[:, 0:T], ACT.Identity, a, bias=shcol(k))
                scr.give(n, b)
            return b

        scrA = [alloc(512) for _ in range(6)]
        scr = Ring(scrA)
        rsx = alloc(T)
        rsc = alloc(T)
        t_rsx = norm_full(xT[:, :, :], ld, rsx, sq, None)
        t_rsc = norm_full(ctxT[:, :, :], ld, rsc, sq, pe.last())
        t_hx = modulated(xT, hx, rsx, t_rsx, lambda k: ga1[:, k:k + 1], lambda k: M(0, k, 0), t_g, scr)
        t_hc = modulated(ctxT, hc, rsc, t_rsc, lambda k: ga1[:, 8 + k:9 + k], lambda k: M(0, k, 1), t_g, scr)

        lam = tiny(1)
        nlam = tiny(1)
        lamt = tiny(4)
        b, ps, fr = bank.take()
        t = tt(dve, lamt[0:64, 0:2], P("lam", 0, 2, 64), P("lam", 2, 2, 64), ALU.mult, ld)
        t = mms(ps[:, 0:2], [(C("ones")[0:64, :], lamt[0:64, 0:2])], t, ld, fr)
        t = af(lamt[:, 2:4], ps[:, 0:2], ACT.Exp, t)
        bank.give(b, t)
        t = tt(dve, lam, lamt[:, 3:4], lamt[:, 2:3], ALU.subtract, t)
        t_lam = ts(dve, nlam, lam, -LAM_INIT, None, ALU.add, None, t)

        def head_norm(ps, tok, b, n, gcol, blk, div, dst, rot=None, needs=None):
            ks, s, fs = scr.take()
            kq, q, fq = scr.take()
            t1 = af(s[:, 0:n], ps[:, 0:n], ACT.Square, tok, fs)
            b2, ps2, fr2 = bank.take()
            m = mms(ps2[:, 0:n], [(blk, s[:, 0:n])], t1, fr2)
            yield
            t2, used = inv_rms(s[:, n:2 * n] if n <= 256 else s[:, 0:n], ps2[:, 0:n], m, div, EPS, None)
            rs = s[:, n:2 * n] if n <= 256 else s[:, 0:n]
            bank.give(b2, used)
            if rot is None:
                t3 = stt(dst, ps[:, 0:n], gcol, rs, ALU.mult, ALU.mult, t2, needs)
                bank.give(b, t3)
                scr.give(ks, t3)
                scr.give(kq)
                yield t3
                return
            R, cs, sn, t_rot = rot
            t3 = stt(q[:, 0:n], ps[:, 0:n], gcol, rs, ALU.mult, ALU.mult, t2, fq)
            bank.give(b, t3)
            yield
            b3, ps3, fr3 = bank.take()
            m = mms(ps3[:, 0:n], [(R, q[:, 0:n])], t3, fr3)
            t4 = tt(dve, q[:, n:2 * n], q[:, 0:n], cs, ALU.mult, t3, t_rot)
            t5 = tt(dve, s[:, 0:n], ps3[:, 0:n], sn, ALU.mult, m, t_rot)
            bank.give(b3, t5)
            t6 = tt(dve, dst, q[:, n:2 * n], s[:, 0:n], ALU.add, t4, t5, needs)
            scr.give(ks, t6)
            scr.give(kq, t6, m)
            yield t6

        qa = alloc3(4, T)
        qb = alloc3(4, T)
        kA = alloc(512)
        kS = alloc(512)
        kb = alloc3(4, 512)
        va = alloc3(4, 128)
        vb = alloc3(4, 512)
        rot1 = (C("r1"), C("cos1", 256), C("sin1", 256), ld)
        T_ = {}

        def run(gen, key):
            for t in gen:
                if t is not None:
                    T_[key] = t
                yield

        def qk_chunk(w, col, rhs, t_rhs, gcol, dst, rot, key, last=False):
            b, ps, fr = bank.take()
            m = mms(ps[:, 0:T], [(w.ap[:, k, col:col + 128], rhs[:, k, :]) for k in range(KT)], w.tok, t_rhs, fr)
            if last:
                w.done(m)
            yield
            yield from run(head_norm(ps, m, b, T, gcol, C("blk"), 64, dst, rot), key)

        W_in = A["w_in"][0]
        w0 = wcols(W_in, 0)
        w1 = wcols(W_in, 512)

        def v_tok(w, c0, n, rhs_tiles, dst, key, done=None):
            for j, (h, tk, q) in enumerate(rhs_tiles):
                b, ps, fr = bank.take()
                m = mms(ps[:, 0:n], [(h[:, k, 128 * q:128 * q + 128], w.ap[:, k, c0:c0 + n]) for k in range(KT)], w.tok, tk, fr)
                T_[key, j] = af(dst(j), ps[:, 0:n], ACT.Copy, m)
                bank.give(b, T_[key, j])
            return m

        four = [(hx, t_hx, 0), (hx, t_hx, 1), (hc, t_hc, 0), (hc, t_hc, 1)]
        pipeline([qk_chunk(w0, 128 * c, hx, t_hx, P("qna"), qa[:, c, :], rot1, ("qa", c), c == 3) for c in range(4)], 2)
        pipeline([qk_chunk(w1, 0, hx, t_hx, P("kna"), kA[:, 0:T], rot1, ("ka", 0)),
                  qk_chunk(w1, 0, hc, t_hc, P("kna"), kA[:, T:2 * T], None, ("ka", 1)),
                  qk_chunk(w1, 256, hx, t_hx, P("qnb"), qb[:, 0, :], rot1, ("qb", 0)),
                  qk_chunk(w1, 384, hx, t_hx, P("qnb"), qb[:, 1, :], rot1, ("qb", 1))], 2)
        m = v_tok(w1, 128, 128, four, lambda j: va[:, j, :], "va")
        w1.done(m)
        b, ps, fr = bank.take()
        m = mms(ps, [(C("swp"), kA)], T_["ka", 0], T_["ka", 1], fr)
        T_["kS"] = af(kS, ps, ACT.Copy, m)
        bank.give(b, T_["kS"])
        w2 = wcols(W_in, 1024)
        w3 = wcols(W_in, 1536)
        w4 = wcols(W_in, 2048)
        gens = [qk_chunk(w2, 0, hx, t_hx, P("qnb"), qb[:, 2, :], rot1, ("qb", 2)),
                qk_chunk(w2, 128, hx, t_hx, P("qnb"), qb[:, 3, :], rot1, ("qb", 3))]
        for c in range(4):
            w, col = (w2, 256 + 128 * c) if c < 2 else (w3, 128 * (c - 2))
            gens.append(qk_chunk(w, col, hx, t_hx, P("knb"), kb[:, c, 0:T], rot1, ("kb", c, 0)))
            gens.append(qk_chunk(w, col, hc, t_hc, P("knb"), kb[:, c, T:2 * T], None, ("kb", c, 1), c == 1))
        pipeline(gens, 2)
        m = v_tok(w3, 256, 256, four, lambda j: vb[:, j, 0:256], "vb0")
        w3.done(m)
        m = v_tok(w4, 0, 256, four, lambda j: vb[:, j, 256:512], "vb1")
        m_w4 = m

        yaT = alloc3(4, T)
        ybT = alloc3(4, T)
        PT = Ring([alloc3(4, T), sq[:, 0:4, :]])

        smcol = sb("smcol", [128, 256])
        smn = [0]

        def smc():
            smn[0] = (smn[0] + 1) % 64
            return smcol[:, 4 * smn[0]:4 * smn[0] + 4]

        def softmax(qap, kap, n, scale, tq, mask=None):
            b, ps, fr = bank.take()
            m = mms(ps[:, 0:n], [(qap, kap)], tq, fr)
            yield
            st = smc()
            src = ps[:, 0:n]
            kp, p, fp = scr.take()
            if mask is not None:
                m = tt(dve, p[:, 0:n], ps[:, 0:n], mask, ALU.add, m, fp)
                bank.give(b, m)
                src = p[:, 0:n]
            t = dve(lambda e: e.tensor_reduce(st[:, 0:1], src, AX, ALU.max), m)
            t = ts(dve, st[:, 1:2], st[:, 0:1], -scale, None, ALU.mult, None, t)
            t = af(p[:, 0:n], src, ACT.Exp, t, fp, bias=st[:, 1:2], scale=scale, accum_out=st[:, 2:3])
            if mask is None:
                bank.give(b, t)
            yield
            t = dve(lambda e: e.reciprocal(st[:, 3:4], st[:, 2:3]), t)
            yield (kp, p, st, t)

        def turn(p, tp, n, pt, qt, ftok):
            b, ps, fr = bank.take()

            def go(e):
                for j in range(n // 128):
                    mm = e.transpose(ps[:, 128 * j:128 * j + 128], p[:, 128 * j:128 * j + 128], C("ident"))
                return mm
            m = pe(go, tp, fr, ld)
            src = ps[:, 0:n].rearrange("p (j q) -> p j q", q=128)
            t = af(pt[:, 0:n // 128, 128 * qt:128 * qt + 128], src, ACT.Copy, m, ftok)
            bank.give(b, t)
            return m, t

        def last_of(gen):
            r = None
            for r in gen:
                if r is None:
                    yield
            return r

        def head_a(h):
            g, half = h // 4, 64 * (h % 2)
            K, tk = (kA, [T_["ka", 0], T_["ka", 1]]) if g == h % 2 else (kS, T_["kS"])
            kpt, pt, fpt = PT.take()
            ev = []
            for qt in range(2):
                kp, p, st, t = yield from last_of(softmax(
                    qa[half:half + 64, h // 2, 128 * qt:128 * qt + 128], K[half:half + 64, :], 512, 0.125,
                    [tk, T_["qa", h // 2]]))
                t = ts(dve, p, p, st[:, 3:4], None, ALU.mult, None, t)
                yield
                m, e = turn(p, t, 512, pt, qt, fpt)
                scr.give(kp, m)
                ev.append(e)
            yield
            b, ps, fr = bank.take()
            m = mms(ps[half:half + 64, 0:T], [(va[:, j, 64 * g:64 * g + 64], pt[:, j, :]) for j in range(4)],
                    ev, [T_["va", j] for j in range(4)], fr)
            PT.give(kpt, m)
            T_["ya", h] = af(yaT[half:half + 64, h // 2, :], ps[half:half + 64, 0:T], ACT.Copy, m)
            bank.give(b, T_["ya", h])
            yield

        pipeline([head_a(h) for h in range(8)], 2)

        def head_b(h):
            kpt, pt, fpt = PT.take()
            ev = []
            for qt in range(2):
                r = []
                for mm in range(2):
                    half = 64 * mm
                    r.append((yield from last_of(softmax(
                        qb[half:half + 64, h, 128 * qt:128 * qt + 128], kb[half:half + 64, h, :], 512, 0.125,
                        [T_["qb", h], T_["kb", h, 0], T_["kb", h, 1]]))))
                (k0, p0, s0, t0), (k1, p1, s1, t1) = r
                t = tt(dve, s1[:, 3:4], s1[:, 3:4], nlam, ALU.mult, t1, t_lam)
                t = ts(dve, p1, p1, s1[:, 3:4], None, ALU.mult, None, t)
                t = stt(p0, p0, s0[:, 3:4], p1, ALU.mult, ALU.add, t, t0)
                scr.give(k1, t)
                yield
                m, e = turn(p0, t, 512, pt, qt, fpt)
                scr.give(k0, m)
                ev.append(e)
            yield
            b, ps, fr = bank.take()
            m = mms(ps[:, 0:T], [(vb[:, j, 128 * h:128 * h + 128], pt[:, j, :]) for j in range(4)],
                    ev, [T_["vb0", j] for j in range(4)], [T_["vb1", j] for j in range(4)], fr)
            PT.give(kpt, m)
            ks, s, fs = scr.take()
            t = af(s[:, 0:T], ps[:, 0:T], ACT.Square, m, fs)
            b2, ps2, fr2 = bank.take()
            m = mms(ps2[:, 0:T], [(C("ones"), s[:, 0:T])], t, fr2)
            yield
            t, used = inv_rms(s[:, T:2 * T], ps2[:, 0:T], m, 128, 1e-5, None)
            bank.give(b2, used)
            t = stt(s[:, 0:T], ps[:, 0:T], P("subln"), s[:, T:2 * T], ALU.mult, ALU.mult, t)
            bank.give(b, t)
            T_["yb", h] = ts(dve, ybT[:, h, :], s[:, 0:T], 1.0 - LAM_INIT, None, ALU.mult, None, t)
            scr.give(ks, T_["yb", h])
            yield

        pipeline([head_b(h) for h in range(4)], 2)

        att = [pe.last(), dve.last(), act.last()]
        sga = ctxT
        sgb = kb.rearrange("p k n -> p (k n)").rearrange("p (k n) -> p k n", k=8)
        w5 = wcols(W_in, 2560)
        w6 = wcols(W_in, 3072)
        w7 = wcols(W_in, 3584)
        w8 = wcols(W_in, 4096, 256)
        gcols = [(w4, 256), (w4, 384)] + [(w, 128 * j) for w in (w5, w6, w7) for j in range(4)] + [(w8, 0), (w8, 128)]
        for i, (w, col) in enumerate(gcols):
            b, ps, fr = bank.take()
            m = mms(ps[:, 0:T], [(w.ap[:, k, col:col + 128], hx[:, k, :]) for k in range(KT)], w.tok, fr, m_w4)
            if i in (1, 5, 9, 13, 15):
                w.done(m)
            dst = (sga if i < 8 else sgb)[:, i % 8, :]
            t = af(dst, ps[:, 0:T], ACT.Sigmoid, m, att)
            bank.give(b, t)
            T_["g", i] = t
        mg = sq
        for half in range(2):
            wa = wcols(A["w_oa"][0], 512 * half, 512, 0, 4)
            wb = wcols(A["w_ob"][0], 512 * half, 512, 0, 4)
            for j in range(4):
                c = 4 * half + j
                b, ps, fr = bank.take()
                m1 = mms(ps[:, 0:T], [(wa.ap[:, k, 128 * j:128 * j + 128], yaT[:, k, :]) for k in range(4)],
                         wa.tok, [T_["ya", h] for h in range(8)], fr)
                m2 = mms(ps[:, T:2 * T], [(wb.ap[:, k, 128 * j:128 * j + 128], ybT[:, k, :]) for k in range(4)],
                         wb.tok, [T_["yb", h] for h in range(4)])
                t1 = tt(dve, mg[:, c, :], ps[:, 0:T], sga[:, c, :], ALU.mult, m2, T_["g", c])
                kt_, u, fu = scr.take()
                t2 = tt(dve, u[:, 0:T], ps[:, T:2 * T], sgb[:, c, :], ALU.mult, m2, T_["g", 8 + c], fu)
                bank.give(b, t2)
                t3 = tt(dve, mg[:, c, :], mg[:, c, :], u[:, 0:T], ALU.add, t1, t2)
                scr.give(kt_, t3)
            wa.done(m1)
            wb.done(m2)

        def project_out(w_, K, src, t_src, gate, split=8):
            for half in range(2):
                ws = [wcols(w_, 512 * half, 512, k0, min(8, K - k0)) for k0 in range(0, K, 8)]
                for j in range(4):
                    c = 4 * half + j
                    b, ps, fr = bank.take()
                    prs = [(ws[k // 8].ap[:, k % 8, 128 * j:128 * j + 128], src[:, k, :]) for k in range(K)]
                    m = mms(ps[:, 0:T], prs, [w.tok for w in ws], t_src, fr)
                    if gate is None:
                        t = tt(dve, xT[:, c, :], ps[:, 0:T], xT[:, c, :], ALU.add, m)
                    else:
                        t = stt(xT[:, c, :], ps[:, 0:T], gate(c), xT[:, c, :], ALU.mult, ALU.add, m)
                    bank.give(b, t)
                for w in ws:
                    w.done(m)
            return t

        t_x = project_out(A["w_out"][0], KT, mg, t3, lambda c: M(2, c))

        def moe(t_x, following):
            phase()
            h2 = alloc3(KT, T)
            sq = alloc3(KT, T)
            scr = Ring([alloc(512) for _ in range(4)])
            rs = alloc(T)
            wT = alloc(T, NE)
            gm1 = tiny(8)
            t_g = stt(gm1, m3[:, 4, :, 0], 1.0, P("norm_mlp", 0, 8), ALU.add, ALU.mult)
            t_rs = norm_full(xT[:, :, :], t_x, rs, sq, None)
            t_h = modulated(xT, h2, rs, t_rs, lambda k: gm1[:, k:k + 1], lambda k: M(3, k), t_g, scr)
            tw, tm, Gs = [], [], []
            mT = alloc(T, NE)
            for q in range(2):
                b, ps, fr = bank.take()
                m = mms(ps[:, 0:NE], [(h2[:, k, 128 * q:128 * q + 128], rw[:, k, :]) for k in range(KT)], t_h, fr)
                L, E_, G, Q, R_ = (tiny(NE) for _ in range(5))
                m8, s = tiny(8), tiny(4)
                t = tt(dve, L, ps[:, 0:NE], rb[:, :], ALU.add, m)
                bank.give(b, t)
                t = dve(lambda e, m8=m8, L=L: e.max(m8, L), t)
                t0 = ts(dve, s[:, 0:1], m8[:, 0:1], -1.0, None, ALU.mult, None, t)
                te = af(E_, L, ACT.Exp, t0, bias=s[:, 0:1])
                t1 = dve(lambda e, G=G, L=L, m8=m8, s=s: e.tensor_scalar(
                    G, L, m8[:, 3:4], 0.0, ALU.is_gt, ALU.add, accum_out=s[:, 1:2]), t)
                t2 = ts(dve, Q, L, m8[:, 3:4], None, ALU.is_equal, None, t)
                t3 = dve(lambda e, R_=R_, Q=Q: e.tensor_tensor_scan(R_, Q, Q, 0.0, ALU.add, ALU.bypass), t2)
                t4 = ts(dve, R_, R_, s[:, 1:2], 4.0, ALU.add, ALU.is_le, t3, t1)
                t5 = tt(dve, Q, Q, R_, ALU.mult, t4)
                t6 = tt(dve, G, G, Q, ALU.add, t5)
                Wt = E_
                t7 = stt(Wt, G, 1.0, E_, ALU.mult, ALU.mult, t6, te, acc=s[:, 2:3])
                t8 = dve(lambda e, s=s: e.reciprocal(s[:, 3:4], s[:, 2:3]), t7)
                t9 = ts(dve, Wt, Wt, s[:, 3:4], None, ALU.mult, None, t8)
                b, ps, fr = bank.take()
                m = pe(lambda e, ps=ps, G=G: e.transpose(ps[0:NE, 0:128], G, C("ident")), t6, fr)
                m = pe(lambda e, ps=ps, Wt=Wt: e.transpose(ps[0:NE, 128:256], Wt, C("ident")), t9)
                ta = af(mT[:, 128 * q:128 * q + 128], ps[0:NE, 0:128], ACT.Copy, m)
                tb = af(wT[:, 128 * q:128 * q + 128], ps[0:NE, 128:256], ACT.Copy, m)
                bank.give(b, tb)
                tm.append(ta)
                tw.append(tb)
                Gs.append((Wt, t9))
            cnt, posT = alloc(T, NE), alloc(T, NE)
            most = alloc(NE, 1)
            flag = alloc(4, 1).bitcast(I32)[:, 0:1]
            posK = tiny(64).rearrange("p (q e) -> p q e", q=2)
            t_cnt = dve(lambda e: e.tensor_tensor_scan(cnt, mT, mT, 0.0, ALU.add, ALU.bypass), tm)
            t = tt(dve, posT, cnt, mT, ALU.mult, t_cnt)
            t = ts(dve, posT, posT, -1.0, None, ALU.add, None, t)
            b, ps, fr = bank.take()
            for q in range(2):
                m = pe(lambda e, ps=ps, q=q: e.transpose(ps[:, NE * q:NE * q + NE], posT[:, 128 * q:128 * q + 128],
                                                         C("ident", NE, NE)), t, fr)
            m2 = pe(lambda e, ps=ps: e.transpose(ps[0:1, 128:128 + NE], cnt[:, T - 1:T], C("ident", NE, NE)), t_cnt)
            t_pos = af(posK, ps[:, 0:64].rearrange("p (q e) -> p q e", q=2), ACT.Copy, m, m2)
            t = dve(lambda e, ps=ps: e.tensor_reduce(most[:, 0:1], ps[0:1, 128:128 + NE], AX, ALU.max), m2, t_pos)
            bank.give(b, t, t_pos)
            t_flag = dve(lambda e: e.tensor_copy(flag, most[:, 0:1]), t)
            Wg, Wu, Wd = A["w_gate"][0], A["w_up"][0], A["w_down"][0]
            for ahead in (True,):
                for half in range(2):
                    for W in (Wg, Wu):
                        wcols(W[0], 512 * half, ahead=True)
                for half in range(2):
                    wcols(Wd[0], 512 * half, ahead=True)
            assert len(bank.free) == 8
            before = [r for _, r in bank.free]
            Y = [PS[4 + c // 2][:, T * (c % 2):T * (c % 2) + T] for c in range(8)]
            for c in range(8):
                mY = pe(lambda e, c=c: e.matmul(Y[c], bdn[:, 128 * c:128 * c + 128], wT, start=c % 2 == 0, stop=False,
                                                skip_group_check=True), before, tw)
            free4 = [(k, r) for k, r in bank.free if k < 4]
            bank.free = free4
            htok = sq.rearrange("p k n -> p (k n)").rearrange("p (q n) -> p q n", q=2)
            for q in range(2):
                for g in range(2):
                    b, ps, fr = bank.take()

                    def go(e, ps=ps, q=q, g=g):
                        for j in range(4):
                            m = e.transpose(ps[:, 128 * j:128 * j + 128],
                                            h2[:, 4 * g + j, 128 * q:128 * q + 128], C("ident"))
                        return m
                    m = pe(go, t_h, fr)
                    t_tok = af(htok[:, q, 512 * g:512 * g + 512], ps, ACT.Copy, m)
                    bank.give(b, t_tok)
            mark = at[0]

            def finish(m):
                for c in range(8):
                    stt(xT[:, c, :], Y[c], M(5, c), xT[:, c, :], ALU.mult, ALU.add, m)
                for args in following:
                    wcols(*args, ahead=True)

            def swiglu(out, ps, gsl, usl, ex, f, m, s, fs, scale_by, free):
                n = gsl.stop - gsl.start
                g, u = s[:, 0:n], s[:, T:T + n]
                t1 = ts(dve, g, ps[:, gsl], P("b_gate", 8 * ex + f), 7.0, ALU.add, ALU.min, m, fs)
                t2 = ts(dve, u, ps[:, usl], P("b_up", 8 * ex + f), 7.0, ALU.add, ALU.min, m, fs)
                t3 = af(out, g, ACT.Sigmoid, t1, free, scale=1.702)
                t4 = ts(dve, u, u, -7.0, 1.0, ALU.max, ALU.add, t2)
                if scale_by is not None:
                    t4 = tt(dve, u, u, scale_by[0], ALU.mult, t4, scale_by[1])
                t5 = tt(dve, g, g, u, ALU.mult, t4, t3)
                return tt(dve, out, out, g, ALU.mult, t5), t2

            def routed():
                at[0] = mark
                xgs = Ring([alloc3(KT, CAP) for _ in range(2)])
                acts = Ring([alloc3(KT, CAP) for _ in range(2)])
                ygs = Ring([alloc(D, CAP) for _ in range(2)])
                PwTs = Ring([alloc(T, CAP) for _ in range(2)])
                Ss = Ring([alloc(4 * CAP).rearrange("p (a q s) -> p a q s", a=2, q=2) for _ in range(2)])
                yts = Ring([alloc(CAP) for _ in range(4)])

                def gather(ex):
                    kS_, S, fS = Ss.take()
                    kx, xg, fx = xgs.take()
                    kp, PwT, fp = PwTs.take()
                    for q in range(2):
                        t1 = ts(dve, S[:, 0, q, :], C("iota", CAP), posK[:, q, ex:ex + 1], None, ALU.is_equal, None,
                                t_pos, fS)
                        t2 = ts(dve, S[:, 1, q, :], C("iota", CAP), posK[:, q, ex:ex + 1], Gs[q][0][:, ex:ex + 1],
                                ALU.is_equal, ALU.mult, t_pos, fS)
                    for g in range(2):
                        b, ps, fr = bank.take()

                        def go(e, ps=ps, g=g):
                            for j in range(4):
                                for q in range(2):
                                    c = 512 * g + 128 * j
                                    m = e.matmul(ps[:, CAP * j:CAP * j + CAP], htok[:, q, c:c + 128], S[:, 0, q, :],
                                                 start=q == 0, stop=q == 1, skip_group_check=True)
                            return m
                        m = pe(go, t1, t_tok, fr)
                        t = af(xg[:, 4 * g:4 * g + 4, :], ps[:, 0:4 * CAP].rearrange("p (j s) -> p j s", j=4),
                               ACT.Copy, m, fx)
                        bank.give(b, t)
                    b, ps, fr = bank.take()

                    def go(e, ps=ps):
                        for q in range(2):
                            m = e.transpose(ps[0:CAP, 128 * q:128 * q + 128], S[:, 1, q, :], C("ident"))
                        return m
                    m = pe(go, t2, fr)
                    tp = af(PwT, ps[0:CAP, 0:T], ACT.Copy, m, fp)
                    bank.give(b, tp)
                    Ss.give(kS_, m)
                    return kx, xg, t, kp, PwT, tp

                nxt = gather(0)
                owed = None
                for ex in range(NE):
                    kx, xg, t_xg, kp, PwT, t_pw = nxt
                    ka, ac, fa = acts.take()
                    toks = []
                    for half in range(2):
                        wg = wcols(Wg[ex], 512 * half)
                        wu = wcols(Wu[ex], 512 * half)
                        for j in range(4):
                            f = 4 * half + j
                            b, ps, fr = bank.take()
                            m1 = mms(ps[:, 0:CAP], [(wg.ap[:, k, 128 * j:128 * j + 128], xg[:, k, :]) for k in range(KT)],
                                     wg.tok, t_xg, fr)
                            m2 = mms(ps[:, CAP:2 * CAP],
                                     [(wu.ap[:, k, 128 * j:128 * j + 128], xg[:, k, :]) for k in range(KT)], wu.tok)
                            ks, s, fs = scr.take()
                            t, used = swiglu(ac[:, f, :], ps, slice(0, CAP), slice(CAP, 2 * CAP), ex, f, m2, s, fs, None, fa)
                            bank.give(b, used)
                            scr.give(ks, t)
                            toks.append(t)
                            if f == 1 and owed is not None:
                                owed()
                                owed = None
                        wg.done(m1)
                        wu.done(m2)
                    xgs.give(kx, m2)
                    if ex + 1 < NE:
                        nxt = gather(ex + 1)
                    ky, yg, fy = ygs.take()
                    t_yg = []
                    turned = []

                    def turn_back(j, yt, kyt, t, b2, ps2, fr2, yg=yg, fy=fy, t_yg=t_yg):
                        m = pe(lambda e: e.transpose(ps2[0:CAP, 128 * (j % 4):128 * (j % 4) + 128], yt, C("ident")), t, fr2)
                        yts.give(kyt, m)
                        if j % 4 == 3:
                            c0 = 512 * (j // 4)
                            t = dve(lambda e: e.tensor_copy(yg[:, c0:c0 + 512], ps2[0:CAP, :]), m, fy)
                            bank.give(b2, t)
                            t_yg.append(t)

                    for half in range(2):
                        wd = wcols(Wd[ex], 512 * half)
                        b2, ps2, fr2 = bank.take()
                        for j in range(4):
                            c = 4 * half + j
                            b, ps, fr = bank.take()
                            m = mms(ps[:, 0:CAP], [(wd.ap[:, k, 128 * j:128 * j + 128], ac[:, k, :]) for k in range(KT)],
                                    wd.tok, toks, fr)
                            kyt, yt, fyt = yts.take()
                            t = af(yt, ps[:, 0:CAP], ACT.Copy, m, fyt)
                            bank.give(b, t)
                            if turned:
                                turn_back(*turned.pop())
                            turned.append((c, yt, kyt, t, b2, ps2, fr2))
                            if c == 7:
                                turn_back(*turned.pop())
                        wd.done(m)
                    acts.give(ka, m)

                    def put_back(ex=ex, yg=yg, ky=ky, PwT=PwT, kp=kp, t_yg=t_yg, t_pw=t_pw):
                        def go(e):
                            for c in range(8):
                                m = e.matmul(Y[c], yg[:, 128 * c:128 * c + 128], PwT, start=False, stop=ex == NE - 1,
                                             skip_group_check=True)
                            return m
                        m = pe(go, t_yg, t_pw)
                        ygs.give(ky, m)
                        PwTs.give(kp, m)
                        return m
                    owed = put_back
                finish(owed())

            def dense():
                at[0] = mark
                acts = Ring([alloc3(KT, T)])
                wb = Ring([alloc(T), alloc(T)])
                for ex in range(NE):
                    ka, ac, fa = acts.take()
                    b, bt, fb = bank.take()
                    m = mms(bt[:, 0:T], [(C("ident")[0:NE, ex:ex + 1].to_broadcast([NE, 128]), wT)], tw, fb)
                    kw, wbt, fw = wb.take()
                    t_wb = af(wbt, bt[:, 0:T], ACT.Copy, m, fw)
                    bank.give(b, t_wb)
                    toks = []
                    for half in range(2):
                        wg = wcols(Wg[ex], 512 * half)
                        wu = wcols(Wu[ex], 512 * half)
                        for j in range(4):
                            f = 4 * half + j
                            b, ps, fr = bank.take()
                            m1 = mms(ps[:, 0:T], [(wg.ap[:, k, 128 * j:128 * j + 128], h2[:, k, :]) for k in range(KT)],
                                     wg.tok, fr)
                            m2 = mms(ps[:, T:2 * T], [(wu.ap[:, k, 128 * j:128 * j + 128], h2[:, k, :]) for k in range(KT)],
                                     wu.tok)
                            ks, s, fs = scr.take()
                            t, used = swiglu(ac[:, f, :], ps, slice(0, T), slice(T, 2 * T), ex, f, m2, s, fs,
                                             (wbt, t_wb), fa)
                            bank.give(b, used)
                            scr.give(ks, t)
                            toks.append(t)
                        wg.done(m1)
                        wu.done(m2)
                    wb.give(kw, t)
                    for half in range(2):
                        wd = wcols(Wd[ex], 512 * half)

                        def go(e, wd=wd, half=half, ac=ac, last=ex == NE - 1):
                            for j in range(4):
                                for k in range(KT):
                                    m = e.matmul(Y[4 * half + j], wd.ap[:, k, 128 * j:128 * j + 128], ac[:, k, :],
                                                 start=False, stop=last and k == KT - 1, skip_group_check=True)
                            return m
                        m = pe(go, wd.tok, toks, mY)
                        wd.done(m)
                    acts.give(ka, m)
                finish(m)

            return fork(flag, t_flag, LIMIT, routed, dense, scr)

        if stage >= 2:
            Wa = A["a_w_in"][0]
            t_x = moe(t_x, [(Wa, 512 * i) for i in range(6)] if stage >= 3 else [])

        def normed(t_x, gname, layer):
            u = alloc3(KT, T)
            sq = alloc3(KT, T)
            rs = alloc(T)
            t_rs = norm_full(xT[:, :, :], t_x, rs, sq, None)
            for k in range(KT):
                t = stt(u[:, k, :], xT[:, k, :], P(gname, 8 * layer + k), rs, ALU.mult, ALU.mult, t_rs)
            return u, t, sq

        def ffn(t_x, layer):
            phase()
            u, t_u, sq = normed(t_x, "norm_ffn", layer)
            g = alloc3(FK, T)
            W = A["ffn_w_in"][layer]
            for s in range(11):
                w = wcols(W, 512 * s)
                for j in range(4):
                    c = 4 * s + j
                    b, ps, fr = bank.take()
                    m = mms(ps[:, 0:T], [(w.ap[:, k, 128 * j:128 * j + 128], u[:, k, :]) for k in range(KT)],
                            w.tok, t_u, fr)
                    if c < FK:
                        t = af(g[:, c, :], ps[:, 0:T], ACT.Silu, m)
                        T_["f", c] = t
                    else:
                        t = tt(dve, g[:, c - FK, :], ps[:, 0:T], g[:, c - FK, :], ALU.mult, m, T_["f", c - FK])
                    bank.give(b, t)
                w.done(m)
            return project_out(A["ffn_w_out"][layer], FK, g, t, None)

        def mlstm(t_x):
            nonlocal scr
            phase()
            u, t_u, sq = normed(t_x, "norm_mix", 0)
            scr = Ring([alloc(512) for _ in range(4)])
            qT = alloc3(4, T)
            kT = alloc3(4, T)
            v = alloc3(2, 1024)
            so = alloc3(8, T)
            y = sq
            qkT = Ring([alloc3(2, T), alloc3(2, T)])
            W = A["a_w_in"][0]
            ig, fg, tmp, F_, a_ = (alloc(T, 4) for _ in range(5))
            b, ps, fr = bank.take()
            m = mms(ps[0:4, 0:T], [(wgt[:, k, 0:4], u[:, k, :]) for k in range(KT)], t_u, fr)
            m = mms(ps[0:4, T:2 * T], [(wgt[:, k, 4:8], u[:, k, :]) for k in range(KT)])
            ti = ts(dve, ig, ps[0:4, 0:T], P("bi", p=4), None, ALU.add, None, m)
            t = ts(dve, fg, ps[0:4, T:2 * T], P("bf", p=4), None, ALU.add, None, m)
            bank.give(b, ti, t)
            t1 = af(tmp, fg, ACT.Abs, t)
            t1 = af(tmp, tmp, ACT.Exp, t1, scale=-1.0)
            t1 = ts(dve, tmp, tmp, 1.0, None, ALU.add, None, t1)
            t1 = af(tmp, tmp, ACT.Ln, t1)
            t = stt(fg, fg, 0.0, tmp, ALU.min, ALU.subtract, t1, t)
            t = dve(lambda e: e.tensor_tensor_scan(F_, fg, fg, 0.0, ALU.add, ALU.bypass), t)
            t_a = tt(dve, a_, ig, F_, ALU.subtract, t, ti)
            Fc = tiny(8)
            b, ps, fr = bank.take()
            for q in range(2):
                m = mms(ps[:, 4 * q:4 * q + 4], [(F_[:, 128 * q:128 * q + 128], C("ident", 4, 4))], t, fr)
            t_F = dve(lambda e, ps=ps: e.tensor_copy(Fc, ps[:, 0:8]), m)
            bank.give(b, t_F)
            tq = {}
            for which, dst in ((0, qT), (1, kT)):
                w = wcols(W, 512 * which)
                for j in range(4):
                    b, ps, fr = bank.take()
                    m = mms(ps[:, 0:T], [(w.ap[:, k, 128 * j:128 * j + 128], u[:, k, :]) for k in range(KT)],
                            w.tok, fr)
                    t = af(dst[:, j, :], ps[:, 0:T], ACT.Copy, m)
                    bank.give(b, t)
                    tq[which, j] = t
                w.done(m)
            tv = []
            for half in range(2):
                w = wcols(W, 1024 + 512 * half)
                for q in range(2):
                    b, ps, fr = bank.take()
                    m = mms(ps, [(u[:, k, 128 * q:128 * q + 128], w.ap[:, k, :]) for k in range(KT)], w.tok, fr)
                    t = af(v[:, q, 512 * half:512 * half + 512], ps, ACT.Copy, m)
                    bank.give(b, t)
                    tv.append(t)
                w.done(m)
            for half in range(2):
                w = wcols(W, 2048 + 512 * half)
                for j in range(4):
                    b, ps, fr = bank.take()
                    m = mms(ps[:, 0:T], [(w.ap[:, k, 128 * j:128 * j + 128], u[:, k, :]) for k in range(KT)],
                            w.tok, fr)
                    t_o = af(so[:, 4 * half + j, :], ps[:, 0:T], ACT.Sigmoid, m)
                    bank.give(b, t_o)
                w.done(m)
            ty = []

            def head(h):
                kq, qk, fqk = qkT.take()
                b, aps, fr = bank.take()
                ma = mms(aps[:, 0:T], [(C("ident", p=4)[:, h:h + 1].to_broadcast([4, 128]), a_)], t_a, fr)
                mz = None
                if True:
                    mz = dve(lambda e: e.memset(qk[:, 1, 0:128], 0.0), fqk)
                ev = [mz]
                for q in range(2):
                    n = 128 * (q + 1)
                    b2, sp_, fr2 = bank.take()
                    ms = mms(sp_[:, 0:n], [(qT[:, h, 128 * q:128 * q + 128], kT[:, h, 0:n])], tq[0, h], tq[1, h], fr2)
                    ks, s, fs = scr.take()
                    st = smc()
                    am, w = s[:, 0:n], s[:, T:T + n]
                    t1 = tt(dve, am, aps[:, 0:n], C(f"mask{q}", n), ALU.add, ma, fs)
                    t2 = dve(lambda e, st=st, am=am: e.tensor_reduce(st[:, 0:1], am, AX, ALU.max), t1)
                    t3 = ts(dve, st[:, 1:2], st[:, 0:1], 0.0, -1.0, ALU.max, ALU.mult, t2)
                    t4 = af(w, am, ACT.Exp, t3, bias=st[:, 1:2])
                    yield
                    t5 = stt(am, sp_[:, 0:n], 128.0 ** -0.5, w, ALU.mult, ALU.mult, t4, ms, acc=st[:, 2:3])
                    bank.give(b2, t5)
                    t6 = tt(dve, st[:, 1:2], st[:, 1:2], Fc[:, 4 * q + h:4 * q + h + 1], ALU.subtract, t4, t_F)
                    t7 = af(st[:, 1:2], st[:, 1:2], ACT.Exp, t6)
                    t8 = af(st[:, 2:3], st[:, 2:3], ACT.Abs, t5)
                    t9 = tt(dve, st[:, 2:3], st[:, 2:3], st[:, 1:2], ALU.max, t7, t8)
                    t10 = dve(lambda e, st=st: e.reciprocal(st[:, 3:4], st[:, 2:3]), t9)
                    t11 = ts(dve, am, am, st[:, 3:4], None, ALU.mult, None, t10)
                    yield
                    mt, te = turn(am, t11, n, qk, q, fqk)
                    scr.give(ks, mt)
                    ev.append(te)
                bank.give(b, t1)
                yield
                b, ps, fr = bank.take()
                for c in range(2):
                    m = mms(ps[:, T * c:T * c + T],
                            [(v[:, j, 256 * h + 128 * c:256 * h + 128 * c + 128], qk[:, j, :]) for j in range(2)],
                            ev, tv, fr)
                qkT.give(kq, m)
                ks, s, fs = scr.take()
                t = af(s, ps, ACT.Square, m, fs)
                b2, ps2, fr2 = bank.take()
                m2 = mms(ps2[:, 0:T], [(C("ones"), s[:, 0:T]), (C("ones"), s[:, T:2 * T])], t, fr2)
                yield
                t, used = inv_rms(s[:, 0:T], ps2[:, 0:T], m2, 256, EPS, None)
                bank.give(b2, used)
                for c in range(2):
                    j = 2 * h + c
                    t1 = stt(y[:, j, :], ps[:, T * c:T * c + T], P("a_g_out", j), s[:, 0:T], ALU.mult, ALU.mult, t)
                    t2 = tt(dve, y[:, j, :], y[:, j, :], so[:, j, :], ALU.mult, t1, t_o)
                bank.give(b, t1)
                scr.give(ks, t1)
                ty.append(t2)
                yield

            pipeline([head(h) for h in range(4)], 2)
            return project_out(A["a_w_out"][0], KT, y, ty, None)

        def moba(t_x):
            nonlocal scr
            phase()
            u, t_u, sq = normed(t_x, "norm_mix", 1)
            scr = Ring([alloc(512) for _ in range(4)])
            qT = alloc3(8, T)
            kT = alloc3(8, T)
            v = alloc3(2, 1024)
            y = alloc3(8, T)
            cs, sn = alloc(T), alloc(T)
            PT = Ring([alloc3(2, T), alloc3(2, T)])
            ang, kk, r = alloc(T), alloc(T), alloc(T)
            t = dve(lambda e: e.tensor_copy(r, pos[:, :]), ld)
            t_ang = ts(dve, ang, r, C("inv", 1), None, ALU.mult, None, t)
            MAGIC = 12582912.0
            C1, C2 = 6.28125, 0.0019350051879882812
            C3 = 2.0 * math.pi - C1 - C2
            tr = None
            for dst, shift in ((sn, 0.0), (cs, 0.25)):
                t = ts(dve, kk, ang, 1.0 / (2.0 * math.pi), shift, ALU.mult, ALU.add, t_ang, tr)
                t = ts(dve, kk, kk, MAGIC, None, ALU.add, None, t)
                t = ts(dve, kk, kk, MAGIC, None, ALU.subtract, None, t)
                t = stt(r, kk, -C1, ang, ALU.mult, ALU.add, t)
                t = stt(r, kk, -C2, r, ALU.mult, ALU.add, t)
                t = stt(r, kk, -C3, r, ALU.mult, ALU.add, t)
                t = ts(dve, r, r, 2.0 * math.pi * shift, 3.1415925, ALU.add, ALU.min, t)
                t = ts(dve, r, r, -3.1415925, None, ALU.max, None, t)
                tr = af(dst, r, ACT.Sin, t)
            rot2 = (C("r2"), cs, sn, tr)
            W = A["b_w_in"][0]

            def chunk(w, col, gcol, dst, key, last):
                b, ps, fr = bank.take()
                m = mms(ps[:, 0:T], [(w.ap[:, k, col:col + 128], u[:, k, :]) for k in range(KT)], w.tok, t_u, fr)
                if last:
                    w.done(m)
                yield
                yield from run(head_norm(ps, m, b, T, gcol, C("ones"), 128, dst, rot2), key)

            ws = [wcols(W, 512 * s) for s in range(4)]
            pipeline([chunk(ws[s], 128 * j, P("gq") if s < 2 else P("gk"), (qT if s < 2 else kT)[:, 4 * (s % 2) + j, :],
                            ("m", s // 2, 4 * (s % 2) + j), j == 3) for s in range(4) for j in range(4)], 2)
            tv = []
            for half in range(2):
                w = wcols(W, 2048 + 512 * half)
                for q in range(2):
                    b, ps, fr = bank.take()
                    m = mms(ps, [(u[:, k, 128 * q:128 * q + 128], w.ap[:, k, :]) for k in range(KT)], w.tok, fr)
                    t = af(v[:, q, 512 * half:512 * half + 512], ps, ACT.Copy, m)
                    bank.give(b, t)
                    tv.append(t)
                w.done(m)
            ty = []

            def head(h):
                kq, pt, fqk = PT.take()
                ev = [dve(lambda e: e.memset(pt[:, 1, 0:128], 0.0), fqk)]
                for q in range(2):
                    n = 128 * (q + 1)
                    kp, p, st, t = yield from last_of(softmax(
                        qT[:, h, 128 * q:128 * q + 128], kT[:, h, 0:n], n, 128.0 ** -0.5,
                        [T_["m", 0, h], T_["m", 1, h]], mask=C(f"mask{q}", n)))
                    t = ts(dve, p[:, 0:n], p[:, 0:n], st[:, 3:4], None, ALU.mult, None, t)
                    yield
                    mt, te = turn(p, t, n, pt, q, fqk)
                    scr.give(kp, mt)
                    ev.append(te)
                yield
                b, ps, fr = bank.take()
                m = mms(ps[:, 0:T], [(v[:, j, 128 * h:128 * h + 128], pt[:, j, :]) for j in range(2)], ev, tv, fr)
                PT.give(kq, m)
                t = af(y[:, h, :], ps[:, 0:T], ACT.Copy, m)
                bank.give(b, t)
                ty.append(t)
                yield

            pipeline([head(h) for h in range(8)], 2)
            return project_out(A["b_w_out"][0], KT, y, ty, None)

        if stage >= 3:
            t_x = mlstm(t_x)
        if stage >= 4:
            t_x = ffn(t_x, 0)
        if stage >= 5:
            t_x = moba(t_x)
        if stage >= 6:
            t_x = ffn(t_x, 1)

        end = sp.dma(lambda e: e.dma_start(A["out"].rearrange("(k p) n -> p k n", p=128), xT[:, :, :]), s_out, 16, t_x)
        sp.wait(end)

        block = ctx.enter_context(nc.Block())
        block.sync(sp.replay)
        block.scalar(act.replay)
        block.vector(dve.replay)
        block.gpsimd(pool.replay)
        block.tensor(pe.replay)


STAGE = 99
_DIRECT = ["b_down", "router_w", "router_b", "w_ada", "w_in", "w_oa", "w_ob", "w_out", "w_gate", "w_up", "w_down"]
_SECOND = {"a_w_in": "a_w_in_2", "a_w_out": "a_w_out_2", "b_w_in": "b_w_in_2", "b_w_out": "b_w_out_2",
           "ffn_w_in": "ffn_w_in_2", "ffn_w_out": "ffn_w_out_2", "positions": "positions_2"}


def kernel(**inputs):
    import numpy as _np
    import concourse.bacc as _bacc
    from concourse import mybir as _mybir
    from concourse.bass_utils import run_bass_kernel_spmd as _run

    I = {k: _np.asarray(v) for k, v in inputs.items()}
    par = _np.zeros((128, NP), _np.float32)

    def put(name, a):
        par[0:a.shape[0], PCOL[name]:PCOL[name] + a.shape[1]] = a

    def cols(v):
        return _np.ascontiguousarray(v.reshape(-1, 128).T)

    def twice(v):
        return _np.concatenate([v, v])[:, None]

    put("norm_attn", cols(I["norm_attn"][0]))
    put("qna", twice(I["q_norm_a"][0]))
    put("kna", twice(I["k_norm_a"][0]))
    put("qnb", twice(I["q_norm_b"][0]))
    put("knb", twice(I["k_norm_b"][0]))
    put("subln", cols(I["subln_b"][0]))
    put("norm_mlp", cols(I["norm_mlp"][0]))
    put("c2", _np.stack([cols(I["c"][0]), cols(I["c_ctx"])], axis=2).reshape(128, 16))
    put("b_ada", _np.repeat(cols(I["b_ada"][0]), 2, axis=1))
    put("b_gate", cols(I["b_gate"][0].reshape(-1)))
    put("b_up", cols(I["b_up"][0].reshape(-1)))
    put("norm_mix", cols(I["norm_mix_2"].reshape(-1)))
    put("norm_ffn", cols(I["norm_ffn_2"].reshape(-1)))
    put("a_g_out", cols(I["a_g_out_2"].reshape(-1)))
    put("gq", cols(I["b_g_q_2"][0]))
    put("gk", cols(I["b_g_k_2"][0]))
    put("lam", _np.stack([I["lambda_q1"][0], I["lambda_q2"][0], I["lambda_k1"][0], I["lambda_k2"][0]], axis=1))
    put("bi", I["a_b_gates_2"][0][0:4, None])
    put("bf", I["a_b_gates_2"][0][4:8, None])
    arrays = {"con": shape_constants(), "par": par,
              "xT": _np.ascontiguousarray(I["x"][0].T), "ctxT": _np.ascontiguousarray(I["ctx"][0].T)}
    for n in _DIRECT:
        arrays[n] = _np.ascontiguousarray(I[n])
    for n, src in _SECOND.items():
        arrays[n] = _np.ascontiguousarray(I[src])
    nc = _bacc.Bacc("TRN2", target_bir_lowering=False, num_devices=1)
    A = {n: nc.dram_tensor(f"in_{n}", a.shape, _mybir.dt.from_np(a.dtype), kind="ExternalInput").ap()
         for n, a in arrays.items()}
    A["out"] = nc.dram_tensor("out_0", (D, T), F32, kind="ExternalOutput").ap()
    build(nc, A, STAGE)
    r = _run(nc, [{f"in_{n}": a for n, a in arrays.items()}], core_ids=[0])
    return _np.ascontiguousarray(_np.asarray(r.results[0]["out_0"]).T)[None]
```

```python
from contextlib import ExitStack
import math

import numpy as np
import concourse.bass as bass
import concourse.mybir as mybir

F32 = mybir.dt.float32
F32R = mybir.dt.float32r
I32 = mybir.dt.int32
ALU = mybir.AluOpType
ACT = mybir.ActivationFunctionType
AX = mybir.AxisListType.X

T = 256
D = 1024
KT = 8
NE = 32
EPS = 1e-6
NEG = -1e30
LAM_INIT = 0.8 - 0.6 * math.exp(0.0)
DFF = 2816
FK = DFF // 128
SLOT = 4096
NSLOT = 6
CAP = 64
LIMIT = CAP
ARENA = 20800

PCOL = {}
_at = 0
for _name, _n in (("norm_attn", 8), ("qna", 1), ("kna", 1), ("qnb", 1), ("knb", 1), ("subln", 1),
                  ("norm_mlp", 8), ("c2", 16), ("b_ada", 96), ("b_gate", 256), ("b_up", 256),
                  ("norm_mix", 16), ("norm_ffn", 16), ("a_g_out", 8), ("gq", 1), ("gk", 1),
                  ("lam", 4), ("bi", 1), ("bf", 1)):
    PCOL[_name] = _at
    _at += _n
NP = _at

CCOL = {}
_at = 0
for _name, _n in (("ident", 128), ("ones", 128), ("e1", 63), ("e2", 62), ("r1", 128), ("r2", 128), ("swp", 128),
                  ("cos1", 256), ("sin1", 256), ("mask0", 256), ("mask1", 256), ("inv", 1), ("iota", 128), ("sel2", 2)):
    CCOL[_name] = _at
    _at += _n
NCC = _at


def shape_constants():
    c = np.zeros((128, NCC), np.float32)

    def put(name, a):
        c[:, CCOL[name]:CCOL[name] + a.shape[1]] = a

    i = np.arange(128)
    put("ident", np.eye(128, dtype=np.float32))
    put("ones", np.ones((128, 128), np.float32))
    put("e1", np.tile(np.arange(63) == 31, (128, 1)).astype(np.float32))
    put("e2", (np.arange(62)[None, :] == 30 + i[:, None] // 64).astype(np.float32))
    r = np.zeros((128, 128), np.float32)
    r[i[1::2], i[0::2]] = -1.0
    r[i[0::2], i[1::2]] = 1.0
    put("r1", r)
    r = np.zeros((128, 128), np.float32)
    r[i[16:32], i[0:16]] = -1.0
    r[i[0:16], i[16:32]] = 1.0
    put("r2", r)
    put("swp", ((i[:, None] + 64) % 128 == i[None, :]).astype(np.float32))
    n = np.arange(T)
    inv = (1.0 / (np.float32(10000.0) ** (np.arange(16, dtype=np.float32) / np.float32(16)))).astype(np.float32)
    ang = np.concatenate([(n // 64).astype(np.float32)[:, None] * inv,
                          (n % 64).astype(np.float32)[:, None] * inv], axis=1)
    pair = (i % 64) // 2
    put("cos1", np.cos(ang.astype(np.float64)).astype(np.float32).T[pair])
    put("sin1", np.sin(ang.astype(np.float64)).astype(np.float32).T[pair])
    for q in range(2):
        put(f"mask{q}", np.where(n[None, :] <= i[:, None] + 128 * q, 0.0, NEG).astype(np.float32))
    iv = np.zeros(128, np.float32)
    half = (np.float32(500000.0) ** (-np.arange(16, dtype=np.float32) * np.float32(2.0 / 32))).astype(np.float32)
    iv[0:16] = half
    iv[16:32] = half
    put("inv", iv[:, None])
    put("sel2", (i[:, None] % 32 == np.arange(2)[None, :]).astype(np.float32))
    put("iota", np.tile(np.arange(128, dtype=np.float32) % CAP, (128, 1)))
    return c


class Queue:

    def __init__(self, sem):
        self.sem, self.n, self.items, self.met = sem, 0, [], {}

    def _waits(self, needs):
        top = {}

        def walk(x):
            if x is None:
                return
            if isinstance(x, list):
                for y in x:
                    walk(y)
                return
            k = id(x[0])
            if x[1] > self.met.get(k, 0) and x[1] > top.get(k, (None, 0))[1]:
                top[k] = x

        for x in needs:
            walk(x)
        for k, x in top.items():
            self.met[k] = x[1]
        return list(top.values())

    def __call__(self, fn, *needs):
        self.n += 1
        self.items.append((self._waits(needs), fn, self.sem, 1))
        return (self.sem, self.n)

    def dma(self, fn, sem, count, *needs):
        self.items.append((self._waits(needs), fn, sem, 16))
        return (sem, count)

    def last(self):
        return (self.sem, self.n)

    def wait(self, *needs):
        self.items.append((self._waits(needs), None, None, 0))

    def replay(self, eng):
        self.play(eng, self.items)

    def play(self, eng, items):
        for waits, fn, sem, inc in items:
            for s, v in waits:
                eng.wait_ge(s, v)
            if sem == "fork":
                flag, within, beyond = fn
                count = eng.value_load(flag, min_val=0, max_val=T)
                with eng.If(count <= inc):
                    self.play(eng, within)
                with eng.Else():
                    self.play(eng, beyond)
            elif sem == "pad":
                eng.sem_inc(self.sem, inc)
            elif fn is not None:
                fn(eng).then_inc(sem, inc)


class Ring:

    def __init__(self, aps):
        self.aps, self.free = aps, [(k, []) for k in range(len(aps))]

    def take(self):
        assert self.free, "no buffer of the ring is free"
        k, readers = self.free.pop(0)
        return k, self.aps[k], readers

    def give(self, k, *readers):
        self.free.append((k, list(readers)))


def pipeline(gens, width):
    gens, active = list(gens), []
    while gens or active:
        if gens and len(active) < width:
            active.append(gens.pop(0))
        still = []
        for g in active:
            try:
                next(g)
                still.append(g)
            except StopIteration:
                pass
        active = still


def build(nc, A, stage=99):
    with ExitStack() as ctx:
        def sb(name, shape, dt=F32):
            return ctx.enter_context(nc.sbuf_tensor(name, shape, dt))

        def sem(name):
            return ctx.enter_context(nc.semaphore(name))

        pe, dve, act, pool, sp = (Queue(sem(f"s_{n}")) for n in ("pe", "dve", "act", "pool", "sp"))

        con = sb("con", [128, NCC])
        par = sb("par", [128, NP])
        xT = sb("xT", [128, KT, T])
        bdn = sb("bdn", [NE, D])
        rw = sb("rw", [128, KT, NE])
        rb = sb("rb", [128, NE])
        wgt = sb("wgt", [128, KT, 8])
        pos = sb("pos", [128, T], I32)
        small = sb("small", [128, 640])
        ringt = sb("ring", [128, NSLOT, SLOT])
        mod = sb("mod", [128, 96])
        rsn = sb("rsn", [128, T])
        smcol = sb("smcol", [128, 256])
        PS = [ctx.enter_context(nc.psum_tensor(f"ps{i}", [128, 512], F32)) for i in range(8)]

        s_ld = sem("s_ld")
        s_ldp = sem("s_ldp")
        s_ldx = sem("s_ldx")
        s_slot = [sem(f"s_slot{i}") for i in range(NSLOT)]
        s_out = sem("s_out")
        s_brow = sem("s_brow")

        def C(name, w=128, p=128):
            return con[0:p, CCOL[name]:CCOL[name] + w]

        def P(name, j=0, w=1, p=128):
            return par[0:p, PCOL[name] + j:PCOL[name] + j + w]

        def load(dst, src, sem=None):
            sem = sem or s_ld
            nld[id(sem)] = nld.get(id(sem), 0) + 16
            return act.dma(lambda e: e.dma_start(dst, src), sem, nld[id(sem)])

        nld = {}

        at = [0]
        rest = ctx.enter_context(ExitStack())
        nph = [0]

        def lay(*parts):
            rest.close()
            nph[0] += 1
            left = ARENA - sum(int(np.prod(p[1:])) for p in parts)
            out = [rest.enter_context(nc.sbuf_tensor(f"part{nph[0]}_{i}", list(p), F32R)) for i, p in enumerate(parts)]
            at[:] = [0, rest.enter_context(nc.sbuf_tensor(f"arena{nph[0]}", [128, left], F32)), left]
            return out

        lay()

        def alloc(cols, p=128):
            a = at[1][0:p, at[0]:at[0] + cols]
            at[0] += cols
            assert at[0] <= at[2], at[0]
            return a

        def alloc3(k, n, p=128):
            return alloc(k * n, p).rearrange("p (k n) -> p k n", k=k)

        smat = [0]

        def tiny(cols, p=128):
            a = small[0:p, smat[0]:smat[0] + cols]
            smat[0] += cols
            assert smat[0] <= 640, smat[0]
            return a

        def phase(*parts):
            ends = [pe.last(), dve.last(), act.last(), pool.last()]
            for q in (pe, dve, act, pool):
                q.wait(ends)
            smat[0] = 0
            return lay(*parts)

        ctxT = alloc3(KT, T)
        load(par[:, :], A["par"], s_ldp)
        ldp = load(con[:, :], A["con"], s_ldp)
        load(xT[:, :, :], A["xT"].rearrange("(k p) n -> p k n", p=128), s_ldx)
        ldx = load(ctxT[:, :, :], A["ctxT"].rearrange("(k p) n -> p k n", p=128), s_ldx)
        load(bdn[:, :], A["b_down"][0])
        load(rw[:, :, :], A["router_w"][0].rearrange("(k p) n -> p k n", p=128))
        load(rb[:, :], A["router_b"].partition_broadcast(128) if False else A["router_b"].broadcast_to([128, NE]))
        load(wgt[:, :, :], A["a_w_in"][0].rearrange("(k p) n -> p k n", p=128)[:, :, 3072:3080])
        ldr = load(pos[:, :], A["positions"].broadcast_to([128, T]))

        slot_n = [0] * NSLOT
        slots = Ring([ringt[:, i, :] for i in range(NSLOT)])

        class Slot:
            def __init__(self, key, src, k, n, ends=None):
                self.key = key
                self.k, ap, free = slots.take()
                self.ap = ap[:, 0:k * n].rearrange("p (k n) -> p k n", k=k)
                for dst, src in ([(self.ap, src)] if ends is None else ends(self.ap)):
                    slot_n[self.k] += 16
                    self.tok = sp.dma(lambda e, dst=dst, src=src: e.dma_start(dst, src), s_slot[self.k],
                                      slot_n[self.k], free)

            def done(self, *toks):
                slots.give(self.k, *toks)

        early = []

        def wcols(w, c0, n=512, k0=0, k=8, ahead=False):
            key = (w.tensor.name, w.offset, c0, n, k0, k)
            if early and not ahead:
                assert early[0].key == key, (early[0].key, key)
                return early.pop(0)
            slot = Slot(key, w.rearrange("(k p) n -> p k n", p=128)[:, k0:k0 + k, c0:c0 + n], k, n)
            if ahead:
                early.append(slot)
            return slot

        queues = [pe, dve, act, pool, sp]

        def fork(flag, t_flag, limit, within, beyond, extra):
            base = [(q.n, dict(q.met)) for q in queues]
            state = (list(bank.free), list(slots.free), list(slot_n), list(early), list(extra.free))
            ends, bodies, left = [], [], []
            kept = [q.items for q in queues]
            for body in (within, beyond):
                bank.free, slots.free, slot_n[:], early[:], extra.free = (list(x) for x in state)
                for q, (n, met) in zip(queues, base):
                    q.n, q.met, q.items = n, dict(met), []
                body()
                ends.append([q.n for q in queues])
                bodies.append([q.items for q in queues])
                left.append(([k for k, _ in slots.free], list(slot_n), [(x.k, x.key) for x in early]))
            assert left[0] == left[1]
            for i, q in enumerate(queues):
                q.n = max(e[i] for e in ends)
                for e, items in zip(ends, bodies):
                    if e[i] < q.n:
                        items[i].append(([(q.sem, e[i])], None, "pad", q.n - e[i]))
                q.items, q.met = kept[i], dict(base[i][1])
                if bodies[0][i] or bodies[1][i]:
                    q.wait(t_flag)
                    q.items.append(([], (flag, bodies[0][i], bodies[1][i]), "fork", limit))
            end = [q.last() for q in (pe, dve, act)]
            bank.free = [(k, end) for k in range(8)]
            slots.free = [(k, end) for k, _ in slots.free]
            return end

        bank = Ring([p[:, :] for p in PS])

        def mms(out, pairs, *needs, each=None):
            pairs = list(pairs)
            if each is not None and pe.met.get(id(each[-1][0]), 0) < each[-1][1]:
                for i, ((l, r), t) in enumerate(zip(pairs, each)):
                    m = pe(lambda e, i=i, l=l, r=r: e.matmul(out, l, r, start=i == 0, stop=i == len(pairs) - 1,
                                                             skip_group_check=True), t, *needs)
                return m

            def go(e):
                for i, (l, r) in enumerate(pairs):
                    m = e.matmul(out, l, r, start=i == 0, stop=i == len(pairs) - 1, skip_group_check=True)
                return m
            return pe(go, *needs)

        def tt(q, out, a, b, op, *needs):
            return q(lambda e: e.tensor_tensor(out, a, b, op), *needs)

        def ts(q, out, a, s1, s2, op0, op1, *needs):
            if op1 is None:
                return q(lambda e: e.tensor_scalar(out, a, s1, None, op0), *needs)
            return q(lambda e: e.tensor_scalar(out, a, s1, s2, op0, op1), *needs)

        def stt(out, a, s, b, op0, op1, *needs, acc=None):
            if acc is None:
                return dve(lambda e: e.scalar_tensor_tensor(out, a, s, b, op0, op1), *needs)
            return dve(lambda e: e.scalar_tensor_tensor(out, a, s, b, op0, op1, accum_out=acc), *needs)

        def af(out, a, func, *needs, **kw):
            return act(lambda e: e.activation(out, a, func, **kw), *needs)

        def inv_rms(out, ss_ps, ss_tok, n, eps, free):
            a = ts(dve, out, ss_ps, 1.0 / n, eps, ALU.mult, ALU.add, ss_tok, free)
            b = af(out, out, ACT.Sqrt, a)
            c = dve(lambda e: e.reciprocal(out, out), b)
            return c, a

        def norm_full(src, src_tok, rs, sqb, free):
            s = af(sqb[:, :, :], src, ACT.Square, src_tok, free)
            b, ps, fr = bank.take()
            m = mms(ps[:, 0:T], [(C("ones"), sqb[:, k, :]) for k in range(KT)], s, ldp, fr)
            t, used = inv_rms(rs, ps[:, 0:T], m, D, EPS, free)
            bank.give(b, used)
            return t

        class SumSquares:

            def __init__(self, ring):
                self.ring, self.n, self.pend = ring, 0, None
                self.b, self.ps, self.fr = bank.take()

            def chunk(self, c, t):
                k, s, f = self.ring.take()
                t = af(s[:, 0:T], xT[:, c, :], ACT.Square, t, f)
                self.flush()
                self.pend = (k, s, t)

            def flush(self):
                if self.pend is not None:
                    k, s, t = self.pend
                    first, last, out = self.n == 0, self.n == KT - 1, self.ps[:, 0:T]
                    self.m = pe(lambda e: e.matmul(out, C("ones"), s[:, 0:T], start=first, stop=last,
                                                   skip_group_check=True), t, self.fr)
                    self.ring.give(k, self.m)
                    self.n, self.pend = self.n + 1, None

            def finish(self):
                self.flush()
                assert self.n == KT
                t, used = inv_rms(rsn[:, :], self.ps[:, 0:T], self.m, D, EPS, None)
                bank.give(self.b, used)
                return t

        hx = alloc3(KT, T)
        hc = ctxT
        sq = alloc3(KT, T)
        c32 = alloc3(KT, 32)
        t_c0 = pool(lambda e: e.memset(c32, 0.0))
        t_silu = af(c32[:, :, 0:2], P("c2", 0, 16).rearrange("p (k t) -> p k t", t=2), ACT.Silu, ldp, t_c0)
        mod_tok = []
        T_ = {}
        scr = Ring([alloc(512) for _ in range(6)])

        def ada(s):
            w = wcols(A["w_ada"][0], 512 * s)
            b, ps, fr = bank.take()

            def go(e):
                for r in range(2):
                    for g in range(4):
                        m = e.matmul(ps[32 * g:32 * g + 32, :], c32[:, g + 4 * r, :], w.ap[:, g + 4 * r, :],
                                     start=r == 0, stop=r == 1, skip_group_check=True)
                return m
            m = pe(go, w.tok, t_silu, fr)
            w.done(m)
            yield
            kr, rows, fr = scr.take()
            t = af(rows, ps, ACT.Copy, m, fr)
            bank.give(b, t)
            yield
            b, ps2, fr = bank.take()

            def go2(e):
                for j in range(4):
                    m = e.matmul(ps2[:, 2 * j:2 * j + 2], rows[:, 128 * j:128 * j + 128], C("sel2", 2),
                                 start=True, stop=True, skip_group_check=True)
                return m
            m = pe(go2, t, fr)
            scr.give(kr, m)
            t = tt(dve, mod[:, 8 * s:8 * s + 8], ps2[:, 0:8], P("b_ada", 8 * s, 8), ALU.add, m, ldp)
            bank.give(b, t)
            mod_tok.append(t)
            yield

        rsx = alloc(T)
        rsc = alloc(T)
        t_rsx = norm_full(xT[:, :, :], ldx, rsx, sq, None)
        t_rsc = norm_full(ctxT[:, :, :], ldx, rsc, sq, pe.last())
        pipeline([ada(s) for s in range(4)], 3)

        def M(part, k, who=0):
            j = 2 * (8 * part + k) + who
            return mod[:, j:j + 1]

        ga1 = tiny(16)
        gm1 = tiny(8)
        m3 = mod[:, :].rearrange("p (c k t) -> p c k t", c=6, t=2)
        for who in range(2):
            g = ga1.rearrange("p (t k) -> p t k", t=2)[:, who, :]
            t_g = stt(g, m3[:, 1, :, who], 1.0, P("norm_attn", 0, 8), ALU.add, ALU.mult, mod_tok[-1], ldp)

        def modulated(src, dst, rs, t_rs, gcol, shcol, t_g, scr):
            out = []
            for k in range(KT):
                n, buf, fr = scr.take()
                a = stt(buf[:, 0:T], src[:, k, :], gcol(k), rs, ALU.mult, ALU.mult, t_rs, t_g, fr)
                b = af(dst[:, k, :], buf[:, 0:T], ACT.Identity, a, bias=shcol(k))
                scr.give(n, b)
                out.append(b)
            return out

        t_hx = modulated(xT, hx, rsx, t_rsx, lambda k: ga1[:, k:k + 1], lambda k: M(0, k, 0), t_g, scr)
        t_hc = modulated(ctxT, hc, rsc, t_rsc, lambda k: ga1[:, 8 + k:9 + k], lambda k: M(0, k, 1), t_g, scr)

        lam = tiny(1)
        nlam = tiny(1)
        lamt = tiny(4)
        b, ps, fr = bank.take()
        t = tt(dve, lamt[0:64, 0:2], P("lam", 0, 2, 64), P("lam", 2, 2, 64), ALU.mult, ldp)
        t = mms(ps[:, 0:2], [(C("ones")[0:64, :], lamt[0:64, 0:2])], t, ldp, fr)
        t = af(lamt[:, 2:4], ps[:, 0:2], ACT.Exp, t)
        bank.give(b, t)
        t = tt(dve, lam, lamt[:, 3:4], lamt[:, 2:3], ALU.subtract, t)
        t_lam = ts(dve, nlam, lam, -LAM_INIT, None, ALU.add, None, t)

        class Norms:

            def __init__(self, n, per, div, eps):
                self.left, self.n, self.per, self.div, self.eps = n, n, per, div, eps
                self.b, self.ps, self.fr = bank.take()

            def add(self, row, sq, *needs):
                e1 = C("e1", 63)[:, 31 - row:63 - row] if self.per == 1 else C("e2", 62)[:, 30 - row:62 - row]
                first, self.left = self.left == self.n, self.left - 1
                last = self.left == 0
                ps = self.ps
                self.m = pe(lambda e: e.matmul(ps[0:32, 0:T], e1, sq, start=first, stop=last, skip_group_check=True),
                            self.fr, ldp, *needs)
                return self.m

            def finish(self, scale=None):
                assert self.left == 0
                self.k, rs, fs = scr.take()
                self.rs = rs[0:32, 0:T]
                r = self.rs
                t = ts(dve, r, self.ps[0:32, 0:T], 1.0 / self.div, self.eps, ALU.mult, ALU.add, self.m, fs)
                bank.give(self.b, t)
                t = af(r, r, ACT.Sqrt, t)
                t = dve(lambda e: e.reciprocal(r, r), t)
                if scale is not None:
                    t = ts(dve, r, r, scale, None, ALU.mult, None, t)
                self.tok = t

            def spread(self, row, out, *needs):
                rs, w = self.rs, 128 // self.per

                def go(e):
                    for r in range(self.per):
                        m = e.matmul(out[w * r:w * r + w, :], C("ident")[0:32, row + r:row + r + 1].to_broadcast([32, w]),
                                     rs, start=True, stop=True, skip_group_check=True)
                    return m
                return pe(go, self.tok, *needs)

            def close(self, *toks):
                scr.give(self.k, *toks)

        def raw_chunk(w, col, rhs, t_rhs, dst, norms, row, key, last=False):
            b, ps, fr = bank.take()
            m = mms(ps[:, 0:T], [(w.ap[:, k, col:col + 128], rhs[:, k, :]) for k in range(KT)], w.tok, fr, each=t_rhs)
            if last:
                w.done(m)
            yield
            ks, s, fs = scr.take()
            T_[key] = af(dst, ps[:, 0:T], ACT.Copy, m)
            t1 = af(s[:, 0:T], ps[:, 0:T], ACT.Square, m, fs)
            bank.give(b, t1)
            m = norms.add(row, s[:, 0:T], t1)
            scr.give(ks, m)
            yield

        def norm_chunk(dst, norms, row, gcol, key, rot=None):
            kq, q, fq = scr.take()
            b, ps, fr = bank.take()
            m = norms.spread(row, ps[:, 0:T], fr)
            if rot is None:
                t = stt(dst, dst, gcol, ps[:, 0:T], ALU.mult, ALU.mult, m, T_[key])
                bank.give(b, t)
                scr.give(kq, fq)
                T_[key] = t
                norms.last = m
                yield
                return
            R, cs, sn, t_rot = rot
            t3 = stt(q[:, 0:T], dst, gcol, ps[:, 0:T], ALU.mult, ALU.mult, m, T_[key], fq)
            yield
            m = mms(ps[:, T:2 * T], [(R, q[:, 0:T])], t3)
            norms.last = m
            t4 = tt(dve, q[:, T:2 * T], q[:, 0:T], cs, ALU.mult, t3, t_rot)
            t5 = tt(dve, dst, ps[:, T:2 * T], sn, ALU.mult, m, t_rot)
            bank.give(b, t5)
            t6 = tt(dve, dst, q[:, T:2 * T], dst, ALU.add, t4, t5)
            scr.give(kq, t6, m)
            T_[key] = t6
            yield

        def mixed(*lists):
            out = []
            for j in range(max(len(x) for x in lists)):
                out += [x[j] for x in lists if j < len(x)]
            return out

        qa = alloc3(4, T)
        qb = alloc3(4, T)
        kA = alloc(512)
        kS = alloc(512)
        kb = alloc3(4, 512)
        va = alloc3(4, 128)
        vb = alloc3(4, 512)
        rot1 = (C("r1"), C("cos1", 256), C("sin1", 256), ldp)

        W_in = A["w_in"][0]
        w0 = wcols(W_in, 0)
        w1 = wcols(W_in, 512)

        def value_chunk(w, c0, n, j, dst, key, done=False):
            h, tk, q = four[j]
            b, ps, fr = bank.take()
            m = mms(ps[:, 0:n], [(h[:, k, 128 * q:128 * q + 128], w.ap[:, k, c0:c0 + n]) for k in range(KT)],
                    w.tok, tk, fr)
            if done:
                w.done(m)
            yield
            T_[key, j] = af(dst, ps[:, 0:n], ACT.Copy, m)
            bank.give(b, T_[key, j])
            yield

        four = [(hx, t_hx, 0), (hx, t_hx, 1), (hc, t_hc, 0), (hc, t_hc, 1)]
        N1 = Norms(8, 2, 64, EPS)
        ones_ = [(w0, 128 * c, hx, t_hx, qa[:, c, :], ("qa", c), P("qna"), rot1) for c in range(4)]
        ones_ += [(w1, 0, hx, t_hx, kA[:, 0:T], ("ka", 0), P("kna"), rot1),
                  (w1, 0, hc, t_hc, kA[:, T:2 * T], ("ka", 1), P("kna"), None),
                  (w1, 256, hx, t_hx, qb[:, 0, :], ("qb", 0), P("qnb"), rot1),
                  (w1, 384, hx, t_hx, qb[:, 1, :], ("qb", 1), P("qnb"), rot1)]
        pipeline([raw_chunk(w, col, h, th, dst, N1, 2 * i, key, i == 3)
                  for i, (w, col, h, th, dst, key, g, rot) in enumerate(ones_)], 3)
        N1.finish()
        w2 = wcols(W_in, 1024)
        w3 = wcols(W_in, 1536)
        w4 = wcols(W_in, 2048)
        N2 = Norms(10, 2, 64, EPS)
        twos = [(w2, 0, hx, t_hx, qb[:, 2, :], ("qb", 2), P("qnb"), rot1),
                (w2, 128, hx, t_hx, qb[:, 3, :], ("qb", 3), P("qnb"), rot1)]
        for c in range(4):
            w, col = (w2, 256 + 128 * c) if c < 2 else (w3, 128 * (c - 2))
            twos.append((w, col, hx, t_hx, kb[:, c, 0:T], ("kb", c, 0), P("knb"), rot1))
            twos.append((w, col, hc, t_hc, kb[:, c, T:2 * T], ("kb", c, 1), P("knb"), None))
        raws = [value_chunk(w1, 128, 128, j, va[:, j, :], "va", j == 3) for j in range(4)]
        raws += [raw_chunk(w, col, h, th, dst, N2, 2 * i, key, i == 5)
                 for i, (w, col, h, th, dst, key, g, rot) in enumerate(twos)]
        pipeline(mixed(raws, [norm_chunk(dst, N1, 2 * i, g, key, rot)
                              for i, (w, col, h, th, dst, key, g, rot) in enumerate(ones_)]), 3)
        N1.close(N1.last)
        N2.finish()
        vals = [value_chunk(w3, 256, 256, j, vb[:, j, 0:256], "vb0", j == 3) for j in range(4)]
        vals += [value_chunk(w4, 0, 256, j, vb[:, j, 256:512], "vb1") for j in range(4)]
        pipeline(mixed(vals, [norm_chunk(dst, N2, 2 * i, g, key, rot)
                              for i, (w, col, h, th, dst, key, g, rot) in enumerate(twos)]), 3)
        N2.close(N2.last)
        b, ps, fr = bank.take()
        m = mms(ps, [(C("swp"), kA)], T_["ka", 0], T_["ka", 1], fr)
        T_["kS"] = af(kS, ps, ACT.Copy, m)
        bank.give(b, T_["kS"])

        yaT = alloc3(4, T)
        ybT = alloc3(4, T)
        PT = Ring([alloc3(4, T), sq[:, 0:4, :], sq[:, 4:8, :]])

        smn = [0]

        def smc():
            smn[0] = (smn[0] + 1) % 64
            return smcol[:, 4 * smn[0]:4 * smn[0] + 4]

        def softmax(qap, kap, n, scale, tq, mask=None):
            b, ps, fr = bank.take()
            m = mms(ps[:, 0:n], [(qap, kap)], tq, fr)
            yield
            st = smc()
            src = ps[:, 0:n]
            kp, p, fp = scr.take()
            if mask is not None:
                m = tt(dve, p[:, 0:n], ps[:, 0:n], mask, ALU.add, m, fp)
                bank.give(b, m)
                src = p[:, 0:n]
            t = dve(lambda e: e.tensor_reduce(st[:, 0:1], src, AX, ALU.max), m)
            t = ts(dve, st[:, 1:2], st[:, 0:1], -scale, None, ALU.mult, None, t)
            t = af(p[:, 0:n], src, ACT.Exp, t, fp, bias=st[:, 1:2], scale=scale, accum_out=st[:, 2:3])
            if mask is None:
                bank.give(b, t)
            yield
            t = dve(lambda e: e.reciprocal(st[:, 3:4], st[:, 2:3]), t)
            yield (kp, p, st, t)

        def turn(p, tp, n, pt, qt, ftok):
            b, ps, fr = bank.take()

            def go(e):
                for j in range(n // 128):
                    mm = e.transpose(ps[:, 128 * j:128 * j + 128], p[:, 128 * j:128 * j + 128], C("ident"))
                return mm
            m = pe(go, tp, fr, ldp)
            src = ps[:, 0:n].rearrange("p (j q) -> p j q", q=128)
            t = af(pt[:, 0:n // 128, 128 * qt:128 * qt + 128], src, ACT.Copy, m, ftok)
            bank.give(b, t)
            return m, t

        def last_of(gen):
            r = None
            for r in gen:
                if r is None:
                    yield
            return r

        def head_a(h):
            g, half = h // 4, 64 * (h % 2)
            K, tk = (kA, [T_["ka", 0], T_["ka", 1]]) if g == h % 2 else (kS, T_["kS"])
            kpt, pt, fpt = PT.take()
            ev = []
            for qt in range(2):
                kp, p, st, t = yield from last_of(softmax(
                    qa[half:half + 64, h // 2, 128 * qt:128 * qt + 128], K[half:half + 64, :], 512, 0.125,
                    [tk, T_["qa", h // 2]]))
                t = ts(dve, p, p, st[:, 3:4], None, ALU.mult, None, t)
                yield
                m, e = turn(p, t, 512, pt, qt, fpt)
                scr.give(kp, m)
                ev.append(e)
            yield
            b, ps, fr = bank.take()
            m = mms(ps[half:half + 64, 0:T], [(va[:, j, 64 * g:64 * g + 64], pt[:, j, :]) for j in range(4)],
                    ev, [T_["va", j] for j in range(4)], fr)
            PT.give(kpt, m)
            T_["ya", h] = af(yaT[half:half + 64, h // 2, :], ps[half:half + 64, 0:T], ACT.Copy, m)
            bank.give(b, T_["ya", h])
            yield

        sga = ctxT
        sgb = kb.rearrange("p k n -> p (k n)").rearrange("p (k n) -> p k n", k=8)
        gw = {4: w4}

        def gate(i, free=None):
            col = 2304 + 128 * i
            n = col // 512
            if n not in gw:
                gw[n] = wcols(W_in, 512 * n, 256 if n == 8 else 512)
            w = gw[n]
            b, ps, fr = bank.take()
            m = mms(ps[:, 0:T], [(w.ap[:, k, col % 512:col % 512 + 128], hx[:, k, :]) for k in range(KT)], w.tok, fr)
            if col % 512 == 384 or i == 15:
                w.done(m)
            yield
            t = af((sga if i < 8 else sgb)[:, i % 8, :], ps[:, 0:T], ACT.Copy, m, free)
            bank.give(b, t)
            T_["g", i] = t
            yield

        gens = []
        for h in range(8):
            gens += [head_a(h), gate(h)]
            if h % 2 == 0:
                gens.append(ada(4 + h // 2))
        pipeline(gens, 4)

        def head_b(h):
            kpt, pt, fpt = PT.take()
            ev = []
            for qt in range(2):
                r = []
                for mm in range(2):
                    half = 64 * mm
                    r.append((yield from last_of(softmax(
                        qb[half:half + 64, h, 128 * qt:128 * qt + 128], kb[half:half + 64, h, :], 512, 0.125,
                        [T_["qb", h], T_["kb", h, 0], T_["kb", h, 1]]))))
                (k0, p0, s0, t0), (k1, p1, s1, t1) = r
                t = tt(dve, s1[:, 3:4], s1[:, 3:4], nlam, ALU.mult, t1, t_lam)
                t = ts(dve, p1, p1, s1[:, 3:4], None, ALU.mult, None, t)
                t = stt(p0, p0, s0[:, 3:4], p1, ALU.mult, ALU.add, t, t0)
                scr.give(k1, t)
                yield
                m, e = turn(p0, t, 512, pt, qt, fpt)
                scr.give(k0, m)
                ev.append(e)
            yield
            b, ps, fr = bank.take()
            m = mms(ps[:, 0:T], [(vb[:, j, 128 * h:128 * h + 128], pt[:, j, :]) for j in range(4)],
                    ev, [T_["vb0", j] for j in range(4)], [T_["vb1", j] for j in range(4)], fr)
            PT.give(kpt, m)
            T_["yb", h] = af(ybT[:, h, :], ps[:, 0:T], ACT.Copy, m)
            ks, s, fs = scr.take()
            t = af(s[:, 0:T], ps[:, 0:T], ACT.Square, m, fs)
            bank.give(b, t)
            yield
            scr.give(ks, NB.add(h, s[:, 0:T], t))
            yield

        NB = Norms(4, 1, 128, 1e-5)
        pipeline([g for h in range(4) for g in (head_b(h), ada(8 + h))], 3)
        NB.finish(1.0 - LAM_INIT)

        att = [pe.last(), dve.last(), act.last()]
        pipeline(mixed([gate(i, att) for i in range(8, 16)],
                       [norm_chunk(ybT[:, h, :], NB, h, P("subln"), ("yb", h)) for h in range(4)]), 3)
        NB.close(NB.last)
        t_sg = [af(g_, g_, ACT.Sigmoid, [T_["g", 8 * j + i] for i in range(8)]) for j, g_ in enumerate((sga, sgb))]
        mg = sq
        for half in range(2):
            wa = wcols(A["w_oa"][0], 512 * half, 512, 0, 4)
            wb = wcols(A["w_ob"][0], 512 * half, 512, 0, 4)
            for j in range(4):
                c = 4 * half + j
                b, ps, fr = bank.take()
                m1 = mms(ps[:, 0:T], [(wa.ap[:, k, 128 * j:128 * j + 128], yaT[:, k, :]) for k in range(4)],
                         wa.tok, [T_["ya", h] for h in range(8)], fr)
                m2 = mms(ps[:, T:2 * T], [(wb.ap[:, k, 128 * j:128 * j + 128], ybT[:, k, :]) for k in range(4)],
                         wb.tok, [T_["yb", h] for h in range(4)])
                t1 = tt(dve, mg[:, c, :], ps[:, 0:T], sga[:, c, :], ALU.mult, m2, t_sg)
                kt_, u, fu = scr.take()
                t2 = tt(dve, u[:, 0:T], ps[:, T:2 * T], sgb[:, c, :], ALU.mult, m2, t_sg, fu)
                bank.give(b, t2)
                t3 = tt(dve, mg[:, c, :], mg[:, c, :], u[:, 0:T], ALU.add, t1, t2)
                scr.give(kt_, t3)
            wa.done(m1)
            wb.done(m2)

        def project_out(w_, K, src, t_src, gate):
            ss = SumSquares(scr)
            for half in range(2):
                ws = [wcols(w_, 512 * half, 512, k0, min(8, K - k0)) for k0 in range(0, K, 8)]
                for j in range(4):
                    c = 4 * half + j
                    b, ps, fr = bank.take()
                    prs = [(ws[k // 8].ap[:, k % 8, 128 * j:128 * j + 128], src[:, k, :]) for k in range(K)]
                    m = mms(ps[:, 0:T], prs, [w.tok for w in ws], t_src, fr)
                    t = stt(xT[:, c, :], ps[:, 0:T], gate(c), xT[:, c, :], ALU.mult, ALU.add, m) if gate else \
                        tt(dve, xT[:, c, :], ps[:, 0:T], xT[:, c, :], ALU.add, m)
                    bank.give(b, t)
                    ss.chunk(c, t)
                for w in ws:
                    w.done(m)
            return ss.finish()

        t_x = project_out(A["w_out"][0], KT, mg, [t3] + mod_tok, lambda c: M(2, c))

        def moe(t_x, following):
            phase()
            for q in (pe, dve, act, pool):
                q.wait(ldr)
            h2 = alloc3(KT, T)
            sq = alloc3(KT, T)
            scr = Ring([alloc(512) for _ in range(4)])
            rs = alloc(T)
            wT = alloc(T, NE)
            gm1 = tiny(8)
            t_g = stt(gm1, m3[:, 4, :, 0], 1.0, P("norm_mlp", 0, 8), ALU.add, ALU.mult)
            t_h = modulated(xT, h2, rsn[:, :], t_x, lambda k: gm1[:, k:k + 1], lambda k: M(3, k), t_g, scr)
            tw, tm, Gs = [], [], []
            mT = alloc(T, NE)
            for q in range(2):
                b, ps, fr = bank.take()
                m = mms(ps[:, 0:NE], [(h2[:, k, 128 * q:128 * q + 128], rw[:, k, :]) for k in range(KT)], t_h, fr)
                L, E_, G, Q, R_ = (tiny(NE) for _ in range(5))
                m8, s = tiny(8), tiny(4)
                t = tt(dve, L, ps[:, 0:NE], rb[:, :], ALU.add, m)
                bank.give(b, t)
                t = dve(lambda e, m8=m8, L=L: e.max(m8, L), t)
                t0 = ts(dve, s[:, 0:1], m8[:, 0:1], -1.0, None, ALU.mult, None, t)
                te = af(E_, L, ACT.Exp, t0, bias=s[:, 0:1])
                t1 = dve(lambda e, G=G, L=L, m8=m8, s=s: e.tensor_scalar(
                    G, L, m8[:, 3:4], 0.0, ALU.is_gt, ALU.add, accum_out=s[:, 1:2]), t)
                t2 = ts(dve, Q, L, m8[:, 3:4], None, ALU.is_equal, None, t)
                t3 = dve(lambda e, R_=R_, Q=Q: e.tensor_tensor_scan(R_, Q, Q, 0.0, ALU.add, ALU.bypass), t2)
                t4 = ts(dve, R_, R_, s[:, 1:2], 4.0, ALU.add, ALU.is_le, t3, t1)
                t5 = tt(dve, Q, Q, R_, ALU.mult, t4)
                t6 = tt(dve, G, G, Q, ALU.add, t5)
                Wt = E_
                t7 = stt(Wt, G, 1.0, E_, ALU.mult, ALU.mult, t6, te, acc=s[:, 2:3])
                t8 = dve(lambda e, s=s: e.reciprocal(s[:, 3:4], s[:, 2:3]), t7)
                t9 = ts(dve, Wt, Wt, s[:, 3:4], None, ALU.mult, None, t8)
                b, ps, fr = bank.take()
                m = pe(lambda e, ps=ps, G=G: e.transpose(ps[0:NE, 0:128], G, C("ident")), t6, fr)
                m = pe(lambda e, ps=ps, Wt=Wt: e.transpose(ps[0:NE, 128:256], Wt, C("ident")), t9)
                ta = af(mT[:, 128 * q:128 * q + 128], ps[0:NE, 0:128], ACT.Copy, m)
                tb = af(wT[:, 128 * q:128 * q + 128], ps[0:NE, 128:256], ACT.Copy, m)
                bank.give(b, tb)
                tm.append(ta)
                tw.append(tb)
                Gs.append((Wt, t9))
            cnt, posT = alloc(T, NE), alloc(T, NE)
            most = alloc(NE, 1)
            flag = alloc(4, 1).bitcast(I32)[:, 0:1]
            posK = tiny(64).rearrange("p (q e) -> p q e", q=2)
            t_cnt = dve(lambda e: e.tensor_tensor_scan(cnt, mT, mT, 0.0, ALU.add, ALU.bypass), tm)
            t = tt(dve, posT, cnt, mT, ALU.mult, t_cnt)
            t = ts(dve, posT, posT, -1.0, None, ALU.add, None, t)
            b, ps, fr = bank.take()
            for q in range(2):
                m = pe(lambda e, ps=ps, q=q: e.transpose(ps[:, NE * q:NE * q + NE], posT[:, 128 * q:128 * q + 128],
                                                         C("ident", NE, NE)), t, fr)
            m2 = pe(lambda e, ps=ps: e.transpose(ps[0:1, 128:128 + NE], cnt[:, T - 1:T], C("ident", NE, NE)), t_cnt)
            t_pos = af(posK, ps[:, 0:64].rearrange("p (q e) -> p q e", q=2), ACT.Copy, m, m2)
            t = dve(lambda e, ps=ps: e.tensor_reduce(most[:, 0:1], ps[0:1, 128:128 + NE], AX, ALU.max), m2, t_pos)
            bank.give(b, t, t_pos)
            t_flag = dve(lambda e: e.tensor_copy(flag, most[:, 0:1]), t)
            Wg, Wu, Wd = A["w_gate"][0], A["w_up"][0], A["w_down"][0]
            order = [(Wg, 0), (Wu, 0), (Wg, 4), (Wu, 4), (Wd, 0), (Wd, 4)]
            for W, k0 in order:
                wcols(W[0], 0, 1024, k0, 4, ahead=True)
            brow = alloc3(2, D)
            t_z = pool(lambda e: e.memset(brow, 0.0), pe.last(), dve.last(), act.last())
            act.dma(lambda e: e.dma_start(brow[0:NE, 0, :], A["b_gate"][0]), s_brow, 16, t_z)
            t_br = act.dma(lambda e: e.dma_start(brow[0:NE, 1, :], A["b_up"][0]), s_brow, 32)
            assert len(bank.free) == 8
            before = [r for _, r in bank.free]
            Y = [PS[4 + c // 2][:, T * (c % 2):T * (c % 2) + T] for c in range(8)]
            for c in range(8):
                mY = pe(lambda e, c=c: e.matmul(Y[c], bdn[:, 128 * c:128 * c + 128], wT, start=c % 2 == 0, stop=False,
                                                skip_group_check=True), before, tw)
            free4 = [(k, r) for k, r in bank.free if k < 4]
            bank.free = free4
            htok = sq.rearrange("p k n -> p (k n)").rearrange("p (q n) -> p q n", q=2)
            for q in range(2):
                for g in range(2):
                    b, ps, fr = bank.take()

                    def go(e, ps=ps, q=q, g=g):
                        for j in range(4):
                            m = e.transpose(ps[:, 128 * j:128 * j + 128],
                                            h2[:, 4 * g + j, 128 * q:128 * q + 128], C("ident"))
                        return m
                    m = pe(go, t_h, fr)
                    t_tok = af(htok[:, q, 512 * g:512 * g + 512], ps, ACT.Copy, m)
                    bank.give(b, t_tok)
            mark = at[0]

            def finish(m):
                ss = SumSquares(scr)
                for c in range(8):
                    ss.chunk(c, stt(xT[:, c, :], Y[c], M(5, c), xT[:, c, :], ALU.mult, ALU.add, m))
                ss.finish()
                for args in following:
                    wcols(*args, ahead=True)

            def swiglu(out, ps, gsl, usl, ex, f, m, s, fs, scale_by, free):
                n = gsl.stop - gsl.start
                g, u = s[:, 0:n], s[:, T:T + n]
                t1 = ts(dve, g, ps[:, gsl], P("b_gate", 8 * ex + f), 7.0, ALU.add, ALU.min, m, fs)
                t2 = ts(dve, u, ps[:, usl], P("b_up", 8 * ex + f), 7.0, ALU.add, ALU.min, m, fs)
                t3 = af(out, g, ACT.Sigmoid, t1, free, scale=1.702)
                t4 = ts(dve, u, u, -7.0, 1.0, ALU.max, ALU.add, t2)
                if scale_by is not None:
                    t4 = tt(dve, u, u, scale_by[0], ALU.mult, t4, scale_by[1])
                t5 = tt(dve, g, g, u, ALU.mult, t4, t3)
                return tt(dve, out, out, g, ALU.mult, t5), t2

            def routed():
                at[0] = mark
                xgs = Ring([alloc3(KT, CAP) for _ in range(2)])
                aTs = Ring([alloc3(KT, CAP) for _ in range(2)])
                ygs = Ring([alloc(512) for _ in range(2)])
                PwTs = Ring([alloc(T) for _ in range(2)])
                Ss = Ring([alloc(6 * CAP) for _ in range(2)])
                guss = Ring([alloc3(3, D, CAP) for _ in range(2)])

                def select(ex):
                    kS_, S, fS = Ss.take()
                    for q in range(2):
                        t1 = ts(dve, S[:, CAP * q:CAP * q + CAP], C("iota", CAP), posK[:, q, ex:ex + 1], None,
                                ALU.is_equal, None, t_pos, fS)
                    for q in range(2):
                        t2 = ts(dve, S[:, 2 * CAP * (q + 1):2 * CAP * (q + 2)], C("iota"), posK[:, q, ex:ex + 1],
                                Gs[q][0][:, ex:ex + 1], ALU.is_equal, ALU.mult, t_pos, fS)
                    return kS_, S, t1, t2

                def gather(kS_, S, t1, t2):
                    kx, xg, fx = xgs.take()
                    kp, PwT, fp = PwTs.take()
                    b, ps, fr = bank.take()

                    def go(e):
                        for j in range(KT):
                            for q in range(2):
                                m = e.matmul(ps[:, CAP * j:CAP * j + CAP], htok[:, q, 128 * j:128 * j + 128],
                                             S[:, CAP * q:CAP * q + CAP], start=q == 0, stop=q == 1,
                                             skip_group_check=True)
                        return m
                    m = pe(go, t1, t_tok, fr)
                    t = af(xg[:, :, :], ps.rearrange("p (j s) -> p j s", j=KT), ACT.Copy, m, fx)
                    bank.give(b, t)
                    b2, ps2, fr2 = bank.take()

                    def go2(e):
                        for q in range(2):
                            m = e.transpose(ps2[:, 128 * q:128 * q + 128], S[:, 2 * CAP * (q + 1):2 * CAP * (q + 2)],
                                            C("ident"))
                        return m
                    m = pe(go2, t2, fr2)
                    tp = af(PwT, ps2[:, 0:T], ACT.Copy, m, fp)
                    bank.give(b2, tp)
                    Ss.give(kS_, m)
                    return kx, xg, t, kp, PwT, tp

                def gate_up(ex, xg, t_xg):
                    two = [bank.take() for _ in range(2)]
                    sel = C("ident")[:, ex:ex + 1].to_broadcast([128, CAP])

                    def bias(e):
                        for h in range(2):
                            for r in range(2):
                                m = e.matmul(two[h][1][CAP * r:CAP * r + CAP, :], sel, brow[:, r, 512 * h:512 * h + 512],
                                             start=True, stop=False, skip_group_check=True)
                        return m
                    pe(bias, t_br, [x[2] for x in two])
                    for kh in range(2):
                        w = [wcols(W[ex], 0, 1024, 4 * kh, 4) for W in (Wg, Wu)]

                        def go(e, w=w, kh=kh):
                            for k in range(4):
                                for h in range(2):
                                    for r in range(2):
                                        m = e.matmul(two[h][1][CAP * r:CAP * r + CAP, :], xg[:, 4 * kh + k, :],
                                                     w[r].ap[:, k, 512 * h:512 * h + 512], start=False,
                                                     stop=kh == 1 and k == 3, skip_group_check=True)
                            return m
                        m = pe(go, [x.tok for x in w], t_xg)
                        for x in w:
                            x.done(m)
                    return two, m

                def act_of(two, m):
                    kg, gus, fg = guss.take()
                    out = []
                    for h in range(2):
                        sl = slice(512 * h, 512 * h + 512)
                        g, u, sg = gus[:, 0, sl], gus[:, 1, sl], gus[:, 2, sl]
                        ps = two[h][1]
                        t1 = ts(dve, g, ps[0:CAP, :], 7.0, None, ALU.min, None, m, fg)
                        t2 = ts(dve, u, ps[CAP:2 * CAP, :], 7.0, -7.0, ALU.min, ALU.max, m, fg)
                        bank.give(two[h][0], t1, t2)
                        t3 = af(sg, g, ACT.Sigmoid, t1, fg, scale=1.702)
                        t4 = stt(u, u, 1.0, g, ALU.add, ALU.mult, t2, t1)
                        out.append(tt(dve, u, u, sg, ALU.mult, t4, t3))
                    return kg, gus, out

                def down(ex, kg, gus, t_act):
                    kaT, aT, fa = aTs.take()
                    b, ps, fr = bank.take()

                    def turn_act(e, h):
                        for j in range(4 * h, 4 * h + 4):
                            m = e.transpose(ps[:, CAP * j:CAP * j + CAP], gus[:, 1, 128 * j:128 * j + 128],
                                            C("ident", CAP, CAP))
                        return m
                    m0 = pe(lambda e: turn_act(e, 0), t_act[0], fr)
                    m1 = pe(lambda e: turn_act(e, 1), t_act[1])
                    guss.give(kg, m1)
                    t = af(aT[:, :, :], ps.rearrange("p (j s) -> p j s", j=KT), ACT.Copy, m1, fa)
                    bank.give(b, t)
                    b, ps2, fr = bank.take()
                    for kh in range(2):
                        wd = wcols(Wd[ex], 0, 1024, 4 * kh, 4)

                        def go(e, wd=wd, kh=kh):
                            for k in range(4):
                                for h in range(2):
                                    m = e.matmul(ps2[CAP * h:CAP * h + CAP, :], aT[:, 4 * kh + k, :],
                                                 wd.ap[:, k, 512 * h:512 * h + 512], start=kh == 0 and k == 0,
                                                 stop=kh == 1 and k == 3, skip_group_check=True)
                            return m
                        m = pe(go, wd.tok, t, fr)
                        wd.done(m)
                    aTs.give(kaT, m)
                    ky, yg, fy = ygs.take()
                    t = af(yg, ps2, ACT.Copy, m, fy)
                    bank.give(b, t)
                    return ky, yg, t

                def put_back(ex, ky, yg, t_yg, kp, PwT, t_pw):
                    def go(e):
                        for c in range(4):
                            for h in range(2):
                                m = e.matmul(Y[4 * h + c], yg[CAP * h:CAP * h + CAP, 128 * c:128 * c + 128],
                                             PwT[CAP * h:CAP * h + CAP, :], start=False, stop=ex == NE - 1,
                                             skip_group_check=True)
                        return m
                    m = pe(go, t_yg, t_pw)
                    ygs.give(ky, m)
                    PwTs.give(kp, m)
                    return m

                nxt = gather(*select(0))
                owed = None
                for ex in range(NE):
                    kx, xg, t_xg, kp, PwT, t_pw = nxt
                    if ex + 1 < NE:
                        sel = select(ex + 1)
                    two, m = gate_up(ex, xg, t_xg)
                    xgs.give(kx, m)
                    kg, gus, t_act = act_of(two, m)
                    if owed is not None:
                        put_back(*owed)
                    if ex + 1 < NE:
                        nxt = gather(*sel)
                    ky, yg, t_yg = down(ex, kg, gus, t_act)
                    owed = (ex, ky, yg, t_yg, kp, PwT, t_pw)
                finish(put_back(*owed))

            def dense():
                at[0] = mark
                acts = Ring([alloc3(KT, T)])
                wb = Ring([alloc(T), alloc(T)])
                for ex in range(NE):
                    ka, ac, fa = acts.take()
                    b, bt, fb = bank.take()
                    m = mms(bt[:, 0:T], [(C("ident")[0:NE, ex:ex + 1].to_broadcast([NE, 128]), wT)], tw, fb)
                    kw, wbt, fw = wb.take()
                    t_wb = af(wbt, bt[:, 0:T], ACT.Copy, m, fw)
                    bank.give(b, t_wb)
                    toks = []
                    w = [wcols(W[ex], 0, 1024, k0, 4) for W, k0 in order[0:4]]
                    for f in range(8):
                        b, ps, fr = bank.take()
                        for r in range(2):
                            m = mms(ps[:, T * r:T * r + T], [(w[2 * (k // 4) + r].ap[:, k % 4, 128 * f:128 * f + 128],
                                                              h2[:, k, :]) for k in range(KT)], [x.tok for x in w], fr)
                        ks, s, fs = scr.take()
                        t, used = swiglu(ac[:, f, :], ps, slice(0, T), slice(T, 2 * T), ex, f, m, s, fs, (wbt, t_wb), fa)
                        bank.give(b, used)
                        scr.give(ks, t)
                        toks.append(t)
                    for x in w:
                        x.done(m)
                    wb.give(kw, t)
                    for kh in range(2):
                        wd = wcols(Wd[ex], 0, 1024, 4 * kh, 4)

                        def go(e, wd=wd, kh=kh, ac=ac, last=ex == NE - 1):
                            for k in range(4):
                                for c in range(8):
                                    m = e.matmul(Y[c], wd.ap[:, k, 128 * c:128 * c + 128], ac[:, 4 * kh + k, :],
                                                 start=False, stop=last and kh == 1 and k == 3, skip_group_check=True)
                            return m
                        m = pe(go, wd.tok, toks, mY)
                        wd.done(m)
                    acts.give(ka, m)
                finish(m)

            return fork(flag, [t_flag, t_br], LIMIT, routed, dense, scr)

        if stage >= 2:
            Wa = A["a_w_in"][0]
            t_x = moe(t_x, [(Wa, 512 * i) for i in range(6)] if stage >= 3 else [])

        def normed(t_x, gname, layer):
            u = alloc3(KT, T)
            return u, [stt(u[:, k, :], xT[:, k, :], P(gname, 8 * layer + k), rsn[:, :], ALU.mult, ALU.mult, t_x)
                       for k in range(KT)]

        def ffn(t_x, layer):
            nonlocal scr
            up, wp = phase((128, 2, KT, T), (128, 6, 2, 512))
            u, t_u = normed(t_x, "norm_ffn", layer)
            scr = Ring([alloc(512) for _ in range(5)])
            g = alloc3(FK, T)
            pieces = Ring([wp[:, i, :, :] for i in range(6)])

            def halves(hi, lo, x, t, *needs):
                t1 = af(hi, x, ACT.Copy, t, *needs)
                t2 = tt(dve, lo, x, hi.bitcast(F32), ALU.subtract, t, t1, *needs)
                return t1, t2

            t_up = [halves(up[:, 0, k, :], up[:, 1, k, :], u[:, k, :], t_u[k])[1] for k in range(KT)]
            W = A["ffn_w_in"][layer].rearrange("(k p) (h n) -> p k h n", p=128, h=2)
            tg = []

            def turn_in(s, sides):
                acts = []
                for q in range(2):
                    b, ps, m = sides[q]
                    ks, sg, fs = scr.take()
                    t = af(sg[:, 0:T], ps[:, 0:T], ACT.Silu, m, fs)
                    t = tt(dve, sg[:, T:2 * T], ps[:, T:2 * T], sg[:, 0:T], ALU.mult, t)
                    bank.give(b, t)
                    acts.append((ks, sg, t))
                yield
                b, ps2, fr = bank.take()

                def go(e):
                    for j in range(2):
                        for q in range(2):
                            m = e.transpose(ps2[:, T * j + 128 * q:T * j + 128 * q + 128],
                                            acts[q][1][:, T + 128 * j:T + 128 * j + 128], C("ident"))
                    return m
                m = pe(go, acts[0][2], acts[1][2], fr)
                scr.give(acts[0][0], m)
                scr.give(acts[1][0], m)
                t = af(g[:, 2 * s:2 * s + 2, :], ps2.rearrange("p (j n) -> p j n", j=2), ACT.Copy, m)
                bank.give(b, t)
                tg.append(t)
                yield

            def split(s):
                w = Slot(None, None, 8, 512, lambda ap: [
                    (ap[:, :, T * h:T * h + T], W[:, :, h, 256 * s:256 * s + 256]) for h in range(2)])
                done = []
                for k in range(KT):
                    kp, pc, fp = pieces.take()
                    t = halves(pc[:, 0, :], pc[:, 1, :], w.ap[:, k, :], w.tok, fp)
                    done += t
                    if k == KT - 1:
                        w.done(*done)
                    yield kp, pc, list(t)

            AHEAD = 4
            source = (x for s in range(11) for x in split(s))
            made = [next(source) for _ in range(AHEAD)]
            owed = None
            for s in range(11):
                banks = [bank.take() for _ in range(2)]
                for k in range(KT):
                    made += [x for x in [next(source, None)] if x]
                    kp, pc, t = made.pop(0)

                    def go(e, k=k, pc=pc, banks=banks):
                        for q in range(2):
                            for i, (a, b) in enumerate(((0, 0), (0, 1), (1, 0))):
                                m = e.matmul(banks[q][1], up[:, a, k, 128 * q:128 * q + 128], pc[:, b, :],
                                             start=k == 0 and i == 0, stop=k == KT - 1 and i == 2,
                                             skip_group_check=True)
                        return m
                    m = pe(go, t, t_up[k], [x[2] for x in banks])
                    pieces.give(kp, m)
                    if owed is not None and k in (0, 3):
                        next(owed)
                owed = turn_in(s, [(x[0], x[1], m) for x in banks])
            Wo = A["ffn_w_out"][layer]
            parts = Ring([up[:, :, k, :] for k in range(KT)])
            parts.free = [(k, [m]) for k, _ in parts.free]

            def split_out():
                for half in range(2):
                    for k0 in range(0, FK, 8):
                        n = min(8, FK - k0)
                        w = wcols(Wo, 512 * half, 512, k0, n)
                        done = []
                        for k in range(n):
                            kp, pc, fp = pieces.take()
                            t = halves(pc[:, 0, :], pc[:, 1, :], w.ap[:, k, :], w.tok, fp)
                            done += t
                            if k == n - 1:
                                w.done(*done)
                            kg, gp, fg = parts.take()
                            t2 = halves(gp[:, 0, :], gp[:, 1, :], g[:, k0 + k, :], tg[(k0 + k) // 2], fg)
                            yield kp, pc, kg, gp, list(t) + list(t2)

            source = split_out()
            made = [next(source) for _ in range(AHEAD)]
            next(owed)
            next(owed)
            ss = None if layer == 1 else SumSquares(scr)
            for half in range(2):
                banks = [bank.take() for _ in range(4)]
                for k in range(FK):
                    made += [x for x in [next(source, None)] if x]
                    kp, pc, kg, gp, t = made.pop(0)

                    def go(e, k=k, pc=pc, gp=gp, banks=banks):
                        for j in range(4):
                            for i, (a, b) in enumerate(((0, 0), (0, 1), (1, 0))):
                                m = e.matmul(banks[j][1][:, 0:T], pc[:, a, 128 * j:128 * j + 128], gp[:, b, :],
                                             start=k == 0 and i == 0, stop=k == FK - 1 and i == 2,
                                             skip_group_check=True)
                        return m
                    m = pe(go, t, [x[2] for x in banks])
                    pieces.give(kp, m)
                    parts.give(kg, m)
                for j in range(4):
                    c = 4 * half + j
                    t = tt(dve, xT[:, c, :], banks[j][1][:, 0:T], xT[:, c, :], ALU.add, m)
                    bank.give(banks[j][0], t)
                    if ss is not None:
                        ss.chunk(c, t)
            return t if layer == 1 else ss.finish()

        def mlstm(t_x):
            nonlocal scr
            phase()
            u, t_u = normed(t_x, "norm_mix", 0)
            scr = Ring([alloc(512) for _ in range(6)])
            qT = alloc3(4, T)
            kT = alloc3(4, T)
            v = alloc3(2, 1024)
            so = alloc3(8, T)
            y = alloc3(KT, T)
            qkT = Ring([alloc3(2, T) for _ in range(3)])
            W = A["a_w_in"][0]
            ig, fg, tmp, F_, a_ = (alloc(T, 4) for _ in range(5))
            b, ps, fr = bank.take()
            m = mms(ps[0:4, 0:T], [(wgt[:, k, 0:4], u[:, k, :]) for k in range(KT)], t_u, fr)
            m = mms(ps[0:4, T:2 * T], [(wgt[:, k, 4:8], u[:, k, :]) for k in range(KT)])
            ti = ts(dve, ig, ps[0:4, 0:T], P("bi", p=4), None, ALU.add, None, m)
            t = ts(dve, fg, ps[0:4, T:2 * T], P("bf", p=4), None, ALU.add, None, m)
            bank.give(b, ti, t)
            t1 = stt(tmp, fg, -1.0, fg, ALU.mult, ALU.max, t)
            t1 = af(tmp, tmp, ACT.Exp, t1, scale=-1.0)
            t1 = ts(dve, tmp, tmp, 1.0, None, ALU.add, None, t1)
            t1 = af(tmp, tmp, ACT.Ln, t1)
            t = stt(fg, fg, 0.0, tmp, ALU.min, ALU.subtract, t1, t)
            t = dve(lambda e: e.tensor_tensor_scan(F_, fg, fg, 0.0, ALU.add, ALU.bypass), t)
            t_a = tt(dve, a_, ig, F_, ALU.subtract, t, ti)
            Fc = tiny(8)
            b, ps, fr = bank.take()
            for q in range(2):
                m = mms(ps[:, 4 * q:4 * q + 4], [(F_[:, 128 * q:128 * q + 128], C("ident", 4, 4))], t, fr)
            t_F = dve(lambda e, ps=ps: e.tensor_copy(Fc, ps[:, 0:8]), m)
            bank.give(b, t_F)
            tq = {}
            for which, dst in ((0, qT), (1, kT)):
                w = wcols(W, 512 * which)
                for j in range(4):
                    b, ps, fr = bank.take()
                    m = mms(ps[:, 0:T], [(w.ap[:, k, 128 * j:128 * j + 128], u[:, k, :]) for k in range(KT)],
                            w.tok, fr)
                    t = af(dst[:, j, :], ps[:, 0:T], ACT.Copy, m)
                    bank.give(b, t)
                    tq[which, j] = t
                w.done(m)
            tv = []
            for half in range(2):
                w = wcols(W, 1024 + 512 * half)
                for q in range(2):
                    b, ps, fr = bank.take()
                    m = mms(ps, [(u[:, k, 128 * q:128 * q + 128], w.ap[:, k, :]) for k in range(KT)], w.tok, fr)
                    t = af(v[:, q, 512 * half:512 * half + 512], ps, ACT.Copy, m)
                    bank.give(b, t)
                    tv.append(t)
                w.done(m)
            ow = {}

            def out_gate(j):
                if j // 4 not in ow:
                    ow[j // 4] = wcols(W, 2048 + 512 * (j // 4))
                w = ow[j // 4]
                b, ps, fr = bank.take()
                c = 128 * (j % 4)
                m = mms(ps[:, 0:T], [(w.ap[:, k, c:c + 128], u[:, k, :]) for k in range(KT)], w.tok, fr)
                if j % 4 == 3:
                    w.done(m)
                yield
                T_["o", j] = af(so[:, j, :], ps[:, 0:T], ACT.Copy, m)
                bank.give(b, T_["o", j])
                yield

            ty = []

            def head(h):
                kq, qk, fqk = qkT.take()
                b, aps, fr = bank.take()
                ma = mms(aps[:, 0:T], [(C("ident", p=4)[:, h:h + 1].to_broadcast([4, 128]), a_)], t_a, fr)
                mz = None
                if True:
                    mz = dve(lambda e: e.memset(qk[:, 1, 0:128], 0.0), fqk)
                ev = [mz]
                for q in range(2):
                    n = 128 * (q + 1)
                    b2, sp_, fr2 = bank.take()
                    ms = mms(sp_[:, 0:n], [(qT[:, h, 128 * q:128 * q + 128], kT[:, h, 0:n])], tq[0, h], tq[1, h], fr2)
                    ks, s, fs = scr.take()
                    st = smc()
                    am, w = s[:, 0:n], s[:, T:T + n]
                    t1 = tt(dve, am, aps[:, 0:n], C(f"mask{q}", n), ALU.add, ma, fs)
                    t2 = dve(lambda e, st=st, am=am: e.tensor_reduce(st[:, 0:1], am, AX, ALU.max), t1)
                    t3 = ts(dve, st[:, 1:2], st[:, 0:1], 0.0, -1.0, ALU.max, ALU.mult, t2)
                    t4 = af(w, am, ACT.Exp, t3, bias=st[:, 1:2])
                    yield
                    t5 = stt(am, sp_[:, 0:n], 128.0 ** -0.5, w, ALU.mult, ALU.mult, t4, ms, acc=st[:, 2:3])
                    bank.give(b2, t5)
                    t6 = tt(dve, st[:, 1:2], st[:, 1:2], Fc[:, 4 * q + h:4 * q + h + 1], ALU.subtract, t4, t_F)
                    t7 = af(st[:, 1:2], st[:, 1:2], ACT.Exp, t6)
                    t8 = stt(st[:, 2:3], st[:, 2:3], -1.0, st[:, 2:3], ALU.mult, ALU.max, t5)
                    t9 = tt(dve, st[:, 2:3], st[:, 2:3], st[:, 1:2], ALU.max, t7, t8)
                    t10 = dve(lambda e, st=st: e.reciprocal(st[:, 3:4], st[:, 2:3]), t9)
                    t11 = ts(dve, am, am, st[:, 3:4], None, ALU.mult, None, t10)
                    yield
                    mt, te = turn(am, t11, n, qk, q, fqk)
                    scr.give(ks, mt)
                    ev.append(te)
                bank.give(b, t1)
                yield
                b, ps, fr = bank.take()
                for c in range(2):
                    m = mms(ps[:, T * c:T * c + T],
                            [(v[:, j, 256 * h + 128 * c:256 * h + 128 * c + 128], qk[:, j, :]) for j in range(2)],
                            ev, tv, fr)
                qkT.give(kq, m)
                ks, s, fs = scr.take()
                t0 = af(y[:, 2 * h:2 * h + 2, :], ps.rearrange("p (c n) -> p c n", c=2), ACT.Copy, m)
                t = af(s, ps, ACT.Square, m, fs)
                bank.give(b, t)
                yield
                NM.add(h, s[:, 0:T], t)
                scr.give(ks, NM.add(h, s[:, T:2 * T], t))
                T_["y", 2 * h] = T_["y", 2 * h + 1] = t0
                yield

            NM = Norms(8, 1, 256, EPS)
            pipeline([g for h in range(4) for g in (out_gate(2 * h), head(h), out_gate(2 * h + 1))], 3)
            NM.finish()
            t_so = af(so[:, :, :], so[:, :, :], ACT.Sigmoid, [T_["o", j] for j in range(8)])
            pipeline([norm_chunk(y[:, j, :], NM, j // 2, P("a_g_out", j), ("y", j)) for j in range(8)], 3)
            NM.close(NM.last)
            for j in range(8):
                ty.append(tt(dve, y[:, j, :], y[:, j, :], so[:, j, :], ALU.mult, T_["y", j], t_so))
            return project_out(A["a_w_out"][0], KT, y, ty, None)

        def moba(t_x):
            nonlocal scr
            phase()
            u, t_u = normed(t_x, "norm_mix", 1)
            scr = Ring([alloc(512) for _ in range(8)])
            qT = alloc3(8, T)
            kT = alloc3(8, T)
            v = alloc3(2, 1024)
            y = alloc3(8, T)
            cs, sn = alloc(T), alloc(T)
            PT = Ring([alloc3(2, T) for _ in range(4)])
            ang, kk, r = alloc(T), alloc(T), alloc(T)
            t = pool(lambda e: e.tensor_copy(r, pos[:, :]), ldr)
            t_ang = ts(pool, ang, r, C("inv", 1), None, ALU.mult, None, t)
            MAGIC = 12582912.0
            C1, C2 = 6.28125, 0.0019350051879882812
            C3 = 2.0 * math.pi - C1 - C2
            for dst, shift in ((sn, 0.0), (cs, 0.25)):
                t = ts(pool, kk, ang, 1.0 / (2.0 * math.pi), shift, ALU.mult, ALU.add, t_ang, t)
                t = ts(pool, kk, kk, MAGIC, None, ALU.add, None, t)
                t = ts(pool, kk, kk, MAGIC, None, ALU.subtract, None, t)
                t1 = ts(pool, r, kk, -C1, None, ALU.mult, None, t)
                t = tt(pool, dst, r, ang, ALU.add, t1)
                for part in (C2, C3):
                    t = ts(pool, r, kk, -part, None, ALU.mult, None, t)
                    t = tt(pool, dst, dst, r, ALU.add, t)
                t = ts(pool, dst, dst, 2.0 * math.pi * shift, 3.1415925, ALU.add, ALU.min, t)
                t = ts(pool, dst, dst, -3.1415925, None, ALU.max, None, t)
            t_angles = t
            W = A["b_w_in"][0]

            ws = [wcols(W, 512 * s) for s in range(4)]
            NQ, NK_ = Norms(8, 1, 128, EPS), Norms(8, 1, 128, EPS)

            def raws(side, dst, norms):
                return [raw_chunk(ws[2 * side + j // 4], 128 * (j % 4), u, t_u, dst[:, j, :], norms, j,
                                  ("m", side, j), j % 4 == 3) for j in range(8)]

            def normed_(side, dst, norms, gcol):
                return [norm_chunk(dst[:, j, :], norms, j, gcol, ("m", side, j), rot2) for j in range(8)]

            pipeline(raws(0, qT, NQ), 3)
            tr = af(sn, sn, ACT.Sin, t_angles)
            tr = af(cs, cs, ACT.Sin, t_angles)
            rot2 = (C("r2"), cs, sn, tr)
            NQ.finish()
            pipeline(mixed(raws(1, kT, NK_), normed_(0, qT, NQ, P("gq"))), 3)
            NQ.close(NQ.last)
            NK_.finish()
            vw = {}

            def values(half, q):
                if half not in vw:
                    vw[half] = wcols(W, 2048 + 512 * half)
                w = vw[half]
                b, ps, fr = bank.take()
                m = mms(ps, [(u[:, k, 128 * q:128 * q + 128], w.ap[:, k, :]) for k in range(KT)], w.tok, fr)
                if q == 1:
                    w.done(m)
                yield
                T_["mv", half, q] = af(v[:, q, 512 * half:512 * half + 512], ps, ACT.Copy, m)
                bank.give(b, T_["mv", half, q])
                yield

            ty = []

            def head(h):
                kq, pt, fqk = PT.take()
                ev = [dve(lambda e: e.memset(pt[:, 1, 0:128], 0.0), fqk)]
                for q in range(2):
                    n = 128 * (q + 1)
                    kp, p, st, t = yield from last_of(softmax(
                        qT[:, h, 128 * q:128 * q + 128], kT[:, h, 0:n], n, 128.0 ** -0.5,
                        [T_["m", 0, h], T_["m", 1, h]], mask=C(f"mask{q}", n)))
                    t = ts(dve, p[:, 0:n], p[:, 0:n], st[:, 3:4], None, ALU.mult, None, t)
                    yield
                    mt, te = turn(p, t, n, pt, q, fqk)
                    scr.give(kp, mt)
                    ev.append(te)
                yield
                b, ps, fr = bank.take()
                m = mms(ps[:, 0:T], [(v[:, j, 128 * h:128 * h + 128], pt[:, j, :]) for j in range(2)], ev,
                        [T_["mv", h // 4, q] for q in range(2)], fr)
                PT.give(kq, m)
                t = af(y[:, h, :], ps[:, 0:T], ACT.Copy, m)
                bank.give(b, t)
                ty.append(t)
                yield

            pipeline(mixed([values(half, q) for half in range(2) for q in range(2)],
                           normed_(1, kT, NK_, P("gk"))), 3)
            NK_.close(NK_.last)
            pipeline([head(h) for h in range(8)], 4)
            return project_out(A["b_w_out"][0], KT, y, ty, None)

        if stage >= 3:
            t_x = mlstm(t_x)
        if stage >= 4:
            t_x = ffn(t_x, 0)
        if stage >= 5:
            t_x = moba(t_x)
        if stage >= 6:
            t_x = ffn(t_x, 1)

        end = sp.dma(lambda e: e.dma_start(A["out"].rearrange("(k p) n -> p k n", p=128), xT[:, :, :]), s_out, 16, t_x)
        sp.wait(end)

        block = ctx.enter_context(nc.Block())
        block.sync(sp.replay)
        block.scalar(act.replay)
        block.vector(dve.replay)
        block.gpsimd(pool.replay)
        block.tensor(pe.replay)


STAGE = 99
_DIRECT = ["b_down", "b_gate", "b_up", "router_w", "router_b", "w_ada", "w_in", "w_oa", "w_ob", "w_out", "w_gate", "w_up", "w_down"]
_SECOND = {"a_w_in": "a_w_in_2", "a_w_out": "a_w_out_2", "b_w_in": "b_w_in_2", "b_w_out": "b_w_out_2",
           "ffn_w_in": "ffn_w_in_2", "ffn_w_out": "ffn_w_out_2", "positions": "positions_2"}


def kernel(**inputs):
    import numpy as _np
    import concourse.bacc as _bacc
    from concourse import mybir as _mybir
    from concourse.bass_utils import run_bass_kernel_spmd as _run

    I = {k: _np.asarray(v) for k, v in inputs.items()}
    par = _np.zeros((128, NP), _np.float32)

    def put(name, a):
        par[0:a.shape[0], PCOL[name]:PCOL[name] + a.shape[1]] = a

    def cols(v):
        return _np.ascontiguousarray(v.reshape(-1, 128).T)

    def twice(v):
        return _np.concatenate([v, v])[:, None]

    put("norm_attn", cols(I["norm_attn"][0]))
    put("qna", twice(I["q_norm_a"][0]))
    put("kna", twice(I["k_norm_a"][0]))
    put("qnb", twice(I["q_norm_b"][0]))
    put("knb", twice(I["k_norm_b"][0]))
    put("subln", cols(I["subln_b"][0]))
    put("norm_mlp", cols(I["norm_mlp"][0]))
    put("c2", _np.stack([cols(I["c"][0]), cols(I["c_ctx"])], axis=2).reshape(128, 16))
    put("b_ada", _np.repeat(cols(I["b_ada"][0]), 2, axis=1))
    put("b_gate", cols(I["b_gate"][0].reshape(-1)))
    put("b_up", cols(I["b_up"][0].reshape(-1)))
    put("norm_mix", cols(I["norm_mix_2"].reshape(-1)))
    put("norm_ffn", cols(I["norm_ffn_2"].reshape(-1)))
    put("a_g_out", cols(I["a_g_out_2"].reshape(-1)))
    put("gq", cols(I["b_g_q_2"][0]))
    put("gk", cols(I["b_g_k_2"][0]))
    put("lam", _np.stack([I["lambda_q1"][0], I["lambda_q2"][0], I["lambda_k1"][0], I["lambda_k2"][0]], axis=1))
    put("bi", I["a_b_gates_2"][0][0:4, None])
    put("bf", I["a_b_gates_2"][0][4:8, None])
    arrays = {"con": shape_constants(), "par": par,
              "xT": _np.ascontiguousarray(I["x"][0].T), "ctxT": _np.ascontiguousarray(I["ctx"][0].T)}
    for n in _DIRECT:
        arrays[n] = _np.ascontiguousarray(I[n])
    for n, src in _SECOND.items():
        arrays[n] = _np.ascontiguousarray(I[src])
    nc = _bacc.Bacc("TRN2", target_bir_lowering=False, num_devices=1)
    A = {n: nc.dram_tensor(f"in_{n}", a.shape, _mybir.dt.from_np(a.dtype), kind="ExternalInput").ap()
         for n, a in arrays.items()}
    A["out"] = nc.dram_tensor("out_0", (D, T), F32, kind="ExternalOutput").ap()
    build(nc, A, STAGE)
    r = _run(nc, [{f"in_{n}": a for n, a in arrays.items()}], core_ids=[0])
    return _np.ascontiguousarray(_np.asarray(r.results[0]["out_0"]).T)[None]
```
